# Optimizing a Trainium2 kernel written in Bass

```python
import math
import jax
import jax.numpy as jnp
from jax import lax
import numpy as np

D_MODEL = 1024
BATCH = 1
SEQ = 256
DEPTH = 2

CHUNK = 64
Q_BLOCK = 128
EPS = 1e-6
ROPE_THETA = 10000.0

A_HEADS = D_MODEL // 128
A_DK = 64
A_DV = 64
B_HEADS = D_MODEL // 128
B_DH = 64
C_DH = 64
C_DV = 2 * C_DH
C_HEADS = D_MODEL // C_DV
N_GROUPS = 4
EXPERTS_PER_GROUP = 8
TOP_K_IN_GROUP = 2
D_EXPERT = D_MODEL // 2

N_EVEN = (DEPTH + 1) // 2
N_ODD = DEPTH // 2

_EVEN_COLS = (A_HEADS * A_DK, A_HEADS * A_DK, A_HEADS * A_DV, A_HEADS * A_DV,
              B_HEADS * B_DH, B_HEADS * B_DH, B_HEADS * B_DH, B_HEADS)
EVEN_IN = sum(_EVEN_COLS)
EVEN_SPLITS = tuple(int(c) for c in np.cumsum(_EVEN_COLS)[:-1])
EVEN_OUT = A_HEADS * A_DV + B_HEADS * B_DH
ODD_IN = C_HEADS * (2 * C_DH + 2 * C_DH + C_DV)
ODD_OUT = C_HEADS * C_DV


def rms_norm(x, gain):
    xf = x.astype(jnp.float32)
    y = xf * lax.rsqrt(jnp.mean(jnp.square(xf), axis=-1, keepdims=True) + EPS)
    return (y * gain.astype(jnp.float32)).astype(x.dtype)

def apply_rope(x, positions):
    half = x.shape[-1] // 2
    inv_freq = ROPE_THETA ** (-jnp.arange(half, dtype=jnp.float32) / half)
    ang = positions.astype(jnp.float32)[..., None] * inv_freq
    ang = ang.reshape(ang.shape[:2] + (1,) * (x.ndim - 3) + (half,))
    cos, sin = jnp.cos(ang), jnp.sin(ang)
    xf = x.astype(jnp.float32)
    x1, x2 = xf[..., :half], xf[..., half:]
    return jnp.concatenate([x1 * cos - x2 * sin, x2 * cos + x1 * sin], axis=-1).astype(x.dtype)

def hgrn2_recurrence(q, f_logit, i, g, lb, out_norm):
    B_, S_, H, DK = q.shape
    DV = i.shape[-1]
    nc = S_ // CHUNK
    qf = jax.nn.silu(q.astype(jnp.float32))
    f = lb + (1.0 - lb) * jax.nn.sigmoid(f_logit.astype(jnp.float32))
    log_f = jnp.log(f)
    k = 1.0 - f

    def to_chunks(t):
        return t.reshape(B_, nc, CHUNK, H, t.shape[-1]).transpose(1, 0, 3, 2, 4)

    qc, kc, vc, lfc = (to_chunks(t) for t in (qf, k, i.astype(jnp.float32), log_f))
    causal = jnp.tril(jnp.ones((CHUNK, CHUNK), dtype=bool))[:, :, None]

    def step(state, inp):
        qb, kb, vb, lf = inp
        cum = jnp.cumsum(lf, axis=2)
        rel = cum[:, :, :, None, :] - cum[:, :, None, :, :]
        decay = jnp.exp(jnp.where(causal, rel, -jnp.inf))
        scores = jnp.einsum('bhtsk,bhsk->bhts', qb[:, :, :, None, :] * decay, kb)
        o = (jnp.einsum('bhts,bhsv->bhtv', scores, vb)
             + jnp.einsum('bhtk,bhkv->bhtv', qb * jnp.exp(cum), state))
        last = cum[:, :, -1:, :]
        state = (jnp.exp(last[:, :, 0, :])[..., None] * state
                 + jnp.einsum('bhsk,bhsv->bhkv', kb * jnp.exp(last - cum), vb))
        return state, o

    state0 = jnp.zeros((B_, H, DK, DV), jnp.float32)
    _, o = lax.scan(step, state0, (qc, kc, vc, lfc))
    o = o.transpose(1, 0, 3, 2, 4).reshape(B_, S_, H, DV)
    o = rms_norm(o, out_norm) * jax.nn.silu(g.astype(jnp.float32))
    return o.astype(q.dtype)

def forgetting_attention(q, k, v, f_logit):
    B_, S_, H, Dh = q.shape
    scale = Dh ** -0.5
    log_f = jax.nn.log_sigmoid(f_logit.astype(jnp.float32))
    cum = jnp.cumsum(log_f, axis=1).transpose(0, 2, 1)
    qh, kh, vh = (t.transpose(0, 2, 1, 3) for t in (q, k, v))
    outs = []
    for q0 in range(0, S_, Q_BLOCK):
        q1 = q0 + Q_BLOCK
        logits = jnp.einsum('bhtd,bhsd->bhts', qh[:, :, q0:q1], kh[:, :, :q1]).astype(jnp.float32) * scale
        logits = logits + cum[:, :, q0:q1, None] - cum[:, :, None, :q1]
        t_pos = jnp.arange(q0, q1)[:, None]
        s_pos = jnp.arange(q1)[None, :]
        logits = jnp.where(s_pos <= t_pos, logits, -jnp.inf)
        p = jax.nn.softmax(logits, axis=-1).astype(v.dtype)
        outs.append(jnp.einsum('bhts,bhsd->bhtd', p, vh[:, :, :q1]))
    return jnp.concatenate(outs, axis=2).transpose(0, 2, 1, 3)

def differential_attention(q, k, v, lam, lambda_init, subln):
    B_, S_, H, _, Dh = q.shape
    scale = Dh ** -0.5
    qh = q.transpose(0, 2, 3, 1, 4)
    kh = k.transpose(0, 2, 3, 1, 4)
    vh = v.transpose(0, 2, 1, 3)
    outs = []
    for q0 in range(0, S_, Q_BLOCK):
        q1 = q0 + Q_BLOCK
        logits = jnp.einsum('bhmtd,bhmsd->bhmts', qh[:, :, :, q0:q1], kh[:, :, :, :q1]).astype(jnp.float32) * scale
        t_chunk = (jnp.arange(q0, q1) // CHUNK)[:, None]
        s_chunk = (jnp.arange(q1) // CHUNK)[None, :]
        logits = jnp.where(s_chunk <= t_chunk, logits, -jnp.inf)
        p = jax.nn.softmax(logits, axis=-1)
        p_diff = (p[:, :, 0] - lam * p[:, :, 1]).astype(v.dtype)
        outs.append(jnp.einsum('bhts,bhsv->bhtv', p_diff, vh[:, :, :q1]))
    o = jnp.concatenate(outs, axis=2).transpose(0, 2, 1, 3)
    return rms_norm(o, subln) * (1.0 - lambda_init)

def even_mixer(u, w_in, w_out, lb, fox_f_bias, hgrn_out_norm, fox_q_norm, fox_k_norm):
    B_, S_, _ = u.shape
    proj = u @ w_in
    a_q, a_f, a_i, a_g, b_q, b_k, b_v, b_f = jnp.split(proj, EVEN_SPLITS, axis=-1)
    heads = lambda t, h: t.reshape(B_, S_, h, t.shape[-1] // h)
    o_a = hgrn2_recurrence(heads(a_q, A_HEADS), heads(a_f, A_HEADS), heads(a_i, A_HEADS),
                           heads(a_g, A_HEADS), lb, hgrn_out_norm)
    o_b = forgetting_attention(rms_norm(heads(b_q, B_HEADS), fox_q_norm),
                               rms_norm(heads(b_k, B_HEADS), fox_k_norm),
                               heads(b_v, B_HEADS), b_f + fox_f_bias)
    o = jnp.concatenate([o_a.reshape(B_, S_, -1), o_b.reshape(B_, S_, -1)], axis=-1)
    return o @ w_out

def odd_mixer(u, positions, w_in, w_out, q_norm, k_norm, lq1, lk1, lq2, lk2, subln, lambda_init):
    B_, S_, _ = u.shape
    q, k, v = jnp.split(u @ w_in, 3, axis=-1)
    q = apply_rope(rms_norm(q.reshape(B_, S_, C_HEADS, 2, C_DH), q_norm), positions)
    k = apply_rope(rms_norm(k.reshape(B_, S_, C_HEADS, 2, C_DH), k_norm), positions)
    v = v.reshape(B_, S_, C_HEADS, C_DV)
    f32 = jnp.float32
    lam = (jnp.exp(jnp.sum(lq1.astype(f32) * lk1.astype(f32)))
           - jnp.exp(jnp.sum(lq2.astype(f32) * lk2.astype(f32))) + lambda_init)
    o = differential_attention(q, k, v, lam, lambda_init, subln)
    return o.reshape(B_, S_, ODD_OUT) @ w_out

def hierarchical_moe(u, w_router_group, w_router_expert, w_gate, w_up, w_down):
    B_, S_, D = u.shape
    x = u.reshape(B_ * S_, D)
    grp_logits = (x @ w_router_group).astype(jnp.float32)
    p_grp = jax.nn.softmax(grp_logits, axis=-1)
    g_onehot = jax.nn.one_hot(jnp.argmax(grp_logits, axis=-1), N_GROUPS, dtype=jnp.float32)
    p_g = jnp.sum(p_grp * g_onehot, axis=-1, keepdims=True)
    exp_logits = jnp.einsum('nd,gde->nge', x, w_router_expert).astype(jnp.float32)
    sel_logits = jnp.einsum('nge,ng->ne', exp_logits, g_onehot)
    p_exp = jax.nn.softmax(sel_logits, axis=-1)
    top_w, top_i = lax.top_k(p_exp, TOP_K_IN_GROUP)
    top_w = top_w / jnp.sum(top_w, axis=-1, keepdims=True)
    w_in_group = jnp.sum(jax.nn.one_hot(top_i, EXPERTS_PER_GROUP, dtype=jnp.float32) * top_w[..., None], axis=1)
    combine = (g_onehot[:, :, None] * (p_g[:, :, None] * w_in_group[:, None, :])).astype(x.dtype)
    y = jnp.zeros_like(x)
    for g in range(N_GROUPS):
        hid = jax.nn.silu(jnp.einsum('nd,edf->nef', x, w_gate[g])) * jnp.einsum('nd,edf->nef', x, w_up[g])
        y = y + jnp.einsum('nef,efd->nd', hid * combine[:, g, :, None], w_down[g])
    return y.reshape(B_, S_, D)

def first_inputs(seed: int = 0) -> dict:
    key = jax.random.key(seed)
    ks = jax.random.split(key, 32)
    f32 = jnp.float32

    def nrm(k, shape, scale):
        return jax.random.normal(k, shape, f32) * scale

    def gain(k, shape):
        return 1.0 + 0.05 * jax.random.normal(k, shape, f32)

    res_scale = (2 * DEPTH) ** -0.5
    x = jax.random.normal(ks[0], (BATCH, SEQ, D_MODEL), f32)
    start = jax.random.randint(ks[1], (BATCH, 1), 0, 4096, dtype=jnp.int32)
    positions = start + jnp.arange(SEQ, dtype=jnp.int32)[None, :]
    return {
        'x': x,
        'positions': positions,
        'hgrn_lb_logits': nrm(ks[2], (N_EVEN + 1, A_HEADS * A_DK), 0.5),
        'norm_mix': gain(ks[3], (DEPTH, D_MODEL)),
        'norm_ffn': gain(ks[4], (DEPTH, D_MODEL)),
        'even_w_in': nrm(ks[5], (N_EVEN, D_MODEL, EVEN_IN), D_MODEL ** -0.5),
        'even_w_out': nrm(ks[6], (N_EVEN, EVEN_OUT, D_MODEL), EVEN_OUT ** -0.5 * res_scale),
        'fox_f_bias': jnp.linspace(1.0, 4.0, B_HEADS, dtype=f32)[None, :] + nrm(ks[7], (N_EVEN, B_HEADS), 0.1),
        'hgrn_out_norm': gain(ks[8], (N_EVEN, A_DV)),
        'fox_q_norm': gain(ks[9], (N_EVEN, B_DH)),
        'fox_k_norm': gain(ks[10], (N_EVEN, B_DH)),
        'odd_w_in': nrm(ks[11], (N_ODD, D_MODEL, ODD_IN), D_MODEL ** -0.5),
        'odd_w_out': nrm(ks[12], (N_ODD, ODD_OUT, D_MODEL), ODD_OUT ** -0.5 * res_scale),
        'diff_q_norm': gain(ks[13], (N_ODD, C_DH)),
        'diff_k_norm': gain(ks[14], (N_ODD, C_DH)),
        'diff_lambda_q1': nrm(ks[15], (N_ODD, C_DH), 0.1),
        'diff_lambda_k1': nrm(ks[16], (N_ODD, C_DH), 0.1),
        'diff_lambda_q2': nrm(ks[17], (N_ODD, C_DH), 0.1),
        'diff_lambda_k2': nrm(ks[18], (N_ODD, C_DH), 0.1),
        'diff_subln': gain(ks[19], (N_ODD, C_DV)),
        'moe_router_group': nrm(ks[20], (DEPTH, D_MODEL, N_GROUPS), D_MODEL ** -0.5),
        'moe_router_expert': nrm(ks[21], (DEPTH, N_GROUPS, D_MODEL, EXPERTS_PER_GROUP), D_MODEL ** -0.5),
        'moe_w_gate': nrm(ks[22], (DEPTH, N_GROUPS, EXPERTS_PER_GROUP, D_MODEL, D_EXPERT), D_MODEL ** -0.5),
        'moe_w_up': nrm(ks[23], (DEPTH, N_GROUPS, EXPERTS_PER_GROUP, D_MODEL, D_EXPERT), D_MODEL ** -0.5),
        'moe_w_down': nrm(ks[24], (DEPTH, N_GROUPS, EXPERTS_PER_GROUP, D_EXPERT, D_MODEL), D_EXPERT ** -0.5 * res_scale),
    }

def first_block(x, positions, hgrn_lb_logits, norm_mix, norm_ffn, even_w_in, even_w_out, fox_f_bias,
              hgrn_out_norm, fox_q_norm, fox_k_norm, odd_w_in, odd_w_out, diff_q_norm, diff_k_norm,
              diff_lambda_q1, diff_lambda_k1, diff_lambda_q2, diff_lambda_k2, diff_subln,
              moe_router_group, moe_router_expert, moe_w_gate, moe_w_up, moe_w_down):
    lower_bounds = jnp.cumsum(jax.nn.softmax(hgrn_lb_logits.astype(jnp.float32), axis=0), axis=0)
    h = x
    for layer in range(DEPTH):
        j = layer // 2
        u = rms_norm(h, norm_mix[layer])
        if layer % 2 == 0:
            mix = even_mixer(u, even_w_in[j], even_w_out[j], lower_bounds[j].reshape(A_HEADS, A_DK),
                             fox_f_bias[j], hgrn_out_norm[j], fox_q_norm[j], fox_k_norm[j])
        else:
            lambda_init = 0.8 - 0.6 * math.exp(-0.3 * layer)
            mix = odd_mixer(u, positions, odd_w_in[j], odd_w_out[j], diff_q_norm[j], diff_k_norm[j],
                            diff_lambda_q1[j], diff_lambda_k1[j], diff_lambda_q2[j], diff_lambda_k2[j],
                            diff_subln[j], lambda_init)
        h = h + mix
        h = h + hierarchical_moe(rms_norm(h, norm_ffn[layer]), moe_router_group[layer], moe_router_expert[layer],
                                 moe_w_gate[layer], moe_w_up[layer], moe_w_down[layer])
    return h


GRID_W = 64
CTX_LEN = 256
N_EVEN_2 = (DEPTH + 1) // 2
N_ODD_2 = DEPTH // 2
N_MOD = 6
D_FF = 4 * D_MODEL
HEAD_DIM = D_MODEL // 16
MLA_HEADS = 8
MLA_NOPE = HEAD_DIM
MLA_ROPE = HEAD_DIM // 2
MLA_V = HEAD_DIM
MLA_Q_LORA = 3 * D_MODEL // 8
MLA_KV_LORA = D_MODEL // 4
GQA_HEADS = 8
GQA_KV_HEADS = 2
GQA_DIM = HEAD_DIM
ATTN_PARTS = (MLA_Q_LORA, MLA_KV_LORA, MLA_ROPE,
              GQA_HEADS * GQA_DIM, GQA_KV_HEADS * GQA_DIM, GQA_KV_HEADS * GQA_DIM)
ATTN_IN = sum(ATTN_PARTS)
ATTN_SPLITS = tuple(sum(ATTN_PARTS[:i + 1]) for i in range(len(ATTN_PARTS) - 1))
MIX_WIDTH = MLA_HEADS * MLA_V + GQA_HEADS * GQA_DIM
HYENA_ORDER = 2
HYENA_SHORT = 3
HYENA_BANDS = 8
HYENA_EMB = 1 + 2 * HYENA_BANDS
HYENA_FILTER_HIDDEN = 64
HYENA_FAST_DECAY = 0.3
HYENA_SLOW_DECAY = 1.5
HYENA_TARGET = 1e-2


F32 = jnp.float32

def rmsnorm(x, g):
    xf = x.astype(F32)
    y = xf * lax.rsqrt(jnp.mean(xf * xf, axis=-1, keepdims=True) + EPS)
    return (y * g.astype(F32)).astype(x.dtype)

def modulate(x, g, shift, scale):
    return rmsnorm(x, g) * (1 + scale) + shift

def _rotate(x, ang):
    n = ang.shape[-1]
    cos = jnp.cos(ang)[None, :, None, :]
    sin = jnp.sin(ang)[None, :, None, :]
    a = x[..., :n].astype(F32)
    b = x[..., n:].astype(F32)
    return jnp.concatenate([a * cos - b * sin, a * sin + b * cos], axis=-1).astype(x.dtype)

def rope_2d(x, row, col):
    half = x.shape[-1] // 2
    nf = half // 2
    inv = ROPE_THETA ** (-jnp.arange(nf, dtype=F32) / nf)
    ang_r = row.astype(F32)[:, None] * inv[None]
    ang_c = col.astype(F32)[:, None] * inv[None]
    return jnp.concatenate([_rotate(x[..., :half], ang_r), _rotate(x[..., half:], ang_c)], axis=-1)

def block_attention(q, k, v):
    B, S, Hq, dk = q.shape
    Hk, dv = k.shape[2], v.shape[-1]
    G = Hq // Hk
    nb = S // Q_BLOCK
    scale = 1.0 / math.sqrt(dk)
    qb = q.reshape(B, nb, Q_BLOCK, Hk, G, dk).transpose(1, 0, 2, 3, 4, 5)

    def one(qblk):
        s = jnp.einsum('bqhgd,bkhd->bhgqk', qblk, k, preferred_element_type=F32) * scale
        p = jax.nn.softmax(s, axis=-1).astype(v.dtype)
        return jnp.einsum('bhgqk,bkhe->bqhge', p, v)

    o = lax.map(one, qb)
    return o.transpose(1, 0, 2, 3, 4, 5).reshape(B, S, Hq, dv)

def attn_heads(z, q_a_g, w_q_b, kv_a_g, w_kv_b, q_norm_g, k_norm_g, pos):
    B, L, _ = z.shape
    cq, ckv, kr, gq, gk, gv = jnp.split(z, ATTN_SPLITS, axis=-1)
    q = (rmsnorm(cq, q_a_g) @ w_q_b).reshape(B, L, MLA_HEADS, MLA_NOPE + MLA_ROPE)
    q_nope, q_rope = q[..., :MLA_NOPE], q[..., MLA_NOPE:]
    kv = (rmsnorm(ckv, kv_a_g) @ w_kv_b).reshape(B, L, MLA_HEADS, MLA_NOPE + MLA_V)
    k_nope, v_mla = kv[..., :MLA_NOPE], kv[..., MLA_NOPE:]
    k_rope = kr[:, :, None, :]
    gq = rmsnorm(gq.reshape(B, L, GQA_HEADS, GQA_DIM), q_norm_g)
    gk = rmsnorm(gk.reshape(B, L, GQA_KV_HEADS, GQA_DIM), k_norm_g)
    gv = gv.reshape(B, L, GQA_KV_HEADS, GQA_DIM)
    if pos is not None:
        row, col = pos
        q_rope = rope_2d(q_rope, row, col)
        k_rope = rope_2d(k_rope, row, col)
        gq = rope_2d(gq, row, col)
        gk = rope_2d(gk, row, col)
    q_mla = jnp.concatenate([q_nope, q_rope], axis=-1)
    k_mla = jnp.concatenate([k_nope, jnp.broadcast_to(k_rope, (B, L, MLA_HEADS, MLA_ROPE))], axis=-1)
    return q_mla, k_mla, v_mla, gq, gk, gv

def attention_mixer(hl, hc, w_in, q_a_g, w_q_b, kv_a_g, w_kv_b, q_norm_g, k_norm_g, w_out,
                    row, col, need_ctx):
    B, S, _ = hl.shape
    lat = attn_heads(hl @ w_in, q_a_g, w_q_b, kv_a_g, w_kv_b, q_norm_g, k_norm_g, (row, col))
    cx = attn_heads(hc @ w_in, q_a_g, w_q_b, kv_a_g, w_kv_b, q_norm_g, k_norm_g, None)
    k_mla = jnp.concatenate([cx[1], lat[1]], axis=1)
    v_mla = jnp.concatenate([cx[2], lat[2]], axis=1)
    k_gqa = jnp.concatenate([cx[4], lat[4]], axis=1)
    v_gqa = jnp.concatenate([cx[5], lat[5]], axis=1)
    o_lat = jnp.concatenate([
        block_attention(lat[0], k_mla, v_mla).reshape(B, S, MLA_HEADS * MLA_V),
        block_attention(lat[3], k_gqa, v_gqa).reshape(B, S, GQA_HEADS * GQA_DIM)], axis=-1) @ w_out
    o_ctx = None
    if need_ctx:
        Lc = hc.shape[1]
        o_ctx = jnp.concatenate([
            block_attention(cx[0], cx[1], cx[2]).reshape(B, Lc, MLA_HEADS * MLA_V),
            block_attention(cx[3], cx[4], cx[5]).reshape(B, Lc, GQA_HEADS * GQA_DIM)], axis=-1) @ w_out
    return o_lat, o_ctx

def short_conv(z, w, b):
    L = z.shape[1]
    p = HYENA_SHORT // 2
    zp = jnp.pad(z, ((0, 0), (p, p), (0, 0)))
    out = b
    for j in range(HYENA_SHORT):
        out = out + zp[:, j:j + L] * w[j]
    return out

def hyena_filters(L, f_w1, f_b1, f_w2, f_b2, f_w3, f_b3, f_freq, f_w4):
    t = jnp.arange(L, dtype=F32)
    t_norm = t / L
    w = 2.0 * math.pi * t / L
    bands = jnp.linspace(1e-4, HYENA_BANDS - 1, HYENA_BANDS, dtype=F32)
    fw = w[:, None] * bands[None]
    feats = jnp.concatenate([t_norm[:, None], jnp.cos(fw), -jnp.sin(fw)], axis=-1)
    fr = f_freq.astype(F32)
    h = jnp.sin(fr[0] * (feats @ f_w1.astype(F32) + f_b1.astype(F32)))
    h = jnp.sin(fr[1] * (h @ f_w2.astype(F32) + f_b2.astype(F32)))
    h = jnp.sin(fr[2] * (h @ f_w3.astype(F32) + f_b3.astype(F32)))
    h = (h @ f_w4.astype(F32)).reshape(L, 2, HYENA_ORDER, D_MODEL)
    max_decay = math.log(HYENA_TARGET) / HYENA_FAST_DECAY
    min_decay = math.log(HYENA_TARGET) / HYENA_SLOW_DECAY
    deltas = jnp.abs(jnp.linspace(min_decay, max_decay, D_MODEL, dtype=F32))
    window = jnp.exp(-t_norm[:, None] * deltas[None])
    h = h * window[:, None, None, :]
    h = h * lax.rsqrt(jnp.sum(h * h, axis=(0, 1), keepdims=True) + EPS)
    return h[:, 0], h[:, 1]

def bidir_long_conv(u, hf, hb, skip):
    L = u.shape[1]
    kfull = jnp.concatenate([hf, jnp.zeros_like(hf[:1]), hb[:0:-1]], axis=0)
    K = jnp.fft.rfft(kfull, n=2 * L, axis=0)
    uf = u.astype(F32)
    U = jnp.fft.rfft(uf, n=2 * L, axis=1)
    y = jnp.fft.irfft(U * K[None], n=2 * L, axis=1)[:, :L]
    return (y + uf * skip.astype(F32)).astype(u.dtype)

def hyena_mixer(h, w_in, conv_w, conv_b, f_w1, f_b1, f_w2, f_b2, f_w3, f_b3, f_freq, f_w4,
                skip, w_out):
    L = h.shape[1]
    z = short_conv(h @ w_in, conv_w, conv_b)
    x1, x2, v = jnp.split(z, 3, axis=-1)
    hf, hb = hyena_filters(L, f_w1, f_b1, f_w2, f_b2, f_w3, f_b3, f_freq, f_w4)
    y = v
    for n, gate in enumerate((x1, x2)):
        y = gate * bidir_long_conv(y, hf[:, n], hb[:, n], skip[n])
    return y @ w_out

def sq_relu_mlp(h, w1, w2):
    return jnp.square(jax.nn.relu(h @ w1)) @ w2

def second_inputs(seed: int = 0) -> dict:
    key = jax.random.key(seed)
    ks = list(jax.random.split(key, 40))

    def nrm(shape, scale):
        return jax.random.normal(ks.pop(), shape, F32) * scale

    def gain(shape):
        return 1.0 + nrm(shape, 0.02)

    D = D_MODEL
    return {
        'x': nrm((BATCH, SEQ, D), 1.0),
        'c': nrm((BATCH, D), 1.0),
        'ctx': nrm((BATCH, CTX_LEN, D), 1.0),
        'c_ctx': nrm((D,), 1.0),
        'w_mod': nrm((DEPTH, D, N_MOD * D), 0.5 * D ** -0.5),
        'b_mod': nrm((DEPTH, N_MOD * D), 0.02),
        'norm1_g': gain((DEPTH, D)),
        'norm2_g': gain((DEPTH, D)),
        'mlp_w1': nrm((DEPTH, D, D_FF), D ** -0.5),
        'mlp_w2': nrm((DEPTH, D_FF, D), D_FF ** -0.5),
        'a_w_in': nrm((N_EVEN_2, D, ATTN_IN), D ** -0.5),
        'a_q_a_g': gain((N_EVEN_2, MLA_Q_LORA)),
        'a_w_q_b': nrm((N_EVEN_2, MLA_Q_LORA, MLA_HEADS * (MLA_NOPE + MLA_ROPE)), MLA_Q_LORA ** -0.5),
        'a_kv_a_g': gain((N_EVEN_2, MLA_KV_LORA)),
        'a_w_kv_b': nrm((N_EVEN_2, MLA_KV_LORA, MLA_HEADS * (MLA_NOPE + MLA_V)), MLA_KV_LORA ** -0.5),
        'a_q_norm_g': gain((N_EVEN_2, GQA_DIM)),
        'a_k_norm_g': gain((N_EVEN_2, GQA_DIM)),
        'a_w_out': nrm((N_EVEN_2, MIX_WIDTH, D), MIX_WIDTH ** -0.5),
        'h_w_in': nrm((N_ODD_2, D, 3 * D), D ** -0.5),
        'h_conv_w': nrm((N_ODD_2, HYENA_SHORT, 3 * D), HYENA_SHORT ** -0.5),
        'h_conv_b': nrm((N_ODD_2, 3 * D), 0.02),
        'h_f_w1': nrm((N_ODD_2, HYENA_EMB, HYENA_FILTER_HIDDEN), HYENA_EMB ** -0.5),
        'h_f_b1': nrm((N_ODD_2, HYENA_FILTER_HIDDEN), 0.1),
        'h_f_w2': nrm((N_ODD_2, HYENA_FILTER_HIDDEN, HYENA_FILTER_HIDDEN), HYENA_FILTER_HIDDEN ** -0.5),
        'h_f_b2': nrm((N_ODD_2, HYENA_FILTER_HIDDEN), 0.1),
        'h_f_w3': nrm((N_ODD_2, HYENA_FILTER_HIDDEN, HYENA_FILTER_HIDDEN), HYENA_FILTER_HIDDEN ** -0.5),
        'h_f_b3': nrm((N_ODD_2, HYENA_FILTER_HIDDEN), 0.1),
        'h_f_freq': gain((N_ODD_2, 3, HYENA_FILTER_HIDDEN)),
        'h_f_w4': nrm((N_ODD_2, HYENA_FILTER_HIDDEN, 2 * HYENA_ORDER * D), HYENA_FILTER_HIDDEN ** -0.5),
        'h_skip': nrm((N_ODD_2, HYENA_ORDER, D), 0.3),
        'h_w_out': nrm((N_ODD_2, D, D), D ** -0.5),
        'final_g': gain((D,)),
    }

def second_block(x, c, ctx, c_ctx, w_mod, b_mod, norm1_g, norm2_g, mlp_w1, mlp_w2,
              a_w_in, a_q_a_g, a_w_q_b, a_kv_a_g, a_w_kv_b, a_q_norm_g, a_k_norm_g, a_w_out,
              h_w_in, h_conv_w, h_conv_b, h_f_w1, h_f_b1, h_f_w2, h_f_b2, h_f_w3, h_f_b3,
              h_f_freq, h_f_w4, h_skip, h_w_out, final_g):
    S = x.shape[1]
    rows = S // GRID_W
    rr, cc = jnp.meshgrid(jnp.arange(rows, dtype=jnp.int32), jnp.arange(GRID_W, dtype=jnp.int32),
                          indexing='ij')
    row, col = rr.reshape(-1), cc.reshape(-1)
    silu_c = jax.nn.silu(c)
    silu_cc = jax.nn.silu(c_ctx)
    for i in range(DEPTH):
        ctx_live = any(j % 2 == 0 for j in range(i + 1, DEPTH))
        j = i // 2
        m_l = (silu_c @ w_mod[i] + b_mod[i])[:, None, :]
        m_c = (silu_cc @ w_mod[i] + b_mod[i])[None, None, :]
        sh1, sc1, g1, sh2, sc2, g2 = jnp.split(m_l, N_MOD, axis=-1)
        csh1, csc1, cg1, csh2, csc2, cg2 = jnp.split(m_c, N_MOD, axis=-1)
        hl = modulate(x, norm1_g[i], sh1, sc1)
        if i % 2 == 0:
            hc = modulate(ctx, norm1_g[i], csh1, csc1)
            ol, oc = attention_mixer(hl, hc, a_w_in[j], a_q_a_g[j], a_w_q_b[j], a_kv_a_g[j],
                                     a_w_kv_b[j], a_q_norm_g[j], a_k_norm_g[j], a_w_out[j],
                                     row, col, ctx_live)
        else:
            hy = (h_w_in[j], h_conv_w[j], h_conv_b[j], h_f_w1[j], h_f_b1[j], h_f_w2[j], h_f_b2[j],
                  h_f_w3[j], h_f_b3[j], h_f_freq[j], h_f_w4[j], h_skip[j], h_w_out[j])
            ol = hyena_mixer(hl, *hy)
            oc = None
            if ctx_live:
                oc = hyena_mixer(modulate(ctx, norm1_g[i], csh1, csc1), *hy)
        x = x + g1 * ol
        x = x + g2 * sq_relu_mlp(modulate(x, norm2_g[i], sh2, sc2), mlp_w1[i], mlp_w2[i])
        if ctx_live:
            ctx = ctx + cg1 * oc
            ctx = ctx + cg2 * sq_relu_mlp(modulate(ctx, norm2_g[i], csh2, csc2), mlp_w1[i], mlp_w2[i])
    return rmsnorm(x, final_g)


def setup_inputs(seed=0):
    out = dict(first_inputs(seed))
    for name, value in second_inputs(seed + 1).items():
        if name != "x":
            out[name + "_2"] = value
    return out


def reference(
    x, positions, hgrn_lb_logits, norm_mix, norm_ffn, even_w_in, even_w_out, fox_f_bias,
    hgrn_out_norm, fox_q_norm, fox_k_norm, odd_w_in, odd_w_out, diff_q_norm, diff_k_norm,
    diff_lambda_q1, diff_lambda_k1, diff_lambda_q2, diff_lambda_k2, diff_subln,
    moe_router_group, moe_router_expert, moe_w_gate, moe_w_up, moe_w_down, c_2, ctx_2, c_ctx_2,
    w_mod_2, b_mod_2, norm1_g_2, norm2_g_2, mlp_w1_2, mlp_w2_2, a_w_in_2, a_q_a_g_2, a_w_q_b_2,
    a_kv_a_g_2, a_w_kv_b_2, a_q_norm_g_2, a_k_norm_g_2, a_w_out_2, h_w_in_2, h_conv_w_2,
    h_conv_b_2, h_f_w1_2, h_f_b1_2, h_f_w2_2, h_f_b2_2, h_f_w3_2, h_f_b3_2, h_f_freq_2,
    h_f_w4_2, h_skip_2, h_w_out_2, final_g_2,
):
    x = first_block(
        x, positions, hgrn_lb_logits, norm_mix, norm_ffn, even_w_in, even_w_out, fox_f_bias,
        hgrn_out_norm, fox_q_norm, fox_k_norm, odd_w_in, odd_w_out, diff_q_norm, diff_k_norm,
        diff_lambda_q1, diff_lambda_k1, diff_lambda_q2, diff_lambda_k2, diff_subln,
        moe_router_group, moe_router_expert, moe_w_gate, moe_w_up, moe_w_down,
    )
    return second_block(
        x, c_2, ctx_2, c_ctx_2, w_mod_2, b_mod_2, norm1_g_2, norm2_g_2, mlp_w1_2, mlp_w2_2,
        a_w_in_2, a_q_a_g_2, a_w_q_b_2, a_kv_a_g_2, a_w_kv_b_2, a_q_norm_g_2, a_k_norm_g_2,
        a_w_out_2, h_w_in_2, h_conv_w_2, h_conv_b_2, h_f_w1_2, h_f_b1_2, h_f_w2_2, h_f_b2_2,
        h_f_w3_2, h_f_b3_2, h_f_freq_2, h_f_w4_2, h_skip_2, h_w_out_2, final_g_2,
    )


_drawn_inputs = setup_inputs


def setup_inputs(seed=0):
    import zlib

    import numpy as np

    out = dict(_drawn_inputs(seed))
    spreads = {}
    factors = {'hgrn_out_norm': 2.874,
     'fox_q_norm': 3.998,
     'fox_k_norm': 3.068,
     'diff_q_norm': 2.743,
     'diff_lambda_k2': 2.895,
     'norm1_g_2': 3.045,
     'norm2_g_2': 4.808,
     'a_q_a_g_2': 8.0,
     'a_kv_a_g_2': 8.0,
     'a_q_norm_g_2': 8.0,
     'a_k_norm_g_2': 8.0,
     'h_f_freq_2': 3.082,
     'final_g_2': 7.276,
     'h_conv_b_2': 5.323}
    for name, (base, spread) in spreads.items():
        noise = np.random.default_rng([zlib.crc32(name.encode()), seed]).standard_normal(out[name].shape)
        drawn = base * np.exp(spread * noise) if base else spread * noise
        out[name] = jnp.asarray(drawn.astype(out[name].dtype))
    for name, factor in factors.items():
        out[name] = (out[name] * factor).astype(out[name].dtype)
    return out
```

```python
from contextlib import ExitStack

import numpy as np

import concourse.bass as bass
from concourse import mybir

F32 = mybir.dt.float32
I32 = mybir.dt.int32
U32 = mybir.dt.uint32
ALU = mybir.AluOpType
ACT = mybir.ActivationFunctionType
AX_X = mybir.AxisListType.X

P = 128
D = 1024
S = 256
NT = S // P
KD = D // P
SLAB = 4096
RING = 6
EPS = 1e-6
N_EXPERTS = 32
PAIRS = N_EXPERTS // 2
SEATS = 64
EXPERT_SLABS = 3
HGRN_LEVELS = (64, 32, 16, 8)
LAST_BLOCK = 8
LAMBDA_INIT = 0.8 - 0.6 * float(np.exp(-0.3))
TWO_PI_HI = 6.28125
TWO_PI_LO = float(2 * np.pi - 6.28125)
ROUNDER = 12582912.0

ROW_PARTS = [("fox_q", 64), ("fox_k", 64), ("hgrn_out", 64), ("diff_q", 64), ("diff_k", 64), ("lam_q1", 64),
             ("lam_k1", 64), ("lam_q2", 64), ("lam_k2", 64), ("subln", 128), ("fox_bias", 8), ("gqa_q", 64),
             ("gqa_k", 64), ("mla_q_a", 384), ("mla_kv_a", 256), ("inv_freq", 32)]
COL_PARTS = [("lb0", 4), ("lb1", 4), ("conv_w", 72), ("conv_b", 24), ("filt_b", 3), ("filt_freq", 3),
             ("c", 8), ("c_ctx", 8), ("not_first", 1)]
GAINS = ["mix0", "ffn0", "mix1", "ffn1", "n1_0", "n2_0", "n1_1", "n2_1", "final"]


def offsets(parts):
    out, at = {}, 0
    for name, n in parts:
        out[name] = (at, n)
        at += n
    return out, at


ROWS, N_ROWS = offsets(ROW_PARTS)
COLS, N_COLS = offsets(COL_PARTS)


class Unit:

    def __init__(self, bank, before):
        self.bank, self.before = bank, before

    def later(self, n):
        return Unit(self.bank, self.before + n)


class Plan:

    def __init__(self):
        self.filled = [0] * 8
        self.next = 0
        self.units = {}
        self.slabs = {}
        self.n_slabs = 0
        self.last_reader = {}

    def take(self, name, n=1, banks=None):
        for _ in range(n):
            b = self.next if banks is None else banks[len(self.units.get(name, [])) % len(banks)]
            if banks is None:
                self.next = (self.next + 1) % 8
            self.units.setdefault(name, []).append(Unit(b, self.filled[b]))
            self.filled[b] += 1

    def slab(self, name, last_unit):
        self.slabs.setdefault(name, []).append(self.n_slabs)
        self.last_reader[self.n_slabs] = last_unit
        self.n_slabs += 1

    def stream(self, name, slabs, per_slab):
        for i in range(slabs):
            self.take(name, per_slab)
            self.slab(name, self.units[name][-1])

    def heads(self, name, steps, maps):
        for s in range(steps + 2):
            if s < steps:
                self.take(name + ".logits", maps)
            if 1 <= s < steps + 1:
                self.take(name + ".turn")
            if s >= 2:
                self.take(name + ".out")

    def experts(self, name):
        self.next = 0
        for _ in range(N_EXPERTS):
            self.take(name + ".gate", 2, (0, 1))
            self.take(name + ".up", 2, (2, 3))
            self.take(name + ".down", 4, (4, 5, 6, 7))
            self.slab(name, self.units[name + ".gate"][-1])
            self.slab(name, self.units[name + ".up"][-1])
            self.slab(name, self.units[name + ".down"][-1])
        for idx in self.slabs[name][-RING:]:
            self.last_reader[idx] = self.units[name + ".down"][-1]

    def mlp(self, name):
        self.next = 0
        for _ in range(8):
            self.take(name + ".hidden", 2, (0, 1))
            self.take(name + ".out", 4, (4, 5, 6, 7))
            self.slab(name, self.units[name + ".hidden"][-1])
            self.slab(name, self.units[name + ".out"][-1])


def make_plan():
    p = Plan()
    p.take("turn.mix0", 4)
    p.stream("hgrn_f", 1, 2)
    p.stream("hgrn_q", 1, 2)
    p.take("fox_f")
    p.stream("hgrn_i", 1, 2)
    p.stream("fox_q", 1, 2)
    p.stream("fox_k", 1, 2)
    p.stream("fox_v", 1, 2)
    p.stream("hgrn_g", 1, 2)
    p.take("fox_cum")
    for L in HGRN_LEVELS:
        p.take(f"level{L}", 4)
    p.take("diagonal", 4)
    p.take("level128", 2)
    p.take("hgrn_o", 2)
    p.take("fox_qT", 4)
    p.take("fox_kT", 4)
    p.heads("fox", 8, 1)
    p.take("turn.even_out", 4)
    p.stream("even_out", 2, 2)
    p.take("turn.ffn0", 4)
    p.take("router0")
    p.take("rank0")
    p.experts("moe0")
    p.take("turn.mix1", 4)
    p.stream("odd_in", 6, 2)
    p.take("diff_qT", 8)
    p.take("diff_kT", 8)
    p.heads("diff", 8, 2)
    p.take("turn.odd_out", 4)
    p.stream("odd_out", 2, 2)
    p.take("turn.ffn1", 4)
    p.take("router1")
    p.take("rank1")
    p.experts("moe1")
    p.stream("mod0.pre1", 4, 2)
    p.take("turn.n1_0", 4)
    p.take("turn.ctx", 4)
    p.stream("mla_cq", 1, 2)
    p.stream("mla_ckv", 1, 4)
    p.stream("gqa_q", 1, 2)
    p.stream("gqa_kv", 1, 4)
    p.take("turn.cq", 2)
    p.take("turn.ckv", 2)
    p.stream("mla_q", 1, 4)
    p.stream("mla_kv", 1, 8)
    p.take("mla_qT", 4)
    p.take("mla_kT", 8)
    p.heads("mla", 16, 1)
    p.take("gqa_qT", 4)
    p.take("gqa_kT", 2)
    p.heads("gqa", 16, 1)
    p.stream("mod0.gate1", 2, 1)
    p.take("turn.a_out", 4)
    p.stream("a_out", 2, 2)
    p.stream("mod0.pre2", 4, 1)
    p.take("turn.n2_0", 4)
    p.stream("mod0.gate2", 2, 1)
    p.mlp("mlp0")
    p.stream("mod1.pre1", 4, 1)
    p.take("turn.n1_1", 4)
    p.take("filter_mlp", 3)
    for n in range(2):
        p.take(f"filter{n}", 8)
        if n == 1:
            p.slab("filter_w4", p.units["filter1"][-1])
        p.take(f"filter_norm{n}", 2)
        p.take(f"filter_dft{n}", 8)
    for i in range(6):
        p.stream("hyena_in", 1, 2)
        p.take("hyena_turn", 2)
    for n in range(2):
        p.take(f"dft{n}", 8)
        p.take(f"idft{n}", 4)
    p.stream("mod1.gate1", 2, 1)
    p.take("turn.hyena_out", 4)
    p.stream("hyena_out", 2, 2)
    p.stream("mod1.pre2", 4, 1)
    p.take("turn.n2_1", 4)
    p.stream("mod1.gate2", 2, 1)
    p.mlp("mlp1")
    return p


def constants():
    f32 = np.float32
    s, t = np.meshgrid(np.arange(P), np.arange(P), indexing="ij")
    resident = np.concatenate([np.eye(P), np.ones((P, 2 * P)), np.broadcast_to(np.arange(SEATS), (P, SEATS)),
                               s <= t], 1).astype(f32)
    low = np.where(t <= s, 0.0, -1e30)
    causal = np.concatenate([low, np.zeros((P, P)), low], 1)
    masks = [((t // (2 * L) == s // (2 * L)) & (t % (2 * L) >= L) & (s % (2 * L) < L)) for L in HGRN_LEVELS]
    masks.append((t // LAST_BLOCK == s // LAST_BLOCK) & (s <= t))
    even = np.concatenate([causal, *masks], 1).astype(f32)
    same = np.where(t // 64 <= s // 64, 0.0, -1e30)
    chunks = np.concatenate([same, np.zeros((P, P)), same], 1).astype(f32)
    tok = np.arange(S)
    place = np.stack([tok // 64, tok % 64], 1).astype(f32)

    def rope(nf):
        inv = (f32(10000.0) ** (-np.arange(nf, dtype=f32) / f32(nf))).astype(f32)
        ang = (place[:, :, None] * inv[None, None]).astype(f32)
        parts = [g(ang).reshape(NT, P, 2 * nf).transpose(1, 0, 2).reshape(P, -1) for g in (np.cos, np.sin)]
        return np.concatenate(parts, 1)

    rope2d = np.concatenate([rope(8), rope(16)], 1).astype(f32)
    f = np.arange(S) + 0.5
    ang = 2 * np.pi * np.outer(np.arange(S), f) / (2 * S)

    def tiles(a):
        return a.reshape(NT, P, S).transpose(1, 0, 2).reshape(P, -1)

    dft = np.concatenate([tiles(np.cos(ang)), tiles(np.sin(ang)), tiles(np.cos(ang).T) / S,
                          tiles(np.sin(ang).T) / S], 1).astype(f32)
    tt = np.arange(S, dtype=f32)
    t_norm = tt / f32(S)
    w = f32(2.0 * np.pi) * tt / f32(S)
    bands = np.linspace(1e-4, 7, 8, dtype=f32)
    fw = w[:, None] * bands[None]
    feats = np.zeros((P, S), f32)
    feats[:17] = np.concatenate([t_norm[:, None], np.cos(fw), -np.sin(fw)], 1).T
    deltas = np.abs(np.linspace(np.log(1e-2) / 1.5, np.log(1e-2) / 0.3, D, dtype=f32))
    window = np.exp(-t_norm[:, None] * deltas[None]).astype(f32)
    inv_freq = (f32(10000.0) ** (-np.arange(32, dtype=f32) / f32(32))).astype(f32)
    return {"resident": resident, "even_tables": even, "chunk_mask": chunks,
            "rope2d": rope2d, "dft": dft, "feats": feats, "window": window, "inv_freq": inv_freq}


def build(nc, A, out):
    plan = make_plan()
    U = plan.units
    K = plan.slabs
    ctx = ExitStack()
    with ctx:
        def sb(name, cols, dt=F32):
            return ctx.enter_context(nc.sbuf_tensor(name, [P, cols], dt))

        sems = {}

        def sem(name):
            if name not in sems:
                sems[name] = ctx.enter_context(nc.semaphore(name))
            return sems[name]

        ring = sb("ring", RING * SLAB)
        h = sb("h", NT * D)
        xT = sb("xT", KD * S)
        gain = sb("gain", 2 * D)
        resident = sb("resident", 4 * P + SEATS)
        rows = sb("rows", N_ROWS)
        cols = sb("cols", N_COLS)
        routers = sb("routers", 2 * KD * 36)
        w_fox_f = sb("w_fox_f", KD * 8)
        stat = sb("stat", 176)
        small = sb("small", 512)
        N_ARENA = 18920
        arena = sb("arena", N_ARENA)
        banks = [ctx.enter_context(nc.psum_tensor(f"bank{b}", [P, 512], F32)) for b in range(8)]

        ident = resident[:, 0:P]
        ones = resident[:, P:2 * P]
        ones256 = resident[:, P:3 * P]
        seats = resident[:, 3 * P:3 * P + SEATS]
        iota8 = resident[:, 3 * P:3 * P + 8]
        tri = resident[:, 3 * P + SEATS:4 * P + SEATS]
        h3 = h[:, :].rearrange("p (t d) -> p t d", t=NT)
        xT3 = xT[:, :].rearrange("p (k s) -> p k s", k=KD)

        def row(name, n=None):
            at, width = ROWS[name]
            return rows[:, at:at + (n or width)]

        def col(name, i=0, n=1, p=P):
            return cols[0:p, COLS[name][0] + i:COLS[name][0] + i + n]

        def at(start, n):
            assert start + n <= N_ARENA, (start, n)
            return arena[:, start:start + n]

        def over(ap, shape, axis):
            return ap.unsqueeze(axis).to_broadcast(shape)

        bank_full = [sem(f"bank{b}_full") for b in range(8)]
        bank_drained = [sem(f"bank{b}_drained") for b in range(8)]
        slab_loaded = [sem(f"slab{r}_loaded") for r in range(RING)]
        stats_ready = sem("stats_ready")
        std_ready = sem("std_ready")
        normed = sem("normed")
        gain_loaded = [sem("gain0_loaded"), sem("gain1_loaded")]
        vec_step = sem("vec_step")
        act_step = sem("act_step")

        def full(eng, u):
            eng.wait_ge(bank_full[u.bank], u.before + 1)

        def drained(eng, u):
            eng.wait_ge(bank_drained[u.bank], u.before + 1)

        def moe_unit(layer, bank, nth, i):
            kind, j = ((".gate", 0), (".gate", 1), (".up", 0), (".up", 1), (".down", 0), (".down", 1), (".down", 2),
                       (".down", 3))[bank]
            first = U[f"moe{layer}{kind}"][j]
            assert first.bank == bank
            return Unit(bank, i * 2 + (first.before + nth))

        def short_path(eng, layer):
            eng.wait_ge(sem("counted"), layer + 1)
            most = eng.alloc_register(f"most{layer}")
            eng.reg_load(most, most_tokens[0:1, layer:layer + 1])
            return eng.If_lt(most, SEATS + 1)

        def slab_ap(idx):
            r = idx % RING
            return ring[:, r * SLAB:(r + 1) * SLAB]

        u_buf = at(0, 2048)
        u3 = u_buf.rearrange("p (t d) -> p t d", t=NT)
        scratch = at(2048, 2048)
        even_tables = at(4096, 384 + 640)
        causal = even_tables[:, 0:384]
        level_mask = [even_tables[:, 384 + 128 * i:512 + 128 * i] for i in range(5)]
        EV = 4096 + 1024
        hg_f = at(EV, 1024)
        hg_q = at(EV + 1024, 1024)
        hg_k = at(EV + 2048, 1024)
        hg_cum = at(EV + 3072, 1024)
        hg_i = at(EV + 4096, 1024).rearrange("p (t d) -> p t d", t=NT)
        hg_g = at(EV + 5120, 1024)
        fx_q = at(EV + 6144, 1024)
        fx_k = at(EV + 7168, 1024)
        fx_v = at(EV + 8192, 1024).rearrange("p (t d) -> p t d", t=NT)
        hg_P = at(EV + 9216, 3072).rearrange("p (b c t) -> p b c t", b=6, c=4)
        hg_qh = at(EV + 12288, 1024)
        hg_kh = at(2560, 1024)
        ev_o = at(2048, 2048).rearrange("p (t d) -> p t d", t=NT)
        fq_aug = at(EV, 1056).rearrange("p (t h d) -> p t h d", t=NT, h=8)
        fk_aug = at(EV + 1056, 1056).rearrange("p (t h d) -> p t h d", t=NT, h=8)
        fx_qT = at(EV + 9216, 2048)
        fx_kT = at(EV + 11264, 2048)
        fx_T = at(EV + 5120, 1024)
        fx_L = at(EV + 6144, 1536)
        att_P = at(0, 2048)
        silu_g = at(4096, 1024)
        hidden = at(5120, 1024)
        comb = at(6720, 2 * 34).rearrange("p (t e) -> p t e", t=NT)
        rank = at(6788, 2 * 34).rearrange("p (t e) -> p t e", t=NT)
        routed = at(6856, 64).rearrange("p (t e) -> p t e", t=NT)
        sel = at(6920, 256).rearrange("p (t c) -> p t c", t=NT)
        weighted = at(7176, 256).rearrange("p (t c) -> p t c", t=NT)
        weightedT = at(7432, 256)
        seated = at(7688, 1024).rearrange("p (k c) -> p k c", k=KD)
        pair_silu = at(8712, 512).rearrange("p (e c) -> p e c", e=2)
        pair_hidden = at(9224, 512).rearrange("p (e c) -> p e c", e=2)
        pair_yT = at(9736, 1024).rearrange("p (k c) -> p k c", k=KD)
        pair_y = at(10760, 1024)
        route = at(6208, 512)
        mlp_y = at(6208, 2048).rearrange("p (t d) -> p t d", t=NT)
        chunk_mask = at(4096, 384)
        od_q = at(4480, 2048)
        od_k = at(6528, 2048)
        od_v = at(8576, 2048).rearrange("p (t d) -> p t d", t=NT)
        od_tab = small[:, 0:256]
        od_qT = at(10624, 4096)
        od_kT = at(14720, 4096)
        od_L = at(2048, 1536)
        od_T = at(4480, 1024)
        od_o = at(6528, 2048).rearrange("p (t d) -> p t d", t=NT)
        c_wide = at(4096, 2048)
        shift, scale = at(6144, 1024), at(7168, 1024)
        shift_c, scale_c = at(8192, 1024), at(9216, 1024)
        ctx_x = at(10240, 2048)
        ctx_u = at(12288, 2048)
        ctxT = at(14336, 2048).rearrange("p (k s) -> p k s", k=KD)
        rope2d = at(6144, 192)
        z_cq = at(6336, 768)
        z_ckv = at(7104, 1024)
        z_kr = at(8128, 128)
        z_gq = at(8256, 1024)
        z_gk = at(9280, 512)
        z_gv = at(9792, 512).rearrange("p (t d) -> p t d", t=4)
        cqT = at(10304, 768).rearrange("p (k s) -> p k s", k=3)
        ckvT = at(11072, 1024).rearrange("p (k s) -> p k s", k=2)
        ml_v = at(16704, 2048).rearrange("p (t h d) -> p t h d", t=4, h=8)
        ml_q = at(12096, 1536)
        ml_k = at(13632, 3072)
        b2_o = at(12096, 2048).rearrange("p (t d) -> p t d", t=NT)
        b2_P = at(14144, 1024)
        b2_T = at(15168, 1024)
        qT2 = xT[:, 0:2048]
        kT2 = at(0, 4096)
        gate = at(6144, 1024)
        gate2 = at(8256, 1024)
        dft = at(0, 2048)
        cosT, sinT, icos, isin = [dft[:, 512 * i:512 * (i + 1)].rearrange("p (k f) -> p k f", k=NT) for i in range(4)]
        f_sum = at(2048, 2048)
        window = at(4096, 2048)
        h4 = at(6144, 4096)
        f_norm = rows[:, 0:1024]
        spectra = at(10728, 8192)
        hy_x = [at(2048, 2048), at(4096, 2048), at(8680, 2048)]
        z_pad = at(6144, 2064)
        conv = rows[:, 0:1024]
        y_re = at(6144, 2048)
        y_im = xT[:, 0:2048]
        prod = [rows[:, 0:512], rows[:, 512:1024]]

        def dma_done(eng, name, n=1):
            eng.wait_ge(sem(name), 16 * n)

        s_sum, s_std, s_inv = stat[:, 0:32], stat[:, 32:64], stat[:, 64:96]
        eps_col, lam, neg_lam = stat[:, 96:97], stat[:, 97:98], stat[:, 98:99]
        lb_col, one_less_lb = stat[:, 100:104], stat[:, 104:108]
        neg_max = stat[:, 112:120].rearrange("p (a m g) -> p a m g", a=2, m=2)
        exp_sum = stat[:, 120:136].rearrange("p (a m g) -> p a m g", a=4, m=2)
        exp_inv = stat[:, 136:152].rearrange("p (a m g) -> p a m g", a=4, m=2)

        route_logf = small[:, 448:464]
        pos_tile = ctx.enter_context(nc.sbuf_tensor("pos_tile", [P, NT], I32))
        od_o_flat = at(6528, 2048)
        most_tokens = ctx.enter_context(nc.sbuf_tensor("most_tokens", [P, 2], I32))
        c_kv = z_ckv.rearrange("p (t d) -> p t d", t=4)
        f_h = small[:, 0:256]
        f_diff = h4[:, 0:2048]
        CAUSAL = [(0, 0, P), (1, P, 2 * P)]
        W_IN = A["even_w_in"]

        def view_k(ap, k, n):
            return ap[:, 0:k * n].rearrange("p (k n) -> p k n", k=k)

        def part(w, c0, n):
            return w[:, c0:c0 + n].rearrange("(k p) n -> p k n", p=P)

        SOURCES = {
            "hgrn_f": [part(W_IN, 512, 512)], "hgrn_q": [part(W_IN, 0, 512)], "hgrn_i": [part(W_IN, 1024, 512)],
            "fox_q": [part(W_IN, 2048, 512)], "fox_k": [part(W_IN, 2560, 512)], "fox_v": [part(W_IN, 3072, 512)],
            "hgrn_g": [part(W_IN, 1536, 512)],
            "even_out": [part(A["even_w_out"], 512 * i, 512) for i in range(2)],
            "odd_in": [part(A["odd_w_in"], 512 * i, 512) for i in range(6)],
            "odd_out": [part(A["odd_w_out"], 512 * i, 512) for i in range(2)],
            "mla_cq": [part(A["a_w_in"], 0, 384)], "mla_ckv": [part(A["a_w_in"], 384, 288)],
            "gqa_q": [part(A["a_w_in"], 672, 512)], "gqa_kv": [part(A["a_w_in"], 1184, 256)],
            "mla_q": [part(A["a_w_q_b"], 0, 768)], "mla_kv": [part(A["a_w_kv_b"], 0, 1024)],
            "a_out": [part(A["a_w_out"], 512 * i, 512) for i in range(2)],
            "hyena_out": [part(A["h_w_out"], 512 * i, 512) for i in range(2)],
            "filter_w4": [A["h_f_w4"]],
        }
        for l in range(2):
            wm = A["w_mod"][l]
            SOURCES[f"mod{l}.pre1"] = [part(wm, 512 * i, 512) for i in range(4)]
            SOURCES[f"mod{l}.gate1"] = [part(wm, 2048 + 512 * i, 512) for i in range(2)]
            SOURCES[f"mod{l}.pre2"] = [part(wm, 3072 + 512 * i, 512) for i in range(4)]
            SOURCES[f"mod{l}.gate2"] = [part(wm, 5120 + 512 * i, 512) for i in range(2)]

        block = ctx.enter_context(nc.Block())

        @block.sync
        def _(sp):
            def load(idx, src, turn=0, slab_idx=None):
                r = idx % RING
                if idx >= RING:
                    reader = plan.last_reader[idx - RING]
                    sp.wait_ge(bank_full[reader.bank], reader.before + 1)
                dst = slab_ap(idx)
                if len(src.shape) == 3:
                    dst = view_k(dst, src.shape[1], src.shape[2])
                    sp.dma_start(dst, src).then_inc(slab_loaded[r], 16)
                else:
                    sp.dma_start(dst[0:src.shape[0], 0:src.shape[1]], src).then_inc(slab_loaded[r], 16)

            def stream(name):
                for idx, src in zip(K[name], SOURCES[name], strict=True):
                    load(idx, src)

            def expert_source(layer, e, which):
                w = (A["moe_w_gate"], A["moe_w_up"], A["moe_w_down"])[which]
                k = KD if which < 2 else 4
                return w[bass.ds(layer * N_EXPERTS + e, 1)].rearrange("a (k p) n -> p (a k) n", p=P)

            def experts(layer):
                name = f"moe{layer}"
                first = K[name][0]
                for j in range(RING):
                    load(first + j, expert_source(layer, j // EXPERT_SLABS, j % EXPERT_SLABS))

                def next_pair(i, j):
                    dst = slab_ap(first + j)
                    src = expert_source(layer, i * 2 + j // EXPERT_SLABS, j % EXPERT_SLABS)
                    sp.dma_start(view_k(dst, src.shape[1], src.shape[2]), src)\
                        .then_inc(slab_loaded[(first + j) % RING], 16)

                with short_path(sp, layer):
                    with sp.Fori(1, PAIRS) as i:
                        for j in (0, 1, 3, 4, 2, 5):
                            e, which = j // EXPERT_SLABS, j % EXPERT_SLABS
                            bank, nth = ((2 * e, e), (2 * e + 1, e), (e, 1))[which]
                            reader = moe_unit(layer, bank, nth, i - 1)
                            sp.wait_ge(bank_full[bank], reader.before + 1)
                            next_pair(i, j)
                with sp.Else():
                    with sp.Fori(1, PAIRS) as i:
                        for j in range(RING):
                            reader = plan.last_reader[first + j]
                            sp.wait_ge(bank_full[reader.bank], (i - 1) * 2 + reader.before + 1)
                            next_pair(i, j)

            def mlp(layer):
                w1, w2 = A["mlp_w1"][layer], A["mlp_w2"][layer]
                for j in range(8):
                    load(K[f"mlp{layer}"][2 * j], part(w1, 512 * j, 512))
                    load(K[f"mlp{layer}"][2 * j + 1],
                         w2[512 * j:512 * (j + 1), :].rearrange("(k p) n -> p k n", p=P))

            for name in ("hgrn_f", "hgrn_q", "hgrn_i", "fox_q", "fox_k", "fox_v", "hgrn_g", "even_out"):
                stream(name)
            experts(0)
            stream("odd_in")
            stream("odd_out")
            experts(1)
            for name in ("mod0.pre1", "mla_cq", "mla_ckv", "gqa_q", "gqa_kv", "mla_q", "mla_kv", "mod0.gate1",
                         "a_out", "mod0.pre2", "mod0.gate2"):
                stream(name)
            mlp(0)
            stream("mod1.pre1")
            stream("filter_w4")
            for i in range(6):
                load(K["hyena_in"][i], part(A["h_w_in"], 512 * i, 512))
            for name in ("mod1.gate1", "hyena_out", "mod1.pre2", "mod1.gate2"):
                stream(name)
            mlp(1)
            sp.wait_ge(sem("result_ready"), 1)
            sp.dma_start(out.rearrange("(t p) d -> p t d", p=P), u3).then_inc(sem("stored"), 16)
            sp.wait_ge(sem("stored"), 16)

        @block.gpsimd
        def _(pool):
            def load(name, dst, src):
                pool.dma_start(dst, src).then_inc(sem(name), 16)

            GAIN_ROWS = ["mix0", "ffn0", "mix1", "ffn1", "n1_0", "n2_0", "n1_1", "skip0", "skip1", "n2_1", "final"]

            def gain_row(n):
                if n >= 2:
                    pool.wait_ge(sem("gain_used"), n - 1)
                pool.dma_start(gain[:, (n % 2) * D:(n % 2 + 1) * D], A["gains"][n].partition_broadcast(P))\
                    .then_inc(gain_loaded[n % 2], 16)

            load("x_loaded", h3, A["x"].rearrange("(t p) d -> p t d", p=P))
            gain_row(0)
            load("resident_loaded", resident[:, :], A["resident"])
            load("rows_loaded", rows[:, :], A["rows"].partition_broadcast(P))
            load("cols_loaded", cols[:, :], A["cols"])
            load("fox_f_loaded", w_fox_f[:, :].rearrange("p (k n) -> p k n", k=KD), part(W_IN, 3584, 8))
            load("cols_loaded", pos_tile[:, :], A["positions"])
            load("even_tables_loaded", even_tables, A["even_tables"])
            for l in range(2):
                load("routers_loaded", routers[:, l * 288:(l + 1) * 288].rearrange("p (k n) -> p k n", k=KD),
                     A["routers"][l].rearrange("(k p) n -> p k n", p=P))
            gain_row(1)
            gain_row(2)
            gain_row(3)
            pool.wait_ge(normed, 3)
            load("chunk_loaded", chunk_mask, A["chunk_mask"])
            gain_row(4)
            pool.wait_ge(sem("moe_done"), 2)
            for dst, k, c in ((shift, 0, 0), (scale, 0, 1), (shift_c, 0, 0), (scale_c, 0, 1)):
                load("bias0_pre1", dst, A["b_mod"][k, c * D:(c + 1) * D].partition_broadcast(P))
            load("ctx_loaded", ctx_x.rearrange("p (t d) -> p t d", t=NT), A["ctx"].rearrange("(t p) d -> p t d", p=P))
            gain_row(5)
            pool.wait_ge(normed, 5)
            load("rope2d_loaded", rope2d, A["rope2d"])
            pool.wait_ge(sem("gqa_o"), 16)
            load("bias0_gate1", gate, A["b_mod"][0, 2 * D:3 * D].partition_broadcast(P))
            gain_row(6)
            pool.wait_ge(sem("gate_used"), 1)
            load("bias0_pre2", shift, A["b_mod"][0, 3 * D:4 * D].partition_broadcast(P))
            load("bias0_pre2", scale, A["b_mod"][0, 4 * D:5 * D].partition_broadcast(P))
            load("bias0_gate2", gate2, A["b_mod"][0, 5 * D:6 * D].partition_broadcast(P))
            gain_row(7)
            pool.wait_ge(sem("mlp_done"), 1)
            load("bias1_pre1", shift, A["b_mod"][1, 0:D].partition_broadcast(P))
            load("bias1_pre1", scale, A["b_mod"][1, D:2 * D].partition_broadcast(P))
            pool.wait_ge(normed, 7)
            load("filter_loaded", small[:, 0:256], A["feats"])
            load("filter_loaded", small[0:17, 256:320], A["h_f_w1"])
            load("filter_loaded", small[0:64, 320:384], A["h_f_w2"])
            load("filter_loaded", small[0:64, 384:448], A["h_f_w3"])
            load("window_loaded", window.rearrange("p (t d) -> p t d", t=NT),
                 A["window"].rearrange("(t p) d -> p t d", p=P))
            turned = U["turn.n1_1"][-1]
            pool.wait_ge(bank_full[turned.bank], turned.before + 1)
            load("dft_loaded", dft, A["dft"])
            gain_row(8)
            gain_row(9)
            gain_row(10)
            pool.wait_ge(sem("hyena_y"), 8)
            load("bias1_gate1", gate, A["b_mod"][1, 2 * D:3 * D].partition_broadcast(P))
            pool.wait_ge(sem("gate_used"), 2)
            load("bias1_pre2", shift, A["b_mod"][1, 3 * D:4 * D].partition_broadcast(P))
            load("bias1_pre2", scale, A["b_mod"][1, 4 * D:5 * D].partition_broadcast(P))
            load("bias1_gate2", gate2, A["b_mod"][1, 5 * D:6 * D].partition_broadcast(P))

        @block.tensor
        def _(pe):
            mm = nc.tensor.matmul

            def claim(u):
                if u.before:
                    pe.wait_ge(bank_drained[u.bank], u.before)

            def tell(ins, u):
                ins.then_inc(bank_full[u.bank], 1)

            def slab_in(idx):
                pe.wait_ge(slab_loaded[idx % RING], 16 * (idx // RING + 1))

            def turn(name, src):
                for j, u in enumerate(U[name]):
                    claim(u)
                    for i in range(4):
                        k = 4 * (j % 2) + i
                        last = nc.tensor.transpose(banks[u.bank][:, i * P:(i + 1) * P],
                                                   src[:, j // 2, k * P:(k + 1) * P], ident)
                    tell(last, u)

            def turned(name):
                for u in U[name]:
                    drained(pe, u)

            def project(units, idx, n, lhs, k_tiles=KD, c0=0, width=None, release=True):
                w = view_k(slab_ap(idx), k_tiles, width or n)
                for tile, u in enumerate(units):
                    claim(u)
                    for k in range(k_tiles):
                        last = mm(banks[u.bank][:, 0:n], lhs(k, tile), w[:, k, c0:c0 + n],
                                  start=(k == 0), stop=(k == k_tiles - 1))
                    tell(last, u)

            def project_cols(units, idx, rhs):
                w = view_k(slab_ap(idx), KD, 512)
                for j, u in enumerate(units):
                    claim(u)
                    for i in range(2):
                        f0 = (2 * j + i) * P
                        for k in range(KD):
                            last = mm(banks[u.bank][:, i * S:(i + 1) * S], w[:, k, f0:f0 + P], rhs[:, k, :],
                                      start=(k == 0), stop=(k == KD - 1))
                    tell(last, u)

            def tokens(k, tile):
                return xT3[:, k, tile * P:(tile + 1) * P]

            def turn_heads(name, n, src, dk, tiles=NT):
                blocks = [(hh, t) for hh in range(n) for t in range(tiles)]
                for j, u in enumerate(U[name]):
                    claim(u)
                    for i, (hh, t) in enumerate(blocks[4 * j:4 * j + 4]):
                        last = nc.tensor.transpose(banks[u.bank][0:dk, i * P:(i + 1) * P], src(hh, t), ident)
                    tell(last, u)

            def attend(name, steps, maps, logits, n_blocks, probs, ready, pT, values):
                for s in range(steps + 2):
                    if s < steps:
                        for m in range(maps):
                            u = U[name + ".logits"][s * maps + m]
                            claim(u)
                            for c0, n, lhsT, rhs in logits(s, m):
                                last = mm(banks[u.bank][:, c0:c0 + n], lhsT, rhs, start=True, stop=True)
                            tell(last, u)
                    if 1 <= s <= steps:
                        u = U[name + ".turn"][s - 1]
                        claim(u)
                        ready(s - 1)
                        for b in range(n_blocks):
                            last = nc.tensor.transpose(banks[u.bank][:, b * P:(b + 1) * P],
                                                       probs(s - 1)[:, b * P:(b + 1) * P], ident)
                        tell(last, u)
                    if s >= 2:
                        u = U[name + ".out"][s - 2]
                        claim(u)
                        drained(pe, U[name + ".turn"][s - 2])
                        for c0, n, terms in values(s - 2):
                            for i, (b, v) in enumerate(terms):
                                last = mm(banks[u.bank][:, c0:c0 + n], pT(s - 2)[:, b * P:(b + 1) * P], v,
                                          start=(i == 0), stop=(i == len(terms) - 1))
                        tell(last, u)

            def add_gate_inputs(name, width):
                for i, idx in enumerate(K[name]):
                    slab_in(idx)
                    per = len(U[name]) // len(K[name])
                    project(U[name][per * i:per * (i + 1)], idx, 512,
                            lambda k, tile: c_wide[:, (tile * KD + k) * P:(tile * KD + k + 1) * P])

            pe.wait_ge(sem("resident_loaded"), 16)

            pe.wait_ge(normed, 1)
            turn("turn.mix0", u3)
            turned("turn.mix0")
            for name in ("hgrn_f", "hgrn_q"):
                slab_in(K[name][0])
                project_cols(U[name], K[name][0], xT3)
            u = U["fox_f"][0]
            pe.wait_ge(sem("fox_f_loaded"), 16)
            for tile in range(NT):
                for k in range(KD):
                    last = mm(banks[u.bank][:, tile * 8:(tile + 1) * 8], tokens(k, tile),
                              w_fox_f[:, k * 8:(k + 1) * 8], start=(k == 0), stop=(k == KD - 1))
            tell(last, u)
            for name in ("hgrn_i", "fox_q", "fox_k", "fox_v", "hgrn_g"):
                slab_in(K[name][0])
                project(U[name], K[name][0], 512, tokens)
            u = U["fox_cum"][0]
            claim(u)
            pe.wait_ge(sem("fox_logf"), 1)
            pe.wait_ge(sem("even_tables_loaded"), 16)
            logf = route_logf
            mm(banks[u.bank][:, 0:8], tri, logf[:, 0:8], start=True, stop=True)
            mm(banks[u.bank][:, 8:16], ones, logf[:, 0:8], start=True, stop=False)
            tell(mm(banks[u.bank][:, 8:16], tri, logf[:, 8:16], start=False, stop=True), u)
            for n, name in enumerate([f"level{L}" for L in HGRN_LEVELS] + ["diagonal", "level128"]):
                pe.wait_ge(sem("hgrn_factors"), n + 1)
                for j, u in enumerate(U[name]):
                    claim(u)
                    half, tile = j % 2, j // 2
                    s0, t0 = (tile, tile) if name != "level128" else (0, 1)
                    for c in range(4):
                        lo = half * 64
                        kh = hg_kh[lo:lo + 64, c * S + s0 * P:c * S + (s0 + 1) * P]
                        qh = hg_qh[lo:lo + 64, c * S + t0 * P:c * S + (t0 + 1) * P]
                        last = mm(banks[u.bank][:, c * P:(c + 1) * P], kh, qh, start=True, stop=True)
                    tell(last, u)
            for u in U["level128"]:
                drained(pe, u)
            for tile in range(NT):
                u = U["hgrn_o"][tile]
                claim(u)
                for hh in range(8):
                    c, half = hh // 2, hh % 2
                    dst = banks[u.bank][:, hh * 64:(hh + 1) * 64]
                    own = hg_P[:, 2 * tile + half, c, :]
                    last = mm(dst, own, hg_i[:, tile, hh * 64:(hh + 1) * 64], start=True, stop=(tile == 0))
                    if tile == 1:
                        last = mm(dst, hg_P[:, 4 + half, c, :], hg_i[:, 0, hh * 64:(hh + 1) * 64],
                                  start=False, stop=True)
                tell(last, u)
            pe.wait_ge(sem("fox_aug"), 1)
            turn_heads("fox_qT", 8, lambda hh, t: fq_aug[:, t, hh, :], 66)
            turn_heads("fox_kT", 8, lambda hh, t: fk_aug[:, t, hh, :], 66)
            turned("fox_qT")
            turned("fox_kT")

            def fox_logits(s, m):
                return [(c0, n, fx_qT[0:66, s * S + t * P:s * S + (t + 1) * P], fx_kT[0:66, s * S:s * S + n])
                        for t, c0, n in CAUSAL]

            attend("fox", 8, 1, fox_logits, 3, lambda s: att_P[:, (s % 2) * 1024:(s % 2) * 1024 + 384],
                   lambda s: pe.wait_ge(sem("fox_exp"), 2 * s + 2),
                   lambda s: fx_T[:, (s % 2) * 512:(s % 2) * 512 + 384],
                   lambda s: [(0, 64, [(0, fx_v[:, 0, s * 64:(s + 1) * 64])]),
                              (64, 64, [(1, fx_v[:, 0, s * 64:(s + 1) * 64]), (2, fx_v[:, 1, s * 64:(s + 1) * 64])])])
            pe.wait_ge(sem("fox_o"), 8)
            turn("turn.even_out", ev_o)
            turned("turn.even_out")
            for i, idx in enumerate(K["even_out"]):
                slab_in(idx)
                project(U["even_out"][2 * i:2 * i + 2], idx, 512, tokens)

            def moe(layer):
                name = f"moe{layer}"
                pe.wait_ge(normed, 2 * layer + 2)
                turn(f"turn.ffn{layer}", u3)
                turned(f"turn.ffn{layer}")
                u = U[f"router{layer}"][0]
                claim(u)
                pe.wait_ge(sem("routers_loaded"), 32)
                for tile in range(NT):
                    for k in range(KD):
                        at_k = layer * 288 + k * 36
                        last = mm(banks[u.bank][:, tile * 36:(tile + 1) * 36], tokens(k, tile),
                                  routers[:, at_k:at_k + 36], start=(k == 0), stop=(k == KD - 1))
                tell(last, u)
                u = U[f"rank{layer}"][0]
                claim(u)
                pe.wait_ge(sem("routed"), layer + 1)
                dst = banks[u.bank]
                mm(dst[:, 0:32], tri, routed[:, 0], start=True, stop=True)
                mm(dst[:, 32:64], ones, routed[:, 0], start=True, stop=False)
                mm(dst[:, 32:64], tri, routed[:, 1], start=False, stop=True)
                mm(dst[:, 64:96], ones, routed[:, 0], start=True, stop=False)
                tell(mm(dst[:, 64:96], ones, routed[:, 1], start=False, stop=True), u)
                with short_path(pe, layer):
                    moe_short(layer)
                with pe.Else():
                    moe_dense(layer)

            def moe_short(layer):
                first = K[f"moe{layer}"][0]

                def enter(u):
                    pe.wait_ge(bank_drained[u.bank], u.before)
                    return banks[u.bank]

                def slab_of(i, j, k, n):
                    idx = first + j
                    pe.wait_ge(slab_loaded[idx % RING], i * 16 + 16 * (idx // RING + 1))
                    return view_k(slab_ap(idx), k, n)

                def gather(i):
                    pe.wait_ge(sem(f"seats{layer}"), i + 1)
                    for j in range(2):
                        u = moe_unit(layer, 2 + j, 0, i)
                        dst = enter(u)
                        for c in range(4):
                            k = 4 * j + c
                            for t in range(NT):
                                last = mm(dst[:, c * P:(c + 1) * P], u3[:, t, k * P:(k + 1) * P], sel[:, t, :],
                                          start=(t == 0), stop=(t == 1))
                        tell(last, u)

                def gate_and_up(i):
                    for j in range(2):
                        drained(pe, moe_unit(layer, 2 + j, 0, i))
                    for e in range(2):
                        for w in range(2):
                            slab = slab_of(i, EXPERT_SLABS * e + w, KD, 512)
                            u = moe_unit(layer, 2 * e + w, e, i)
                            dst = enter(u)
                            for f in range(4):
                                for k in range(KD):
                                    last = mm(dst[:, f * SEATS:(f + 1) * SEATS], slab[:, k, f * P:(f + 1) * P],
                                              seated[:, k, e * SEATS:(e + 1) * SEATS], start=(k == 0), stop=(k == KD - 1))
                            tell(last, u)

                def turn_back(i):
                    for e in range(2):
                        drained(pe, moe_unit(layer, e, 1, i))
                    for j in range(2):
                        u = moe_unit(layer, 4 + j, 0, i)
                        dst = enter(u)
                        for c in range(4):
                            last = nc.tensor.transpose(dst[:, c * P:(c + 1) * P], pair_yT[:, 4 * j + c, :], ident)
                        tell(last, u)
                    pe.wait_ge(sem(f"weights{layer}"), i + 1)
                    for t in range(NT):
                        u = moe_unit(layer, 6 + t, 0, i)
                        tell(nc.tensor.transpose(enter(u)[:, 0:P], weighted[:, t, :], ident), u)

                def down(i):
                    for e in range(2):
                        slab = slab_of(i, EXPERT_SLABS * e + 2, 4, D)
                        drained(pe, moe_unit(layer, 2 * e + 1, e, i))
                        u = moe_unit(layer, e, 1, i)
                        dst = enter(u)
                        for k in range(KD):
                            for f in range(4):
                                last = mm(dst[:, k * SEATS:(k + 1) * SEATS], slab[:, f, k * P:(k + 1) * P],
                                          pair_hidden[:, e, f * SEATS:(f + 1) * SEATS], start=(f == 0), stop=(f == 3))
                        tell(last, u)

                def scatter(i):
                    for j in range(2):
                        drained(pe, moe_unit(layer, 4 + j, 0, i))
                        drained(pe, moe_unit(layer, 6 + j, 0, i))
                    for j in range(4):
                        u = moe_unit(layer, 4 + j, 1, i)
                        tell(mm(enter(u)[:, :], weightedT[:, (j // 2) * P:(j // 2 + 1) * P],
                                pair_y[:, (j % 2) * 512:(j % 2 + 1) * 512], start=True, stop=True), u)

                gather(0)
                gate_and_up(0)
                down(0)
                gather(1)
                with pe.Fori(1, PAIRS - 1) as i:
                    gate_and_up(i)
                    turn_back(i - 1)
                    down(i)
                    gather(i + 1)
                    scatter(i - 1)
                gate_and_up(PAIRS - 1)
                turn_back(PAIRS - 2)
                down(PAIRS - 1)
                scatter(PAIRS - 2)
                turn_back(PAIRS - 1)
                scatter(PAIRS - 1)

            def moe_dense(layer):
                name = f"moe{layer}"
                first = K[name][0]
                with pe.Fori(0, PAIRS) as i:
                    for e in range(2):
                        ups = [[x.later(i * 2) for x in U[name + kind][2 * e:2 * e + 2]] for kind in (".gate", ".up")]
                        for w, units in enumerate(ups):
                            idx = first + EXPERT_SLABS * e + w
                            pe.wait_ge(slab_loaded[idx % RING], i * 16 + 16 * (idx // RING + 1))
                            slab = view_k(slab_ap(idx), KD, 512)
                            for j, u in enumerate(units):
                                pe.wait_ge(bank_drained[u.bank], u.before)
                                for c in range(2):
                                    f0 = (2 * j + c) * P
                                    for k in range(KD):
                                        last = mm(banks[u.bank][:, c * S:(c + 1) * S], slab[:, k, f0:f0 + P],
                                                  xT3[:, k, :], start=(k == 0), stop=(k == KD - 1))
                                tell(last, u)
                        idx = first + EXPERT_SLABS * e + 2
                        pe.wait_ge(slab_loaded[idx % RING], i * 16 + 16 * (idx // RING + 1))
                        for u in ups[1]:
                            pe.wait_ge(bank_drained[u.bank], u.before + 1)
                        slab = view_k(slab_ap(idx), 4, D)
                        for j in range(4):
                            u = U[name + ".down"][4 * e + j].later(i * 2)
                            pe.wait_ge(bank_drained[u.bank], u.before)
                            for f in range(4):
                                last = mm(banks[u.bank][:, :], hidden[:, f * S + (j // 2) * P:f * S + (j // 2 + 1) * P],
                                          slab[:, f, (j % 2) * 512:(j % 2 + 1) * 512], start=(f == 0), stop=(f == 3))
                            tell(last, u)

            moe(0)

            pe.wait_ge(normed, 3)
            turn("turn.mix1", u3)
            turned("turn.mix1")
            for i, idx in enumerate(K["odd_in"]):
                slab_in(idx)
                project(U["odd_in"][2 * i:2 * i + 2], idx, 512, tokens)
            pe.wait_ge(sem("odd_qk"), 1)
            turn_heads("diff_qT", 16, lambda hh, t: od_q[:, t * D + hh * 64:t * D + (hh + 1) * 64], 64)
            pe.wait_ge(sem("odd_qk"), 2)
            turn_heads("diff_kT", 16, lambda hh, t: od_k[:, t * D + hh * 64:t * D + (hh + 1) * 64], 64)
            turned("diff_qT")
            turned("diff_kT")

            def diff_logits(s, m):
                c = (2 * s + m) * S
                return [(c0, n, od_qT[0:64, c + t * P:c + (t + 1) * P], od_kT[0:64, c:c + n]) for t, c0, n in CAUSAL]

            attend("diff", 8, 2, diff_logits, 3, lambda s: att_P[:, (s % 2) * 1024:(s % 2) * 1024 + 384],
                   lambda s: pe.wait_ge(sem("diff_probs"), s + 1),
                   lambda s: od_T[:, (s % 2) * 512:(s % 2) * 512 + 384],
                   lambda s: [(0, P, [(0, od_v[:, 0, s * P:(s + 1) * P])]),
                              (P, P, [(1, od_v[:, 0, s * P:(s + 1) * P]), (2, od_v[:, 1, s * P:(s + 1) * P])])])
            pe.wait_ge(sem("diff_o"), 1)
            turn("turn.odd_out", od_o)
            turned("turn.odd_out")
            for i, idx in enumerate(K["odd_out"]):
                slab_in(idx)
                project(U["odd_out"][2 * i:2 * i + 2], idx, 512, tokens)
            moe(1)

            pe.wait_ge(sem("c_wide_ready"), 1)
            add_gate_inputs("mod0.pre1", 2)
            pe.wait_ge(sem("ctx_normed"), 1)
            turn("turn.n1_0", ctx_u.rearrange("p (t d) -> p t d", t=NT))
            pe.wait_ge(normed, 5)
            turn("turn.ctx", u3)
            turned("turn.n1_0")
            turned("turn.ctx")

            def all_tokens(k, tile):
                return tokens(k, tile) if tile < 2 else ctxT[:, k, (tile - 2) * P:(tile - 1) * P]

            for name, n in (("mla_cq", 384), ("mla_ckv", 288), ("gqa_q", 512), ("gqa_kv", 256)):
                slab_in(K[name][0])
                project(U[name], K[name][0], n, all_tokens)
            pe.wait_ge(sem("lora_ready"), 1)
            for t, u in enumerate(U["turn.cq"]):
                claim(u)
                for k in range(3):
                    c0 = t * 384 + k * P
                    last = nc.tensor.transpose(banks[u.bank][:, k * P:(k + 1) * P], z_cq[:, c0:c0 + P], ident)
                tell(last, u)
            for k, u in enumerate(U["turn.ckv"]):
                claim(u)
                for t in range(4):
                    last = nc.tensor.transpose(banks[u.bank][:, t * P:(t + 1) * P],
                                               c_kv[:, t, k * P:(k + 1) * P], ident)
                tell(last, u)
            turned("turn.cq")
            turned("turn.ckv")
            slab_in(K["mla_q"][0])
            for half in range(2):
                project(U["mla_q"][2 * half:2 * half + 2], K["mla_q"][0], 384,
                        lambda k, tile: cqT[:, k, tile * P:(tile + 1) * P], 3, 384 * half, 768)
            slab_in(K["mla_kv"][0])
            for half in range(2):
                project(U["mla_kv"][4 * half:4 * half + 4], K["mla_kv"][0], 512,
                        lambda k, tile: ckvT[:, k, tile * P:(tile + 1) * P], 2, 512 * half, D)
            pe.wait_ge(sem("mla_qk"), 1)
            turn_heads("mla_qT", 8, lambda hh, t: ml_q[:, t * 768 + hh * 96:t * 768 + (hh + 1) * 96], 96)
            turn_heads("mla_kT", 8, lambda hh, t: ml_k[:, t * 768 + hh * 96:t * 768 + (hh + 1) * 96], 96, 4)
            turned("mla_qT")
            turned("mla_kT")

            def full_logits(dk, group):
                def logits(s, m):
                    hh, t = s // 2, s % 2
                    kv = hh // group
                    return [(0, 512, qT2[0:dk, hh * S + t * P:hh * S + (t + 1) * P], kT2[0:dk, kv * 512:(kv + 1) * 512])]
                return logits

            def b2_probs(s):
                return b2_P[:, (s % 2) * 512:(s % 2 + 1) * 512]

            def b2_turned(s):
                return b2_T[:, (s % 2) * 512:(s % 2 + 1) * 512]

            attend("mla", 16, 1, full_logits(96, 1), 4, b2_probs,
                   lambda s: drained(pe, U["mla.logits"][s]), b2_turned,
                   lambda s: [(0, 64, [(t, ml_v[:, t, s // 2, :]) for t in range(4)])])
            pe.wait_ge(sem("gqa_qk"), 1)
            turn_heads("gqa_qT", 8, lambda hh, t: z_gq[:, t * 512 + hh * 64:t * 512 + (hh + 1) * 64], 64)
            turn_heads("gqa_kT", 2, lambda hh, t: z_gk[:, t * P + hh * 64:t * P + (hh + 1) * 64], 64, 4)
            turned("gqa_qT")
            turned("gqa_kT")
            attend("gqa", 16, 1, full_logits(64, 4), 4, b2_probs,
                   lambda s: drained(pe, U["gqa.logits"][s]), b2_turned,
                   lambda s: [(0, 64, [(t, z_gv[:, t, s // 8 * 64:(s // 8 + 1) * 64]) for t in range(4)])])
            add_gate_inputs("mod0.gate1", 1)
            pe.wait_ge(sem("gqa_o"), 16)
            turn("turn.a_out", b2_o)
            turned("turn.a_out")
            for i, idx in enumerate(K["a_out"]):
                slab_in(idx)
                project(U["a_out"][2 * i:2 * i + 2], idx, 512, tokens)
            add_gate_inputs("mod0.pre2", 1)

            def mlp(layer):
                name = f"mlp{layer}"
                for j in range(8):
                    idx = K[name][2 * j]
                    slab_in(idx)
                    project_cols(U[name + ".hidden"][2 * j:2 * j + 2], idx, xT3)
                    slab_in(idx + 1)
                    for u in U[name + ".hidden"][2 * j:2 * j + 2]:
                        drained(pe, u)
                    slab = view_k(slab_ap(idx + 1), 4, D)
                    for i in range(4):
                        u = U[name + ".out"][4 * j + i]
                        claim(u)
                        for f in range(4):
                            last = mm(banks[u.bank][:, :], hidden[:, f * S + (i // 2) * P:f * S + (i // 2 + 1) * P],
                                      slab[:, f, (i % 2) * 512:(i % 2 + 1) * 512], start=(f == 0), stop=(f == 3))
                        tell(last, u)

            pe.wait_ge(normed, 6)
            turn("turn.n2_0", u3)
            turned("turn.n2_0")
            add_gate_inputs("mod0.gate2", 1)
            mlp(0)

            pe.wait_ge(sem("c_wide_ready"), 2)
            add_gate_inputs("mod1.pre1", 1)
            pe.wait_ge(normed, 7)
            turn("turn.n1_1", u3)
            turned("turn.n1_1")
            pe.wait_ge(sem("filter_loaded"), 64)
            for i, u in enumerate(U["filter_mlp"]):
                claim(u)
                if i == 0:
                    last = mm(banks[u.bank][0:64, 0:S], small[0:17, 256:320], small[0:17, 0:256], start=True, stop=True)
                else:
                    pe.wait_ge(sem("filter_h"), i)
                    last = mm(banks[u.bank][0:64, 0:S], small[0:64, 256 + 64 * i:320 + 64 * i], f_h[0:64, :],
                              start=True, stop=True)
                tell(last, u)
            pe.wait_ge(sem("filter_h"), 3)
            idx = K["filter_w4"][0]
            slab_in(idx)
            pe.wait_ge(sem("dft_loaded"), 16)
            for n in range(2):
                for j, u in enumerate(U[f"filter{n}"]):
                    direction, tile, half = j // 4, j // 2 % 2, j % 2
                    claim(u)
                    c0 = direction * 2048 + n * D + half * 512
                    tell(mm(banks[u.bank][:, :], f_h[0:64, tile * P:(tile + 1) * P], slab_ap(idx)[0:64, c0:c0 + 512],
                            start=True, stop=True), u)
                for half, u in enumerate(U[f"filter_norm{n}"]):
                    claim(u)
                    pe.wait_ge(sem("filter_squares"), 2 * n + half + 1)
                    for i in range(4):
                        last = mm(banks[u.bank][:, :], ones, f_sum[:, i * 512:(i + 1) * 512], start=(i == 0), stop=(i == 3))
                    tell(last, u)
                for j, u in enumerate(U[f"filter_dft{n}"]):
                    kind, ft, half = j // 4, j // 2 % 2, j % 2
                    claim(u)
                    pe.wait_ge(sem("filter_sums"), 2 * n + kind + 1)
                    table, src = ((cosT, f_sum), (sinT, f_diff))[kind]
                    for k in range(NT):
                        last = mm(banks[u.bank][:, :], table[:, k, ft * P:(ft + 1) * P],
                                  src[:, k * D + half * 512:k * D + (half + 1) * 512], start=(k == 0), stop=(k == 1))
                    tell(last, u)
            for i in range(6):
                idx = K["hyena_in"][i]
                slab_in(idx)
                project_cols(U["hyena_in"][2 * i:2 * i + 2], idx, xT3)
                pe.wait_ge(sem("conv_ready"), i + 1)
                for tile in range(NT):
                    u = U["hyena_turn"][2 * i + tile]
                    claim(u)
                    for c in range(4):
                        last = nc.tensor.transpose(banks[u.bank][:, c * P:(c + 1) * P],
                                                   conv[:, c * S + tile * P:c * S + (tile + 1) * P], ident)
                    tell(last, u)
            for u in U["hyena_turn"]:
                drained(pe, u)
            for n in range(2):
                if n == 1:
                    pe.wait_ge(sem("hyena_y"), 4)
                for j, u in enumerate(U[f"dft{n}"]):
                    ft, half, kind = j // 4, j // 2 % 2, j % 2
                    claim(u)
                    table = (cosT, sinT)[kind]
                    for k in range(NT):
                        last = mm(banks[u.bank][:, :], table[:, k, ft * P:(ft + 1) * P],
                                  hy_x[2][:, k * D + half * 512:k * D + (half + 1) * 512], start=(k == 0), stop=(k == 1))
                    tell(last, u)
                pe.wait_ge(sem("spectrum_ready"), 4 * (n + 1))
                for j, u in enumerate(U[f"idft{n}"]):
                    tile, half = j // 2, j % 2
                    claim(u)
                    for i, (table, src) in enumerate(((icos, y_re), (isin, y_im))):
                        for k in range(NT):
                            last = mm(banks[u.bank][:, :], table[:, k, tile * P:(tile + 1) * P],
                                      src[:, k * D + half * 512:k * D + (half + 1) * 512],
                                      start=(i == 0 and k == 0), stop=(i == 1 and k == 1))
                    tell(last, u)
            pe.wait_ge(sem("c_wide_ready"), 3)
            add_gate_inputs("mod1.gate1", 1)
            pe.wait_ge(sem("hyena_y"), 8)
            turn("turn.hyena_out", hy_x[2].rearrange("p (t d) -> p t d", t=NT))
            turned("turn.hyena_out")
            for i, idx in enumerate(K["hyena_out"]):
                slab_in(idx)
                project(U["hyena_out"][2 * i:2 * i + 2], idx, 512, tokens)
            add_gate_inputs("mod1.pre2", 1)
            pe.wait_ge(normed, 8)
            turn("turn.n2_1", u3)
            turned("turn.n2_1")
            add_gate_inputs("mod1.gate2", 1)
            mlp(1)

        @block.scalar
        def _(act):
            act_fn = nc.scalar.activation
            calls = [0]
            steps = [0]

            def link(ins):
                steps[0] += 1
                ins.then_inc(act_step, 1)
                act.wait_ge(act_step, steps[0])

            def root(n, groups, src=None):
                calls[0] += 1
                act.wait_ge(stats_ready, calls[0])
                act_fn(s_std[:, 0:groups], s_sum[:, 0:groups], ACT.Sqrt, bias=eps_col, scale=1.0 / n)\
                    .then_inc(std_ready, 1)

            def copy_out(u, dst, src, func=ACT.Copy):
                full(act, u)
                act_fn(dst, src, func).then_inc(bank_drained[u.bank], 1)

            def turn(name, dst):
                for j in (1, 3):
                    u = U[name][j]
                    copy_out(u, dst[:, 4:8, (j // 2) * P:(j // 2 + 1) * P],
                             banks[u.bank][:, :].rearrange("p (k s) -> p k s", k=4))

            def copies(name, dst, p=P):
                for j, u in enumerate(U[name]):
                    copy_out(u, dst[0:p, j * 512:(j + 1) * 512], banks[u.bank][0:p, :])

            act.wait_ge(sem("eps_ready"), 1)
            root(D, NT)
            turn("turn.mix0", xT3)
            act.wait_ge(sem("lb_diff"), 1)
            act_fn(lb_col, s_inv[:, 0:4], ACT.Sigmoid).then_inc(sem("lb_ready"), 1)
            for j, u in enumerate(U["hgrn_f"]):
                copy_out(u, hg_f[:, j * 512:(j + 1) * 512], banks[u.bank][:, :], ACT.Sigmoid)
            for j, u in enumerate(U["hgrn_q"]):
                copy_out(u, hg_q[:, j * 512:(j + 1) * 512], banks[u.bank][:, :], ACT.Silu)
            for j, u in enumerate(U["hgrn_i"]):
                copy_out(u, hg_i[:, j, :], banks[u.bank][:, :])
            for j, u in enumerate(U["fox_v"]):
                copy_out(u, fx_v[:, j, :], banks[u.bank][:, :])
            for j, u in enumerate(U["hgrn_g"]):
                copy_out(u, hg_g[:, j * 512:(j + 1) * 512], banks[u.bank][:, :], ACT.Silu)
            act.wait_ge(sem("hgrn_forget"), 1)
            act_fn(hg_qh, hg_f, ACT.Ln).then_inc(sem("hgrn_logf"), 1)
            act.wait_ge(sem("fox_absf"), 1)
            link(act_fn(small[:, 464:480], small[:, 464:480], ACT.Exp))
            act_fn(small[:, 464:480], small[:, 464:480], ACT.Ln, bias=1.0).then_inc(sem("fox_softplus"), 1)
            for n in range(6):
                act.wait_ge(sem("hgrn_exponents"), n + 1)
                src, dst = at(0, 1024), at(1024, 1024)
                if n == len(HGRN_LEVELS):
                    act_fn(hg_kh, src, ACT.Exp, scale=-1.0).then_inc(sem("hgrn_exps"), 1)
                    act_fn(dst, src, ACT.Exp).then_inc(sem("hgrn_exps"), 1)
                else:
                    act_fn(dst, src, ACT.Exp).then_inc(sem("hgrn_exps"), 1)
            root(64, 16)
            root(64, 16)
            root(64, 16)
            copies("fox_qT", fx_qT, 66)
            copies("fox_kT", fx_kT, 66)
            SEG = [(0, P), (P, 2 * P)]

            def masked_attend(name, maps, L, pT, done):
                for s in range(9):
                    if s < 8:
                        for m in range(maps):
                            act.wait_ge(sem(name + "_max"), s * maps + m + 1)
                            if s >= 2 and m == 0:
                                full(act, U[name + ".turn"][s - 2])
                            P_m = att_P[:, (s % 2) * 1024 + m * 384:(s % 2) * 1024 + (m + 1) * 384]
                            L_m = L[:, (s % 2) * 768 + m * 384:(s % 2) * 768 + (m + 1) * 384]
                            for g, (c0, n) in enumerate(SEG):
                                ins = act_fn(P_m[:, c0:c0 + n], L_m[:, c0:c0 + n], ACT.Exp,
                                             bias=neg_max[:, s % 2, m, g:g + 1],
                                             accum_out=exp_sum[:, s % 4, m, g:g + 1])
                                ins.then_inc(sem(done), 1)
                    if s >= 1:
                        u = U[name + ".turn"][s - 1]
                        if s >= 3:
                            full(act, U[name + ".out"][s - 3])
                        T = pT[:, ((s - 1) % 2) * 512:((s - 1) % 2) * 512 + 384]
                        copy_out(u, T, banks[u.bank][:, 0:384])

            def full_attend(name):
                for s in range(17):
                    if s < 16:
                        u = U[name + ".logits"][s]
                        act.wait_ge(sem(name + "_max"), s + 1)
                        if s >= 2:
                            full(act, U[name + ".turn"][s - 2])
                        act_fn(b2_P[:, (s % 2) * 512:(s % 2 + 1) * 512], banks[u.bank][:, :], ACT.Exp,
                               bias=neg_max[:, s % 2, 0, 0:1],
                               accum_out=exp_sum[:, s % 4, 0, 0:1]).then_inc(bank_drained[u.bank], 1)
                    if s >= 1:
                        u = U[name + ".turn"][s - 1]
                        if s >= 3:
                            full(act, U[name + ".out"][s - 3])
                        copy_out(u, b2_T[:, ((s - 1) % 2) * 512:((s - 1) % 2 + 1) * 512], banks[u.bank][:, :])

            masked_attend("fox", 1, fx_L, fx_T, "fox_exp")
            turn("turn.even_out", xT3)

            def moe(layer):
                name = f"moe{layer}"
                root(D, NT)
                turn(f"turn.ffn{layer}", xT3)
                act.wait_ge(sem("routed"), layer + 1)
                act_fn(route[:, 64:64 + 2 * 8], route[:, 64:64 + 2 * 8], ACT.Exp).then_inc(sem("route_exp_out"), 1)
                with short_path(act, layer):
                    moe_short(layer)
                with act.Else():
                    moe_dense(layer)

            def moe_short(layer):
                def out_of(u, dst, src, func=ACT.Copy):
                    act.wait_ge(bank_full[u.bank], u.before + 1)
                    act_fn(dst, src, func).then_inc(bank_drained[u.bank], 1)

                def gather(i):
                    for j in range(2):
                        u = moe_unit(layer, 2 + j, 0, i)
                        out_of(u, seated[:, 4 * j:4 * j + 4, :], banks[u.bank][:, :].rearrange("p (k c) -> p k c", k=4))

                def gate(i):
                    for e in range(2):
                        u = moe_unit(layer, 2 * e, e, i)
                        out_of(u, pair_silu[:, e, :], banks[u.bank][:, 0:4 * SEATS], ACT.Silu)

                def turn_back(i):
                    for j in range(2):
                        u = moe_unit(layer, 4 + j, 0, i)
                        out_of(u, pair_y[:, j * 512:(j + 1) * 512], banks[u.bank][:, :])
                    for t in range(NT):
                        u = moe_unit(layer, 6 + t, 0, i)
                        out_of(u, weightedT[:, t * P:(t + 1) * P], banks[u.bank][:, 0:P])

                def down(i):
                    for e in range(2):
                        u = moe_unit(layer, e, 1, i)
                        out_of(u, pair_yT[:, :, e * SEATS:(e + 1) * SEATS],
                               banks[u.bank][:, :].rearrange("p (k c) -> p k c", k=KD))

                gather(0)
                gate(0)
                down(0)
                gather(1)
                with act.Fori(1, PAIRS - 1) as i:
                    gate(i)
                    turn_back(i - 1)
                    down(i)
                    gather(i + 1)
                gate(PAIRS - 1)
                turn_back(PAIRS - 2)
                down(PAIRS - 1)
                turn_back(PAIRS - 1)

            def moe_dense(layer):
                name = f"moe{layer}"
                with act.Fori(0, PAIRS) as i:
                    for e in range(2):
                        for j in range(2):
                            u = U[name + ".gate"][2 * e + j].later(i * 2)
                            up = U[name + ".up"][2 * e + j].later(i * 2)
                            act.wait_ge(bank_drained[up.bank], up.before)
                            act.wait_ge(bank_full[u.bank], u.before + 1)
                            act_fn(silu_g[:, j * 512:(j + 1) * 512], banks[u.bank][:, :], ACT.Silu)\
                                .then_inc(bank_drained[u.bank], 1)

            moe(0)
            root(D, NT)
            turn("turn.mix1", xT3)
            for j, u in enumerate(U["odd_in"]):
                dst = (od_q.rearrange("p (t d) -> p t d", t=NT), od_k.rearrange("p (t d) -> p t d", t=NT), od_v)[j // 4]
                copy_out(u, dst[:, j % 2, (j // 2 % 2) * 512:(j // 2 % 2 + 1) * 512], banks[u.bank][:, :])
            act.wait_ge(sem("angles_ready"), 1)
            act_fn(od_tab[:, 0:128], od_tab[:, 0:128], ACT.Sin).then_inc(sem("rope_ready"), 1)
            act.wait_ge(sem("lam_sums"), 1)
            act_fn(small[:, 480:482], small[:, 480:482], ACT.Exp).then_inc(sem("lam_exps"), 1)
            root(64, 32)
            root(64, 32)
            copies("diff_qT", od_qT, 64)
            copies("diff_kT", od_kT, 64)
            masked_attend("diff", 2, od_L, od_T, "diff_exp")
            root(P, 16)
            turn("turn.odd_out", xT3)
            moe(1)
            act.wait_ge(sem("c_copied"), 1)
            act_fn(small[:, 464:480], small[:, 464:480], ACT.Silu).then_inc(sem("c_silu"), 1)
            root(D, NT)
            turn("turn.n1_0", ctxT)
            root(D, NT)
            turn("turn.ctx", xT3)
            for j, u in enumerate(U["mla_cq"]):
                copy_out(u, z_cq[:, j * 384:(j + 1) * 384], banks[u.bank][:, 0:384])
            for j, u in enumerate(U["mla_ckv"]):
                full(act, u)
                link(act_fn(z_kr[:, j * 32:(j + 1) * 32], banks[u.bank][:, 256:288], ACT.Copy))
                act_fn(c_kv[:, j, :], banks[u.bank][:, 0:256], ACT.Copy).then_inc(bank_drained[u.bank], 1)
            for j, u in enumerate(U["gqa_q"]):
                copy_out(u, z_gq[:, j * 512:(j + 1) * 512], banks[u.bank][:, :])
            for j, u in enumerate(U["gqa_kv"]):
                full(act, u)
                link(act_fn(z_gk[:, j * P:(j + 1) * P], banks[u.bank][:, 0:P], ACT.Copy))
                act_fn(z_gv[:, j, :], banks[u.bank][:, P:2 * P], ACT.Copy).then_inc(bank_drained[u.bank], 1)
            root(384, 2)
            root(256, 4)
            for t, u in enumerate(U["turn.cq"]):
                copy_out(u, cqT[:, :, t * P:(t + 1) * P], banks[u.bank][:, 0:384].rearrange("p (k s) -> p k s", k=3))
            for k, u in enumerate(U["turn.ckv"]):
                copy_out(u, ckvT[:, k, :], banks[u.bank][:, :])
            root(64, 16)
            root(64, 8)
            for j, u in enumerate(U["mla_q"]):
                half, t = j // 2, j % 2
                c0 = t * 768 + half * 384
                copy_out(u, ml_q[:, c0:c0 + 384], banks[u.bank][:, 0:384])
            ml_k4 = ml_k.rearrange("p (t h d) -> p t h d", t=4, h=8)
            for j, u in enumerate(U["mla_kv"]):
                half, t = j // 4, j % 4
                src = banks[u.bank][:, :].rearrange("p (h d) -> p h d", h=4)
                full(act, u)
                link(act_fn(ml_k4[:, t, 4 * half:4 * half + 4, 0:64], src[:, :, 0:64], ACT.Copy))
                act_fn(ml_v[:, t, 4 * half:4 * half + 4, :], src[:, :, 64:P], ACT.Copy)\
                    .then_inc(bank_drained[u.bank], 1)
            copies("mla_qT", qT2, 96)
            copies("mla_kT", kT2, 96)
            full_attend("mla")
            copies("gqa_qT", qT2, 64)
            copies("gqa_kT", kT2, 64)
            full_attend("gqa")
            turn("turn.a_out", xT3)
            root(D, NT)
            turn("turn.n2_0", xT3)
            act.wait_ge(sem("c_copied"), 2)
            act_fn(small[:, 464:480], small[:, 464:480], ACT.Silu).then_inc(sem("c_silu"), 1)
            root(D, NT)
            turn("turn.n1_1", xT3)
            for i in range(3):
                act.wait_ge(sem("filter_angle"), i + 1)
                act_fn(f_h[0:64, :], at(10240, 256)[0:64, :], ACT.Sin).then_inc(sem("filter_h"), 1)
            for n in range(2):
                for half, u in enumerate(U[f"filter_norm{n}"]):
                    full(act, u)
                    if n:
                        act.wait_ge(sem("filter_sums"), 2)
                    act_fn(f_norm[:, half * 512:(half + 1) * 512], banks[u.bank][:, :], ACT.Sqrt, bias=eps_col)\
                        .then_inc(bank_drained[u.bank], 1)
                for j, u in enumerate(U[f"filter_dft{n}"]):
                    c0 = n * 4096 + j * 512
                    copy_out(u, spectra[:, c0:c0 + 512], banks[u.bank][:, :])
            for i in range(6):
                for j in range(2):
                    u = U["hyena_in"][2 * i + j]
                    z4 = z_pad[:, (i % 2) * 1032:(i % 2 + 1) * 1032].rearrange("p (c s) -> p c s", c=4)
                    if i < 2:
                        act.wait_ge(sem("pad_ready"), 1)
                    else:
                        act.wait_ge(sem("conv_ready"), i - 1)
                    copy_out(u, z4[:, 2 * j:2 * j + 2, 1:S + 1],
                             banks[u.bank][:, :].rearrange("p (c s) -> p c s", c=2))
                for tile in range(NT):
                    u = U["hyena_turn"][2 * i + tile]
                    c0 = tile * D + (i % 2) * 512
                    copy_out(u, hy_x[i // 2][:, c0:c0 + 512], banks[u.bank][:, :])
            act.wait_ge(sem("c_copied"), 3)
            act_fn(small[:, 464:480], small[:, 464:480], ACT.Silu).then_inc(sem("c_silu"), 1)
            turn("turn.hyena_out", xT3)
            root(D, NT)
            turn("turn.n2_1", xT3)
            root(D, NT)

        @block.vector
        def _(dve):
            v = nc.vector
            steps = [0]
            calls = [0]
            norms = [0]
            rows_used = [0]

            def link(ins):
                steps[0] += 1
                ins.then_inc(vec_step, 1)
                dve.wait_ge(vec_step, steps[0])

            def drain(ins, u):
                ins.then_inc(bank_drained[u.bank], 1)
                dve.wait_ge(bank_drained[u.bank], u.before + 1)

            def tell(ins, name, count=None):
                told[name] = told.get(name, 0) + 1
                ins.then_inc(sem(name), 1)
                dve.wait_ge(sem(name), told[name])

            told = {}

            def inverse_rms(squares, groups):
                link(v.tensor_reduce(s_sum[:, 0:groups], squares, AX_X, ALU.add))
                calls[0] += 1
                v.tensor_copy(s_sum[:, 0:1], s_sum[:, 0:1]).then_inc(stats_ready, 1)
                dve.wait_ge(std_ready, calls[0])
                link(v.reciprocal(s_inv[:, 0:groups], s_std[:, 0:groups]))

            def group_norm(x, groups, n, squares, gain_ap, outs=None):
                x3 = x.rearrange("p (g n) -> p g n", g=groups)
                sq3 = squares.rearrange("p (g n) -> p g n", g=groups)
                link(v.tensor_tensor(sq3, x3, x3, ALU.mult))
                inverse_rms(sq3, groups)
                link(v.tensor_tensor(sq3, x3, over(s_inv[:, 0:groups], [P, groups, n], 2), ALU.mult))
                dst = x3 if outs is None else outs
                return v.tensor_tensor(dst, sq3 if len(dst.shape) == 3 else sq3.rearrange("p (a g) n -> p a g n", a=2),
                                       over(gain_ap, [P, groups, n], 1) if len(dst.shape) == 3 else
                                       gain_ap.unsqueeze(1).unsqueeze(1).to_broadcast([P, 2, groups // 2, n]), ALU.mult)

            def gain_row():
                n = rows_used[0]
                rows_used[0] += 1
                dve.wait_ge(gain_loaded[n % 2], 16 * (n // 2 + 1))
                return gain[:, (n % 2) * D:(n % 2 + 1) * D]

            def norm(src, dst, g):
                s3 = src.rearrange("p (t d) -> p t d", t=NT)
                d3 = dst.rearrange("p (t d) -> p t d", t=NT)
                link(v.tensor_tensor(d3, s3, s3, ALU.mult))
                inverse_rms(d3, NT)
                for t in range(NT):
                    ins = v.scalar_tensor_tensor(d3[:, t], s3[:, t], s_inv[:, t:t + 1], g, ALU.mult, ALU.mult)
                    if t == 0:
                        link(ins)
                return ins

            def norm_input():
                g = gain_row()
                link(norm(h[:, :], u_buf, g))
                v.tensor_copy(stat[:, 160:161], g[:, 0:1]).then_inc(sem("gain_used"), 1)
                v.tensor_copy(stat[:, 161:162], u_buf[:, 0:1]).then_inc(normed, 1)

            def modulated(src, dst, g, sc, sh):
                d3 = dst.rearrange("p (t d) -> p t d", t=NT)
                link(v.scalar_tensor_tensor(sc, sc, 1.0, g, ALU.add, ALU.mult))
                link(norm(src, dst, sc))
                return v.tensor_tensor(d3, d3, over(sh, [P, NT, D], 1), ALU.add)

            def modulated_input():
                g = gain_row()
                link(modulated(h[:, :], u_buf, g, scale, shift))
                v.tensor_copy(stat[:, 160:161], g[:, 0:1]).then_inc(sem("gain_used"), 1)
                v.tensor_copy(stat[:, 161:162], u_buf[:, 0:1]).then_inc(normed, 1)

            def turn(name, dst):
                for j in (0, 2):
                    u = U[name][j]
                    full(dve, u)
                    drain(v.tensor_copy(dst[:, 0:4, (j // 2) * P:(j // 2 + 1) * P],
                                        banks[u.bank][:, :].rearrange("p (k s) -> p k s", k=4)), u)

            def add_to_h(name):
                for j, u in enumerate(U[name]):
                    full(dve, u)
                    dst = h3[:, j % 2, (j // 2) * 512:(j // 2 + 1) * 512]
                    drain(v.tensor_tensor(dst, dst, banks[u.bank][:, :], ALU.add), u)

            def add_gated(name, g):
                for j, u in enumerate(U[name]):
                    full(dve, u)
                    half = slice((j // 2) * 512, (j // 2 + 1) * 512)
                    tmp = scratch[:, 0:512]
                    drain(v.tensor_tensor(tmp, banks[u.bank][:, :], g[:, half], ALU.mult), u)
                    dst = h3[:, j % 2, half]
                    link(v.tensor_tensor(dst, dst, tmp, ALU.add))

            def add_bias(name, dsts, bias, loads):
                dma_done(dve, bias, loads)
                per = len(U[name]) // len(K[name])
                for j, u in enumerate(U[name]):
                    i, c = j // per, j % per
                    dst = dsts[2 * c + i // 2][:, (i % 2) * 512:(i % 2 + 1) * 512]
                    full(dve, u)
                    drain(v.tensor_tensor(dst, dst, banks[u.bank][:, :], ALU.add), u)

            def widen_c(n):
                tell(v.tensor_copy(small[:, 464:480], cols[:, COLS["c"][0]:COLS["c"][0] + 16]), "c_copied")
                dve.wait_ge(sem("c_silu"), n)
                tell(v.tensor_copy(c_wide.rearrange("p (k n) -> p k n", k=16),
                                   over(small[:, 464:480], [P, 16, P], 2)), "c_wide_ready")

            def rotate(x, groups, axes, nf, cos, sin, tmp):
                shape = [P, groups, axes, nf] if axes > 1 else [P, groups, nf]

                def half(a):
                    return x[:, :, :, a, :] if axes > 1 else x[:, :, a, :]

                def table(c):
                    return c.unsqueeze(1).to_broadcast(shape)

                n = groups * axes * nf
                pat = "p (g a n) -> p g a n" if axes > 1 else "p (g n) -> p g n"
                t = [tmp[:, i * n:(i + 1) * n].rearrange(pat, **({"g": groups, "a": axes} if axes > 1 else {"g": groups}))
                     for i in range(4)]
                link(v.tensor_tensor(t[0], half(0), table(cos), ALU.mult))
                link(v.tensor_tensor(t[1], half(1), table(sin), ALU.mult))
                link(v.tensor_tensor(t[2], half(0), table(sin), ALU.mult))
                link(v.tensor_tensor(t[3], half(1), table(cos), ALU.mult))
                link(v.tensor_tensor(half(0), t[0], t[1], ALU.subtract))
                link(v.tensor_tensor(half(1), t[2], t[3], ALU.add))

            def wrap_angle(x, turns, shift_turns=0.0, p=P):
                link(v.tensor_scalar(turns, x, 1.0 / (2 * np.pi), shift_turns, ALU.mult, ALU.add))
                link(v.tensor_scalar(turns, turns, ROUNDER, None, ALU.add))
                link(v.tensor_scalar(turns, turns, ROUNDER, None, ALU.subtract))
                link(v.scalar_tensor_tensor(x, turns, -TWO_PI_HI, x, ALU.mult, ALU.add))
                link(v.scalar_tensor_tensor(x, turns, -TWO_PI_LO, x, ALU.mult, ALU.add))
                link(v.tensor_scalar(x, x, 2 * np.pi * shift_turns, 3.1415925, ALU.add, ALU.min))
                link(v.tensor_scalar(x, x, -3.1415925, None, ALU.max))

            def masked_attend(name, maps, mask, L, dv, o, done, combine=None):
                for s in range(10):
                    if s < 8:
                        for m in range(maps):
                            u = U[name + ".logits"][s * maps + m]
                            full(dve, u)
                            if s >= 2:
                                dve.wait_ge(sem(done), (s - 2) * maps * 2 + 2 * m + 2)
                            L_m = L[:, (s % 2) * 768 + m * 384:(s % 2) * 768 + (m + 1) * 384]
                            drain(v.tensor_tensor(L_m, banks[u.bank][:, 0:384], mask, ALU.add), u)
                            for g, (c0, n) in enumerate(((0, P), (P, 2 * P))):
                                ins = v.tensor_reduce(neg_max[:, s % 2, m, g:g + 1], L_m[:, c0:c0 + n], AX_X, ALU.max,
                                                      negate=True)
                                if g == 0:
                                    link(ins)
                            tell(ins, name + "_max")
                    if combine and 1 <= s <= 8:
                        combine(s - 1)
                    if s >= 2:
                        a = s - 2
                        u = U[name + ".out"][a]
                        full(dve, u)
                        if not combine:
                            dve.wait_ge(sem(done), a * maps * 2 + 2)
                            link(v.reciprocal(exp_inv[:, a % 4, 0, :], exp_sum[:, a % 4, 0, :]))
                        for t in range(NT):
                            dst = o[:, t, a * dv:(a + 1) * dv]
                            src = banks[u.bank][:, t * dv:(t + 1) * dv]
                            if combine:
                                ins = v.tensor_copy(dst, src)
                            else:
                                ins = v.tensor_scalar(dst, src, exp_inv[:, a % 4, 0, t:t + 1], None, ALU.mult)
                            if t == 0:
                                link(ins)
                        drain(ins, u)
                        if not combine:
                            v.tensor_copy(stat[:, 162:163], stat[:, 163:164]).then_inc(sem(name + "_o"), 1)

            def full_attend(name, o):
                for s in range(18):
                    if s < 16:
                        u = U[name + ".logits"][s]
                        full(dve, u)
                        if s >= 2:
                            before = U[name + ".logits"][s - 2]
                            drained(dve, before)
                        tell(v.tensor_reduce(neg_max[:, s % 2, 0, 0:1], banks[u.bank][:, :], AX_X, ALU.max,
                                             negate=True), name + "_max")
                    if s >= 2:
                        a = s - 2
                        u = U[name + ".out"][a]
                        full(dve, u)
                        drained(dve, U[name + ".logits"][a])
                        link(v.reciprocal(exp_inv[:, a % 4, 0, 0:1], exp_sum[:, a % 4, 0, 0:1]))
                        hh, t = a // 2, a % 2
                        drain(v.tensor_scalar(o[:, t, hh * 64:(hh + 1) * 64], banks[u.bank][:, 0:64],
                                              exp_inv[:, a % 4, 0, 0:1], None, ALU.mult), u)
                        v.tensor_copy(stat[:, 162:163], stat[:, 163:164]).then_inc(sem(name + "_o"), 1)

            link(v.memset(stat[:, :], 0.0))
            tell(v.memset(eps_col, EPS), "eps_ready")

            dma_done(dve, "x_loaded")
            norm_input()
            turn("turn.mix0", xT3)
            dma_done(dve, "cols_loaded", 2)
            tell(v.tensor_tensor(s_inv[:, 0:4], col("lb0", 0, 4), col("lb1", 0, 4), ALU.subtract), "lb_diff")
            dve.wait_ge(sem("lb_ready"), 1)
            link(v.tensor_scalar(one_less_lb, lb_col, -1.0, 1.0, ALU.mult, ALU.add))
            for u in U["hgrn_f"]:
                drained(dve, u)
            for c in range(4):
                f_c = hg_f[:, c * S:(c + 1) * S]
                link(v.tensor_scalar(f_c, f_c, one_less_lb[:, c:c + 1], lb_col[:, c:c + 1], ALU.mult, ALU.add))
            tell(v.tensor_scalar(hg_k, hg_f, -1.0, 1.0, ALU.mult, ALU.add), "hgrn_forget")
            u = U["fox_f"][0]
            full(dve, u)
            dma_done(dve, "rows_loaded")
            dma_done(dve, "resident_loaded")
            xf = route_logf
            drain(v.tensor_tensor(xf.rearrange("p (t n) -> p t n", t=NT),
                                  banks[u.bank][:, 0:16].rearrange("p (t n) -> p t n", t=NT),
                                  over(row("fox_bias"), [P, NT, 8], 1), ALU.add), u)
            link(v.tensor_scalar(small[:, 464:480], xf, -1.0, None, ALU.mult))
            tell(v.tensor_tensor(small[:, 464:480], small[:, 464:480], xf, ALU.min), "fox_absf")
            for j, u in enumerate(U["fox_q"]):
                full(dve, u)
                drain(v.tensor_copy(fx_q[:, j * 512:(j + 1) * 512], banks[u.bank][:, :]), u)
            for j, u in enumerate(U["fox_k"]):
                full(dve, u)
                drain(v.tensor_copy(fx_k[:, j * 512:(j + 1) * 512], banks[u.bank][:, :]), u)
            dve.wait_ge(sem("fox_softplus"), 1)
            link(v.tensor_scalar(xf, xf, 0.0, None, ALU.min))
            tell(v.tensor_tensor(xf, xf, small[:, 464:480], ALU.subtract), "fox_logf")
            dve.wait_ge(sem("hgrn_logf"), 1)
            for c in range(4):
                cs = slice(c * S, (c + 1) * S)
                link(v.tensor_tensor_scan(hg_cum[:, cs], ones256, hg_qh[:, cs], 0.0, ALU.mult, ALU.add))
            u = U["fox_cum"][0]
            full(dve, u)
            drain(v.tensor_copy(small[:, 480:496], banks[u.bank][:, 0:16]), u)
            link(v.memset(hg_qh, 0.0))
            link(v.memset(hg_kh, 0.0))
            for u in U["hgrn_q"]:
                drained(dve, u)
            dma_done(dve, "even_tables_loaded")
            expo, exps = at(0, 1024), at(1024, 1024)
            tmp = at(2048, 512)
            exps_done = 0
            for n, L in enumerate(list(HGRN_LEVELS) + [None, P]):
                name = f"level{L}" if L else "diagonal"
                if n:
                    prev = f"level{HGRN_LEVELS[n - 1]}" if n <= 4 else "diagonal"
                    full(dve, U[prev][-1])
                if L:
                    blocks = lambda a: a.rearrange("p (b w l) -> p b w l", w=2, l=L)
                    first, second = (lambda a: blocks(a)[:, :, 0, :]), (lambda a: blocks(a)[:, :, 1, :])
                    nb = 1024 // (2 * L)
                    ref = first(hg_cum)[:, :, L - 1:L].to_broadcast([P, nb, L])
                    link(v.tensor_tensor(second(expo), second(hg_cum), ref, ALU.subtract))
                    tell(v.tensor_tensor(first(expo), ref, first(hg_cum), ALU.subtract), "hgrn_exponents")
                    exps_done += 1
                    dve.wait_ge(sem("hgrn_exps"), exps_done)
                    link(v.tensor_tensor(second(hg_qh), second(hg_q), second(exps), ALU.mult))
                    tell(v.tensor_tensor(first(hg_kh), first(hg_k), first(exps), ALU.mult), "hgrn_factors")
                else:
                    b3 = lambda a: a.rearrange("p (b l) -> p b l", l=LAST_BLOCK)
                    mid = b3(hg_cum)[:, :, LAST_BLOCK // 2 - 1:LAST_BLOCK // 2].to_broadcast([P, 1024 // 8, 8])
                    tell(v.tensor_tensor(b3(expo), b3(hg_cum), mid, ALU.subtract), "hgrn_exponents")
                    exps_done += 2
                    dve.wait_ge(sem("hgrn_exps"), exps_done)
                    link(v.tensor_tensor(hg_qh, hg_q, exps, ALU.mult))
                    tell(v.tensor_tensor(hg_kh, hg_k, hg_kh, ALU.mult), "hgrn_factors")
                for j, u in enumerate(U[name]):
                    full(dve, u)
                    src = banks[u.bank][:, :].rearrange("p (c t) -> p c t", c=4)
                    if L == P:
                        drain(v.tensor_copy(hg_P[:, 4 + j], src), u)
                        continue
                    mask = over(level_mask[n], [P, 4, P], 1)
                    t3 = tmp.rearrange("p (c t) -> p c t", c=4)
                    dst = hg_P[:, j]
                    if n == 0:
                        drain(v.tensor_tensor(dst, src, mask, ALU.mult), u)
                    else:
                        drain(v.scalar_tensor_tensor(t3, src, 3e38, mask, ALU.min, ALU.mult), u)
                        link(v.tensor_tensor(dst, dst, t3, ALU.add))
            for u in U["hgrn_g"]:
                drained(dve, u)
            for t, u in enumerate(U["hgrn_o"]):
                full(dve, u)
                drain(v.tensor_copy(expo[:, t * 512:(t + 1) * 512], banks[u.bank][:, :]), u)
            link(group_norm(expo, 16, 64, exps, row("hgrn_out")))
            link(v.tensor_tensor(ev_o[:, :, 0:512], expo.rearrange("p (t d) -> p t d", t=NT),
                                 hg_g.rearrange("p (t d) -> p t d", t=NT), ALU.mult))
            link(v.tensor_scalar(row("fox_q"), row("fox_q"), 0.125, None, ALU.mult))
            link(group_norm(fx_q, 16, 64, exps, row("fox_q"), fq_aug[:, :, :, 0:64]))
            link(group_norm(fx_k, 16, 64, exps, row("fox_k"), fk_aug[:, :, :, 0:64]))
            cum4 = small[:, 480:496].rearrange("p (t h d) -> p t h d", t=NT, h=8)
            link(v.memset(fq_aug[:, :, :, 64:65], 1.0))
            link(v.tensor_copy(fq_aug[:, :, :, 65:66], cum4))
            link(v.tensor_scalar(fk_aug[:, :, :, 64:65], cum4, -1.0, None, ALU.mult))
            tell(v.memset(fk_aug[:, :, :, 65:66], 1.0), "fox_aug")
            masked_attend("fox", 1, causal, fx_L, 64, ev_o[:, :, 512:1024], "fox_exp")
            turn("turn.even_out", xT3)
            add_to_h("even_out")

            def moe(layer):
                name = f"moe{layer}"
                norm_input()
                turn(f"turn.ffn{layer}", xT3)
                u = U[f"router{layer}"][0]
                full(dve, u)
                lg = route[:, 256:328]
                drain(v.tensor_copy(lg, banks[u.bank][:, 0:72]), u)
                best, place = route[:, 0:8], route[:, 16:24].bitcast(U32)
                padded, picked = route[:, 32:40], route[:, 40:48]
                ex = route[:, 64:80].rearrange("p (t n) -> p t n", t=NT)
                keep = [route[:, 336 + 32 * t:368 + 32 * t] for t in range(NT)]
                both = route[:, 400:408]
                link(v.memset(padded, -1e30))
                link(v.memset(route[:, 64:80], 0.0))
                link(v.memset(comb[:, :, 32:34], 0.0))
                link(v.memset(rank[:, :, 32:34], -1.0))
                for t in range(NT):
                    g4 = lg[:, t * 36:t * 36 + 4]
                    link(v.tensor_copy(padded[:, 0:4], g4))
                    link(v.max(best, padded))
                    link(v.max_index(place, best, padded))
                    link(v.tensor_copy(route[:, 24:32], place))
                    hot = keep[t][:, 0:4]
                    link(v.tensor_scalar(hot, iota8[:, 0:4], route[:, 24:25], None, ALU.is_equal))
                    link(v.tensor_scalar(ex[:, t, 0:4], g4, best[:, 0:1], None, ALU.subtract))
                    e3 = lg[:, t * 36 + 4:t * 36 + 36].rearrange("p (g e) -> p g e", g=4)
                    link(v.tensor_scalar(picked, e3[:, 0], hot[:, 0:1], None, ALU.mult))
                    for g in range(1, 4):
                        link(v.scalar_tensor_tensor(picked, e3[:, g], hot[:, g:g + 1], picked, ALU.mult, ALU.add))
                    link(v.max(best, picked))
                    link(v.max_index(place, best, picked))
                    link(v.tensor_copy(route[:, 24:32], place))
                    link(v.tensor_tensor(ex[:, t, 4:5], best[:, 1:2], best[:, 0:1], ALU.subtract))
                    for r in range(2):
                        link(v.tensor_scalar(keep[t][:, 8 + 8 * r:16 + 8 * r], iota8, route[:, 24 + r:25 + r], None,
                                             ALU.is_equal))
                    link(v.tensor_tensor(both, keep[t][:, 8:16], keep[t][:, 16:24], ALU.add))
                    link(v.tensor_tensor(routed[:, t].rearrange("p (g e) -> p g e", g=4), over(hot, [P, 4, 8], 2),
                                         over(both, [P, 4, 8], 1), ALU.mult))
                tell(v.tensor_copy(route[:, 12:13], route[:, 0:1]), "routed")
                dve.wait_ge(sem("route_exp_out"), layer + 1)
                for t in range(NT):
                    hot = keep[t][:, 0:4]
                    link(v.tensor_reduce(route[:, 80:81], ex[:, t, 0:4], AX_X, ALU.add))
                    link(v.tensor_scalar(route[:, 81:82], ex[:, t, 4:5], 1.0, None, ALU.add))
                    link(v.reciprocal(route[:, 82:84], route[:, 80:82]))
                    link(v.tensor_tensor(route[:, 84:85], route[:, 82:83], route[:, 83:84], ALU.mult))
                    link(v.tensor_tensor(route[:, 85:86], route[:, 84:85], ex[:, t, 4:5], ALU.mult))
                    link(v.tensor_scalar(both, keep[t][:, 8:16], route[:, 84:85], None, ALU.mult))
                    link(v.scalar_tensor_tensor(both, keep[t][:, 16:24], route[:, 85:86], both, ALU.mult, ALU.add))
                    link(v.tensor_tensor(comb[:, t, 0:32].rearrange("p (g e) -> p g e", g=4), over(hot, [P, 4, 8], 2),
                                         over(both, [P, 4, 8], 1), ALU.mult))
                u = U[f"rank{layer}"][0]
                full(dve, u)
                ps = banks[u.bank]
                link(v.tensor_tensor(rank[:, :, 0:32], ps[:, 0:64].rearrange("p (t e) -> p t e", t=NT), routed, ALU.mult))
                link(v.tensor_scalar(rank[:, :, 0:32], rank[:, :, 0:32], -1.0, None, ALU.add))
                drain(v.tensor_reduce(route[:, 14:15], ps[:, 64:96], AX_X, ALU.max), u)
                tell(v.tensor_copy(most_tokens[:, layer:layer + 1], route[:, 14:15]), "counted")
                with short_path(dve, layer):
                    moe_short(layer)
                with dve.Else():
                    moe_dense(layer)
                for j in range(4):
                    drained(dve, U[name + ".down"][-4 + j])
                tell(v.tensor_copy(stat[:, 164:165], stat[:, 163:164]), "moe_done")

            def moe_short(layer):
                def seat(table, i, weights, name):
                    for e in range(2):
                        for t in range(NT):
                            dst = table[:, t, e * SEATS:(e + 1) * SEATS]
                            r = rank[:, t, bass.ds(i * 2 + e, 1)]
                            if weights:
                                last = v.tensor_scalar(dst, seats, r, comb[:, t, bass.ds(i * 2 + e, 1)],
                                                       ALU.is_equal, ALU.mult)
                            else:
                                last = v.tensor_scalar(dst, seats, r, None, ALU.is_equal)
                    last.then_inc(sem(name), 1)

                def take_seats(i):
                    seat(sel, i, False, f"seats{layer}")

                def weigh(i):
                    seat(weighted, i, True, f"weights{layer}")

                def filled(u):
                    dve.wait_ge(bank_full[u.bank], u.before + 1)

                def hide(i):
                    for e in range(2):
                        gate_u, up = moe_unit(layer, 2 * e, e, i), moe_unit(layer, 2 * e + 1, e, i)
                        filled(up)
                        dve.wait_ge(bank_drained[gate_u.bank], gate_u.before + 1)
                        v.tensor_tensor(pair_hidden[:, e, :], pair_silu[:, e, :], banks[up.bank][:, 0:4 * SEATS],
                                        ALU.mult).then_inc(bank_drained[up.bank], 1)

                def scatter(i):
                    for j in range(4):
                        u = moe_unit(layer, 4 + j, 1, i)
                        filled(u)
                        dst = h3[:, j // 2, (j % 2) * 512:(j % 2 + 1) * 512]
                        v.tensor_tensor(dst, dst, banks[u.bank][:, :], ALU.add).then_inc(bank_drained[u.bank], 1)

                take_seats(0)
                weigh(0)
                filled(moe_unit(layer, 3, 0, 0))
                take_seats(1)
                hide(0)
                filled(moe_unit(layer, 3, 0, 1))
                take_seats(2)
                with dve.Fori(1, PAIRS - 1) as i:
                    hide(i)
                    filled(moe_unit(layer, 7, 0, i - 1))
                    weigh(i)
                    filled(moe_unit(layer, 3, 0, i + 1))
                    take_seats(i + 2)
                    scatter(i - 1)
                hide(PAIRS - 1)
                filled(moe_unit(layer, 7, 0, PAIRS - 2))
                weigh(PAIRS - 1)
                scatter(PAIRS - 2)
                scatter(PAIRS - 1)

            def moe_dense(layer):
                name = f"moe{layer}"
                with dve.Fori(0, PAIRS) as i:
                    for e in range(2):
                        for j in range(2):
                            gate_u = U[name + ".gate"][2 * e + j].later(i * 2)
                            up_u = U[name + ".up"][2 * e + j].later(i * 2)
                            dve.wait_ge(bank_full[up_u.bank], up_u.before + 1)
                            dve.wait_ge(bank_drained[gate_u.bank], gate_u.before + 1)
                            last_down = U[name + ".down"][4 * e + 3].later(i * 2)
                            dve.wait_ge(bank_full[last_down.bank], last_down.before)
                            v.tensor_tensor(hidden[:, j * 512:(j + 1) * 512], silu_g[:, j * 512:(j + 1) * 512],
                                            banks[up_u.bank][:, :], ALU.mult).then_inc(bank_drained[up_u.bank], 1)
                        for j in range(4):
                            u = U[name + ".down"][4 * e + j].later(i * 2)
                            dve.wait_ge(bank_full[u.bank], u.before + 1)
                            dve.wait_ge(bank_drained[u.bank], u.before)
                            dst = h3[:, j // 2, (j % 2) * 512:(j % 2 + 1) * 512]
                            v.scalar_tensor_tensor(dst, banks[u.bank][:, :], comb[:, j // 2, bass.ds(i * 2 + e, 1)],
                                                   dst, ALU.mult, ALU.add).then_inc(bank_drained[u.bank], 1)

            moe(0)
            norm_input()
            link(v.tensor_copy(stat[:, 170:172], pos_tile[:, :]))
            ang = od_tab[:, 0:128].rearrange("p (k t n) -> p k t n", k=2, t=NT)
            for kind in range(2):
                for t in range(NT):
                    link(v.tensor_scalar(ang[:, kind, t], row("inv_freq"), stat[:, 170 + t:171 + t], None, ALU.mult))
            wrap_angle(od_tab[:, 0:64], od_tab[:, 128:192])
            wrap_angle(od_tab[:, 64:128], od_tab[:, 128:192], 0.25)
            tell(v.tensor_copy(stat[:, 165:166], od_tab[:, 0:1]), "angles_ready")
            for i, (a, b) in enumerate((("lam_q1", "lam_k1"), ("lam_q2", "lam_k2"))):
                link(v.tensor_tensor(od_tab[:, 192:256], row(a), row(b), ALU.mult))
                link(v.tensor_reduce(small[:, 480 + i:481 + i], od_tab[:, 192:256], AX_X, ALU.add))
            tell(v.tensor_copy(stat[:, 165:166], small[:, 480:481]), "lam_sums")
            turn("turn.mix1", xT3)
            dve.wait_ge(sem("lam_exps"), 1)
            link(v.tensor_tensor(lam, small[:, 480:481], small[:, 481:482], ALU.subtract))
            link(v.tensor_scalar(neg_lam, lam, LAMBDA_INIT, -1.0, ALU.add, ALU.mult))
            dve.wait_ge(sem("rope_ready"), 1)
            link(v.tensor_scalar(row("diff_q"), row("diff_q"), 0.125, None, ALU.mult))
            link(v.tensor_scalar(row("subln"), row("subln"), 1.0 - LAMBDA_INIT, None, ALU.mult))
            for i, (x, g) in enumerate(((od_q, "diff_q"), (od_k, "diff_k"))):
                for u in U["odd_in"][4 * i:4 * i + 4]:
                    drained(dve, u)
                link(group_norm(x, 32, 64, scratch, row(g)))
                for t in range(NT):
                    x4 = x[:, t * D:(t + 1) * D].rearrange("p (g a n) -> p g a n", g=16, a=2)
                    rotate(x4, 16, 1, 32, ang[:, 1, t], ang[:, 0, t], u_buf)
                tell(v.tensor_copy(stat[:, 165:166], x[:, 0:1]), "odd_qk")
            dma_done(dve, "chunk_loaded")

            def combine(s):
                dve.wait_ge(sem("diff_exp"), 4 * s + 4)
                link(v.reciprocal(exp_inv[:, s % 4], exp_sum[:, s % 4]))
                link(v.tensor_scalar(exp_inv[:, s % 4, 1, :], exp_inv[:, s % 4, 1, :], neg_lam, None, ALU.mult))
                P0 = att_P[:, (s % 2) * 1024:(s % 2) * 1024 + 384]
                P1 = att_P[:, (s % 2) * 1024 + 384:(s % 2) * 1024 + 768]
                for g, (c0, n) in enumerate(((0, P), (P, 2 * P))):
                    link(v.tensor_scalar(P0[:, c0:c0 + n], P0[:, c0:c0 + n], exp_inv[:, s % 4, 0, g:g + 1], None,
                                         ALU.mult))
                    ins = v.scalar_tensor_tensor(P0[:, c0:c0 + n], P1[:, c0:c0 + n], exp_inv[:, s % 4, 1, g:g + 1],
                                                 P0[:, c0:c0 + n], ALU.mult, ALU.add)
                    if g == 0:
                        link(ins)
                tell(ins, "diff_probs")

            masked_attend("diff", 2, chunk_mask, od_L, P, od_o, "diff_exp", combine)
            link(group_norm(od_o_flat, 16, P, u_buf, row("subln")))
            tell(v.tensor_copy(stat[:, 165:166], od_o_flat[:, 0:1]), "diff_o")
            turn("turn.odd_out", xT3)
            add_to_h("odd_out")
            moe(1)

            widen_c(1)
            add_bias("mod0.pre1", [shift, scale, shift_c, scale_c], "bias0_pre1", 4)
            dma_done(dve, "ctx_loaded")
            g = gain_row()
            link(modulated(ctx_x, ctx_u, g, scale_c, shift_c))
            tell(v.tensor_copy(stat[:, 165:166], ctx_u[:, 0:1]), "ctx_normed")
            link(modulated(h[:, :], u_buf, g, scale, shift))
            v.tensor_copy(stat[:, 160:161], g[:, 0:1]).then_inc(sem("gain_used"), 1)
            v.tensor_copy(stat[:, 161:162], u_buf[:, 0:1]).then_inc(normed, 1)
            turn("turn.n1_0", ctxT)
            turn("turn.ctx", xT3)
            for u in U["mla_cq"]:
                drained(dve, u)
            link(group_norm(z_cq, 2, 384, at(0, 768), row("mla_q_a")))
            for u in U["mla_ckv"]:
                drained(dve, u)
            link(group_norm(z_ckv, 4, 256, at(0, 1024), row("mla_kv_a")))
            tell(v.tensor_copy(stat[:, 165:166], z_ckv[:, 0:1]), "lora_ready")
            dma_done(dve, "rope2d_loaded")

            def tables(start, nf, t):
                n = 2 * nf
                return [rope2d[:, start + (2 * kind + t) * n:start + (2 * kind + t + 1) * n]
                        .rearrange("p (a n) -> p a n", a=2) for kind in range(2)]

            for u in U["gqa_q"]:
                drained(dve, u)
            link(v.tensor_scalar(row("gqa_q"), row("gqa_q"), 0.125, None, ALU.mult))
            link(group_norm(z_gq, 16, 64, at(0, 1024), row("gqa_q")))
            for u in U["gqa_kv"]:
                drained(dve, u)
            link(group_norm(z_gk, 8, 64, at(0, 512), row("gqa_k")))
            tmp4 = at(0, 2048)
            for t in range(NT):
                cos, sin = tables(64, 16, t)
                rotate(z_gq[:, t * 512:(t + 1) * 512].rearrange("p (g a b n) -> p g a b n", g=8, a=2, b=2), 8, 2, 16,
                       cos, sin, tmp4)
                rotate(z_gk[:, t * P:(t + 1) * P].rearrange("p (g a b n) -> p g a b n", g=2, a=2, b=2), 2, 2, 16,
                       cos, sin, tmp4)
                cos, sin = tables(0, 8, t)
                rotate(z_kr[:, t * 32:(t + 1) * 32].rearrange("p (g a b n) -> p g a b n", g=1, a=2, b=2), 1, 2, 8,
                       cos, sin, tmp4)
            for u in U["mla_q"]:
                drained(dve, u)
            q4 = ml_q.rearrange("p (t h d) -> p t h d", t=NT, h=8)
            k4 = ml_k.rearrange("p (t h d) -> p t h d", t=4, h=8)
            for t in range(NT):
                cos, sin = tables(0, 8, t)
                link(v.tensor_copy(at(2048, 256).rearrange("p (g n) -> p g n", g=8), q4[:, t, :, 64:96]))
                rotate(at(2048, 256).rearrange("p (g a b n) -> p g a b n", g=8, a=2, b=2), 8, 2, 8, cos, sin, tmp4)
                link(v.tensor_copy(q4[:, t, :, 64:96], at(2048, 256).rearrange("p (g n) -> p g n", g=8)))
            link(v.tensor_scalar(ml_q, ml_q, float(96 ** -0.5), None, ALU.mult))
            for u in U["mla_kv"]:
                drained(dve, u)
            tell(v.tensor_copy(k4[:, :, :, 64:96], over(z_kr.rearrange("p (t d) -> p t d", t=4), [P, 4, 8, 32], 2)),
                 "mla_qk")
            full_attend("mla", b2_o)
            tell(v.tensor_copy(stat[:, 165:166], z_gq[:, 0:1]), "gqa_qk")
            full_attend("gqa", b2_o[:, :, 512:1024])
            add_bias("mod0.gate1", [gate], "bias0_gate1", 1)
            turn("turn.a_out", xT3)
            add_gated("a_out", gate)
            tell(v.tensor_copy(stat[:, 165:166], gate[:, 0:1]), "gate_used")

            def mlp(layer):
                name = f"mlp{layer}"
                for j in range(8):
                    for i, u in enumerate(U[name + ".hidden"][2 * j:2 * j + 2]):
                        full(dve, u)
                        if j:
                            full(dve, U[name + ".out"][4 * j - 1])
                        link(v.tensor_scalar(silu_g[:, i * 512:(i + 1) * 512], banks[u.bank][:, :], 0.0, None, ALU.max))
                        drain(v.tensor_tensor(hidden[:, i * 512:(i + 1) * 512], silu_g[:, i * 512:(i + 1) * 512],
                                              silu_g[:, i * 512:(i + 1) * 512], ALU.mult), u)
                    for i, u in enumerate(U[name + ".out"][4 * j:4 * j + 4]):
                        full(dve, u)
                        dst = mlp_y[:, i // 2, (i % 2) * 512:(i % 2 + 1) * 512]
                        if j == 0:
                            drain(v.tensor_copy(dst, banks[u.bank][:, :]), u)
                        else:
                            drain(v.tensor_tensor(dst, dst, banks[u.bank][:, :], ALU.add), u)
                link(v.tensor_tensor(mlp_y, mlp_y, over(gate2, [P, NT, D], 1), ALU.mult))
                link(v.tensor_tensor(h3, h3, mlp_y, ALU.add))
                tell(v.tensor_copy(stat[:, 164:165], stat[:, 163:164]), "mlp_done")

            add_bias("mod0.pre2", [shift, scale], "bias0_pre2", 2)
            modulated_input()
            turn("turn.n2_0", xT3)
            add_bias("mod0.gate2", [gate2], "bias0_gate2", 1)
            mlp(0)

            widen_c(2)
            add_bias("mod1.pre1", [shift, scale], "bias1_pre1", 2)
            modulated_input()
            turn("turn.n1_1", xT3)
            for i, u in enumerate(U["filter_mlp"]):
                full(dve, u)
                x, turns = at(10240, 256)[0:64, :], at(10496, 256)[0:64, :]
                drain(v.tensor_scalar(x, banks[u.bank][0:64, 0:S], col("filt_b", i, 1, 64), col("filt_freq", i, 1, 64),
                                      ALU.add, ALU.mult), u)
                wrap_angle(x, turns)
                tell(v.tensor_copy(stat[:, 165:166], stat[:, 163:164]), "filter_angle")
                dve.wait_ge(sem("filter_h"), i + 1)
            dma_done(dve, "window_loaded")
            h44 = h4.rearrange("p (a t d) -> p a t d", a=2, t=NT)
            w3 = window.rearrange("p (t d) -> p t d", t=NT)
            f3 = f_sum.rearrange("p (i d) -> p i d", i=4)
            for n in range(2):
                for j, u in enumerate(U[f"filter{n}"]):
                    direction, tile, half = j // 4, j // 2 % 2, j % 2
                    full(dve, u)
                    hs = slice(half * 512, (half + 1) * 512)
                    drain(v.tensor_tensor(h44[:, direction, tile, hs], banks[u.bank][:, :], w3[:, tile, hs], ALU.mult), u)
                h4i = h4.rearrange("p (i d) -> p i d", i=4)
                for half in range(2):
                    hs = slice(half * 512, (half + 1) * 512)
                    if half:
                        full(dve, U[f"filter_norm{n}"][0])
                    tell(v.tensor_tensor(f3, h4i[:, :, hs], h4i[:, :, hs], ALU.mult), "filter_squares")
                full(dve, U[f"filter_norm{n}"][1])
                for half, u in enumerate(U[f"filter_norm{n}"]):
                    drained(dve, u)
                link(v.reciprocal(f_norm, f_norm))
                link(v.tensor_scalar(h44[:, 1, 0], h44[:, 1, 0], col("not_first"), None, ALU.mult))
                fs3 = f_sum.rearrange("p (t d) -> p t d", t=NT)
                nrm = over(f_norm, [P, NT, D], 1)
                link(v.tensor_tensor(fs3, h44[:, 0], h44[:, 1], ALU.add))
                tell(v.tensor_tensor(fs3, fs3, nrm, ALU.mult), "filter_sums")
                link(v.tensor_tensor(h44[:, 0], h44[:, 0], h44[:, 1], ALU.subtract))
                tell(v.tensor_tensor(h44[:, 0], h44[:, 0], nrm, ALU.mult), "filter_sums")
            last_norm = U["filter_dft1"][-1]
            full(dve, last_norm)
            tell(v.memset(z_pad, 0.0), "pad_ready")
            for i in range(6):
                z4 = z_pad[:, (i % 2) * 1032:(i % 2 + 1) * 1032].rearrange("p (c s) -> p c s", c=4)
                for u in U["hyena_in"][2 * i:2 * i + 2]:
                    drained(dve, u)
                if i:
                    full(dve, U["hyena_turn"][2 * i - 1])
                for c in range(4):
                    ct = 4 * i + c
                    dst = conv[:, c * S:(c + 1) * S]
                    w = [col("conv_w", 24 * k + ct) for k in range(3)]
                    link(v.tensor_scalar(dst, z4[:, c, 0:S], w[0], col("conv_b", ct), ALU.mult, ALU.add))
                    link(v.scalar_tensor_tensor(dst, z4[:, c, 1:S + 1], w[1], dst, ALU.mult, ALU.add))
                    link(v.scalar_tensor_tensor(dst, z4[:, c, 2:S + 2], w[2], dst, ALU.mult, ALU.add))
                tell(v.tensor_copy(stat[:, 165:166], conv[:, 0:1]), "conv_ready")
            for u in U["hyena_turn"]:
                drained(dve, u)
            sp5 = spectra.rearrange("p (n k f d) -> p n k f d", n=2, k=2, f=NT)
            for n in range(2):
                skip = gain_row()
                for j in range(4):
                    ft, half = j // 2, j % 2
                    uc, us = U[f"dft{n}"][2 * j:2 * j + 2]
                    hs = slice(half * 512, (half + 1) * 512)
                    A_, B_ = sp5[:, n, 0, ft, hs], sp5[:, n, 1, ft, hs]
                    re = y_re[:, ft * D + half * 512:ft * D + (half + 1) * 512]
                    im = y_im[:, ft * D + half * 512:ft * D + (half + 1) * 512]
                    full(dve, uc)
                    full(dve, us)
                    link(v.tensor_tensor(prod[0], banks[uc.bank][:, :], A_, ALU.mult))
                    link(v.tensor_tensor(prod[1], banks[us.bank][:, :], B_, ALU.mult))
                    link(v.tensor_tensor(re, prod[0], prod[1], ALU.subtract))
                    drain(v.tensor_tensor(prod[0], banks[uc.bank][:, :], B_, ALU.mult), uc)
                    drain(v.tensor_tensor(prod[1], banks[us.bank][:, :], A_, ALU.mult), us)
                    tell(v.tensor_tensor(im, prod[0], prod[1], ALU.add), "spectrum_ready")
                for j, u in enumerate(U[f"idft{n}"]):
                    tile, half = j // 2, j % 2
                    cs = slice(tile * D + half * 512, tile * D + (half + 1) * 512)
                    y = hy_x[2][:, cs]
                    full(dve, u)
                    link(v.tensor_tensor(y, y, skip[:, half * 512:(half + 1) * 512], ALU.mult))
                    drain(v.tensor_tensor(y, y, banks[u.bank][:, :], ALU.add), u)
                    tell(v.tensor_tensor(y, y, hy_x[n][:, cs], ALU.mult), "hyena_y")
                v.tensor_copy(stat[:, 160:161], skip[:, 0:1]).then_inc(sem("gain_used"), 1)
            widen_c(3)
            add_bias("mod1.gate1", [gate], "bias1_gate1", 1)
            turn("turn.hyena_out", xT3)
            add_gated("hyena_out", gate)
            tell(v.tensor_copy(stat[:, 165:166], gate[:, 0:1]), "gate_used")
            add_bias("mod1.pre2", [shift, scale], "bias1_pre2", 2)
            modulated_input()
            turn("turn.n2_1", xT3)
            add_bias("mod1.gate2", [gate2], "bias1_gate2", 1)
            mlp(1)
            link(norm(h[:, :], u_buf, gain_row()))
            v.tensor_copy(stat[:, 161:162], u_buf[:, 0:1]).then_inc(sem("result_ready"), 1)


_ORDER = ["x", "ctx", "gains", "rows", "cols", "positions", "routers", "even_w_in", "even_w_out", "odd_w_in",
          "odd_w_out", "moe_w_gate", "moe_w_up", "moe_w_down", "w_mod", "b_mod", "mlp_w1", "mlp_w2", "a_w_in",
          "a_w_q_b", "a_w_kv_b", "a_w_out", "h_w_in", "h_f_w1", "h_f_w2", "h_f_w3", "h_f_w4", "h_w_out",
          "resident", "even_tables", "chunk_mask", "rope2d", "dft", "feats", "window"]


def lay_out(I):
    a = {k: np.asarray(x) for k, x in I.items()}
    table = constants()

    def per_partition(x, n):
        return np.ascontiguousarray(x.reshape(n, P).T)

    d = {"x": a["x"][0], "ctx": a["ctx_2"][0]}
    d["gains"] = np.stack([a["norm_mix"][0], a["norm_ffn"][0], a["norm_mix"][1], a["norm_ffn"][1], a["norm1_g_2"][0],
                           a["norm2_g_2"][0], a["norm1_g_2"][1], a["h_skip_2"][0, 0], a["h_skip_2"][0, 1],
                           a["norm2_g_2"][1], a["final_g_2"]])
    d["rows"] = np.concatenate([x.reshape(-1) for x in (
        a["fox_q_norm"], a["fox_k_norm"], a["hgrn_out_norm"], a["diff_q_norm"], a["diff_k_norm"],
        a["diff_lambda_q1"], a["diff_lambda_k1"], a["diff_lambda_q2"], a["diff_lambda_k2"], a["diff_subln"],
        a["fox_f_bias"], a["a_q_norm_g_2"], a["a_k_norm_g_2"], a["a_q_a_g_2"], a["a_kv_a_g_2"],
        table["inv_freq"])])
    filt = np.zeros((P, 6), np.float32)
    for i, n in enumerate(("h_f_b1_2", "h_f_b2_2", "h_f_b3_2")):
        filt[0:64, i] = a[n][0]
        filt[0:64, 3 + i] = a["h_f_freq_2"][0, i]
    not_first = np.ones((P, 1), np.float32)
    not_first[0] = 0
    d["cols"] = np.concatenate([
        per_partition(a["hgrn_lb_logits"], 8), per_partition(a["h_conv_w_2"], 72), per_partition(a["h_conv_b_2"], 24),
        filt, per_partition(a["c_2"], 8), per_partition(a["c_ctx_2"], 8), not_first], 1)
    d["positions"] = np.ascontiguousarray(a["positions"].reshape(NT, P).T)
    d["routers"] = np.concatenate([a["moe_router_group"],
                                   a["moe_router_expert"].transpose(0, 2, 1, 3).reshape(2, D, N_EXPERTS)], 2)
    for n in ("moe_w_gate", "moe_w_up"):
        d[n] = a[n].reshape(2 * N_EXPERTS, D, 512)
    d["moe_w_down"] = a["moe_w_down"].reshape(2 * N_EXPERTS, 512, D)
    for n in ("even_w_in", "even_w_out", "odd_w_in", "odd_w_out"):
        d[n] = a[n][0]
    for n in ("a_w_in", "a_w_q_b", "a_w_kv_b", "a_w_out", "h_w_in", "h_f_w1", "h_f_w2", "h_f_w3", "h_f_w4", "h_w_out"):
        d[n] = a[n + "_2"][0]
    for n in ("w_mod", "b_mod", "mlp_w1", "mlp_w2"):
        d[n] = a[n + "_2"]
    for n in ("resident", "even_tables", "chunk_mask", "rope2d", "dft", "feats", "window"):
        d[n] = table[n]
    return {n: np.ascontiguousarray(d[n]) for n in _ORDER}


def kernel(**inputs):
    import concourse.bacc as bacc
    from concourse.bass_utils import run_bass_kernel_spmd

    nc = bacc.Bacc("TRN2", target_bir_lowering=False, num_devices=1)
    arrays = {f"in_{n}": a for n, a in lay_out(inputs).items()}
    args = {n[3:]: nc.dram_tensor(n, a.shape, mybir.dt.from_np(a.dtype), kind="ExternalInput").ap()
            for n, a in arrays.items()}
    out = nc.dram_tensor("out_0", (S, D), F32, kind="ExternalOutput").ap()
    build(nc, args, out)
    got = run_bass_kernel_spmd(nc, [arrays], core_ids=[0])
    return got.results[0]["out_0"].reshape(1, S, D)
```

```python
from contextlib import ExitStack

import numpy as np

import concourse.bass as bass
from concourse import mybir

F32 = mybir.dt.float32
I32 = mybir.dt.int32
F32R = mybir.dt.float32r
U32 = mybir.dt.uint32
ALU = mybir.AluOpType
ACT = mybir.ActivationFunctionType
AX_X = mybir.AxisListType.X

P = 128
D = 1024
S = 256
NT = S // P
KD = D // P
SLAB = 4096
RING = 6
EPS = 1e-6
N_EXPERTS = 32
PAIRS = N_EXPERTS // 2
SEATS = 64
EXPERT_SLABS = 3
HGRN_LEVELS = (64, 32, 16, 8)
MLP_STEPS = 8
GATE_SUMS = (3, 5)
LAST_BLOCK = 8
LAMBDA_INIT = 0.8 - 0.6 * float(np.exp(-0.3))
TWO_PI_HI = 6.28125
TWO_PI_LO = float(2 * np.pi - 6.28125)
ROUNDER = 12582912.0

ROW_PARTS = [("fox_q", 64), ("fox_k", 64), ("hgrn_out", 64), ("diff_q", 64), ("diff_k", 64), ("lam_q1", 64),
             ("lam_k1", 64), ("lam_q2", 64), ("lam_k2", 64), ("subln", 128), ("fox_bias", 8), ("gqa_q", 64),
             ("gqa_k", 64), ("mla_q_a", 384), ("mla_kv_a", 256), ("inv_freq", 32)]
COL_PARTS = [("lb0", 4), ("lb1", 4), ("conv_w", 72), ("conv_b", 24), ("filt_b", 3), ("filt_freq", 3),
             ("c", 8), ("c_ctx", 8), ("not_first", 1)]


def offsets(parts):
    out, at = {}, 0
    for name, n in parts:
        out[name] = (at, n)
        at += n
    return out, at


ROWS, N_ROWS = offsets(ROW_PARTS)
COLS, N_COLS = offsets(COL_PARTS)


FILLS = (("gate0", 0), ("up0", 1), ("down1.0", 2), ("down1.1", 3), ("fold0", 4), ("turn", 5), ("gate1", 6), ("up1", 7),
         ("out0", 0), ("out1", 1), ("out2", 2), ("out3", 3), ("down0.0", 4), ("down0.1", 5), ("gather0", 6),
         ("gather1", 7), ("fold1", 2))
OF_PAIR_BEFORE = ("down1.0", "down1.1", "turn", "out0", "out1", "out2", "out3")
FIRST_FILLS = (("gather0", 6), ("gather1", 7)) + tuple(x for x in FILLS if x[0] not in OF_PAIR_BEFORE)
LAST_FILLS = tuple(x for x in FILLS if x[0] in OF_PAIR_BEFORE)
PER_PAIR = (2, 2, 3, 2, 2, 2, 2, 2)
WEIGHTS = ("gate0", "up0", "down1", "gate1", "up1", "down0")
FIRST_WEIGHTS = ("gate0", "up0", "gate1", "up1", "down0")
SLAB_OF = {"gate0": 0, "up0": 1, "down0": 2, "gate1": 3, "up1": 4, "down1": 5}


def fills_before(fills, name):
    bank = dict(FILLS)[name]
    last = max(i for i, x in enumerate(fills) if x[0] == name)
    return sum(b == bank for _, b in fills[:last])


MLP_PARTS = [(w, j - w, half) for j in range(MLP_STEPS + 1) for w in range(2) if 0 <= j - w < MLP_STEPS
             for half in range(2)]


class Unit:

    def __init__(self, bank, before):
        self.bank, self.before = bank, before

    def later(self, n):
        return Unit(self.bank, self.before + n)


class Plan:

    def __init__(self):
        self.filled = [0] * 8
        self.next = 0
        self.units = {}
        self.slabs = {}
        self.n_slabs = 0
        self.last_reader = {}

    def take(self, name, n=1, banks=None):
        for _ in range(n):
            b = self.next if banks is None else banks[len(self.units.get(name, [])) % len(banks)]
            if banks is None:
                self.next = (self.next + 1) % 8
            self.units.setdefault(name, []).append(Unit(b, self.filled[b]))
            self.filled[b] += 1

    def slab(self, name, last_unit):
        self.slabs.setdefault(name, []).append(self.n_slabs)
        self.last_reader[self.n_slabs] = last_unit
        self.n_slabs += 1

    def stream(self, name, slabs, per_slab):
        for i in range(slabs):
            self.take(name, per_slab)
            self.slab(name, self.units[name][-1])

    def heads(self, name, steps, maps):
        for s in range(steps + 2):
            if s < steps:
                self.take(name + ".logits", maps)
            if 1 <= s < steps + 1:
                self.take(name + ".turn")
            if s >= 2:
                self.take(name + ".out")

    def experts(self, name):
        self.next = 0
        for e in range(N_EXPERTS):
            self.take(name + ".gate", 2, (0, 1))
            self.take(name + ".up", 2, (2, 3))
            self.take(name + ".down", 4, (4, 5, 6, 7))
            self.slab(name, self.units[name + ".gate"][-1])
            self.slab(name, self.units[name + ".up"][-1])
            self.slab(name, self.units[name + ".down"][-1])
            if e % 2:
                self.take(name + ".even", 1, (2,))
        for idx in self.slabs[name][-RING:]:
            self.last_reader[idx] = self.units[name + ".even"][-1]

    def vector_slabs(self, name, slabs):
        for _ in range(slabs):
            self.slab(name, None)

    def sum_up(self, name, i, banks=None):
        self.take(name, 1, banks)
        self.last_reader[self.slabs[name][i]] = self.units[name][-1]

    def mlp(self, name, gate):
        self.next = 0
        for j in range(MLP_STEPS + 1):
            if j in GATE_SUMS:
                self.sum_up(gate, GATE_SUMS.index(j), (0,))
            if j < MLP_STEPS:
                self.take(name + ".hidden", 2, (0, 1, 2, 3))
                self.slab(name + ".w1", self.units[name + ".hidden"][-1])
            if j > 0:
                self.take(name + ".out", 4, (4, 5, 6, 7))
                self.slab(name + ".w2", self.units[name + ".out"][-1])
            if j + 2 in GATE_SUMS:
                self.vector_slabs(gate, 1)


def make_plan():
    p = Plan()
    p.take("turn.mix0", 4)
    p.stream("hgrn_f", 1, 2)
    p.stream("hgrn_q", 1, 2)
    p.take("fox_f")
    p.stream("hgrn_i", 1, 2)
    p.stream("fox_q", 1, 2)
    p.stream("fox_k", 1, 2)
    p.stream("fox_v", 1, 2)
    p.stream("hgrn_g", 1, 2)
    p.take("fox_cum")
    for L in HGRN_LEVELS:
        p.take(f"level{L}", 4)
    p.take("diagonal", 4)
    p.take("level128", 2)
    p.take("hgrn_o", 2)
    p.take("fox_qT", 4)
    p.take("fox_kT", 4)
    p.heads("fox", 8, 1)
    p.take("turn.even_out", 4)
    p.stream("even_out", 2, 2)
    p.take("turn.ffn0", 4)
    p.take("router0")
    p.take("rank0")
    p.experts("moe0")
    p.take("turn.mix1", 4)
    p.stream("odd_in", 6, 2)
    p.take("diff_qT", 8)
    p.take("diff_kT", 8)
    p.heads("diff", 8, 2)
    p.take("turn.odd_out", 4)
    p.stream("odd_out", 2, 2)
    p.take("turn.ffn1", 4)
    p.take("router1")
    p.take("rank1")
    p.experts("moe1")
    p.stream("mod0.pre1", 4, 2)
    for i, idx in enumerate(p.slabs["mod0.pre1"]):
        p.last_reader[idx] = p.units["mod0.pre1"][2 * i]
    p.take("turn.n1_0", 4)
    p.take("turn.ctx", 4)
    p.stream("mla_cq", 1, 2)
    p.stream("mla_ckv", 1, 4)
    p.stream("gqa_q", 1, 2)
    p.stream("gqa_kv", 1, 4)
    p.take("turn.cq", 2)
    p.take("turn.ckv", 2)
    p.stream("mla_q", 1, 4)
    p.stream("mla_kv", 1, 8)
    p.take("mla_qT", 4)
    p.take("mla_kT", 8)
    p.heads("mla", 16, 1)
    p.take("gqa_qT", 4)
    p.take("gqa_kT", 2)
    p.heads("gqa", 16, 1)
    p.vector_slabs("mod0.gate1", 2)
    p.take("turn.a_out", 4)
    for i in range(2):
        p.stream("a_out", 1, 2)
        if i == 0:
            for k in range(2):
                p.sum_up("mod0.gate1", k)
    p.vector_slabs("mod0.pre2", 4)
    for k in range(4):
        p.sum_up("mod0.pre2", k)
    p.take("turn.n2_0", 4)
    p.mlp("mlp0", "mod0.gate2")
    p.stream("mod1.pre1", 2, 1)
    p.vector_slabs("mod1.pre1", 2)
    for k in range(2, 4):
        p.sum_up("mod1.pre1", k)
    p.take("turn.n1_1", 4)
    p.take("filter_mlp", 3)
    for n in range(2):
        p.take(f"filter{n}", 8)
        if n == 1:
            p.slab("filter_w4", p.units["filter1"][-1])
        p.take(f"filter_norm{n}", 2)
        p.take(f"filter_dft{n}", 8)
    for i in range(7):
        if i < 6:
            p.stream("hyena_in", 1, 2)
        if i > 0:
            p.take("hyena_turn", 2)
    for n in range(2):
        p.take(f"dft{n}", 8)
        p.take(f"idft{n}", 4)
    p.vector_slabs("mod1.gate1", 2)
    p.take("turn.hyena_out", 4)
    for i in range(2):
        p.stream("hyena_out", 1, 2)
        if i == 0:
            for k in range(2):
                p.sum_up("mod1.gate1", k)
    p.vector_slabs("mod1.pre2", 4)
    for k in range(4):
        p.sum_up("mod1.pre2", k)
    p.take("turn.n2_1", 4)
    p.mlp("mlp1", "mod1.gate2")
    return p


def constants():
    f32 = np.float32
    s, t = np.meshgrid(np.arange(P), np.arange(P), indexing="ij")
    resident = np.concatenate([np.eye(P), np.ones((P, 2 * P)), np.broadcast_to(np.arange(SEATS), (P, SEATS)),
                               s <= t], 1).astype(f32)
    low = np.where(t <= s, 0.0, -1e30)
    causal = np.concatenate([low, np.zeros((P, P)), low], 1)
    masks = [((t // (2 * L) == s // (2 * L)) & (t % (2 * L) >= L) & (s % (2 * L) < L)) for L in HGRN_LEVELS]
    masks.append((t // LAST_BLOCK == s // LAST_BLOCK) & (s <= t))
    even = np.concatenate([causal, *masks], 1).astype(f32)
    same = np.where(t // 64 <= s // 64, 0.0, -1e30)
    chunks = np.concatenate([same, np.zeros((P, P)), same], 1).astype(f32)
    tok = np.arange(S)
    place = np.stack([tok // 64, tok % 64], 1).astype(f32)

    def rope(nf):
        inv = (f32(10000.0) ** (-np.arange(nf, dtype=f32) / f32(nf))).astype(f32)
        ang = (place[:, :, None] * inv[None, None]).astype(f32)
        parts = [g(ang).reshape(NT, P, 2 * nf).transpose(1, 0, 2).reshape(P, -1) for g in (np.cos, np.sin)]
        return np.concatenate(parts, 1)

    rope2d = np.concatenate([rope(8), rope(16)], 1).astype(f32)
    f = np.arange(S) + 0.5
    ang = 2 * np.pi * np.outer(np.arange(S), f) / (2 * S)

    def tiles(a):
        return a.reshape(NT, P, S).transpose(1, 0, 2).reshape(P, -1)

    dft = np.concatenate([tiles(np.cos(ang)), tiles(np.sin(ang)), tiles(np.cos(ang).T) / S,
                          tiles(np.sin(ang).T) / S], 1).astype(f32)
    tt = np.arange(S, dtype=f32)
    t_norm = tt / f32(S)
    w = f32(2.0 * np.pi) * tt / f32(S)
    bands = np.linspace(1e-4, 7, 8, dtype=f32)
    fw = w[:, None] * bands[None]
    feats = np.zeros((P, S), f32)
    feats[:17] = np.concatenate([t_norm[:, None], np.cos(fw), -np.sin(fw)], 1).T
    deltas = np.abs(np.linspace(np.log(1e-2) / 1.5, np.log(1e-2) / 0.3, D, dtype=f32))
    window = np.exp(-t_norm[:, None] * deltas[None]).astype(f32)
    inv_freq = (f32(10000.0) ** (-np.arange(32, dtype=f32) / f32(32))).astype(f32)
    return {"resident": resident, "even_tables": even, "chunk_mask": chunks,
            "rope2d": rope2d, "dft": dft, "feats": feats, "window": window, "inv_freq": inv_freq}


def build(nc, A, out):
    plan = make_plan()
    U = plan.units
    K = plan.slabs
    ctx = ExitStack()
    with ctx:
        def sb(name, cols, dt=F32):
            return ctx.enter_context(nc.sbuf_tensor(name, [P, cols], dt))

        sems = {}

        def sem(name):
            if name not in sems:
                sems[name] = ctx.enter_context(nc.semaphore(name))
            return sems[name]

        def parts_of(name, cols, offset):
            return nc.alloc_sbuf_tensor_at(name, [P, cols], F32R, offset=offset)

        def next_at():
            return (nc.sbuf_base + 31) // 32 * 32

        ring_at = next_at()
        ring = sb("ring", RING * SLAB)
        ring_parts = [parts_of(f"slab{r}_parts", SLAB, ring_at + 4 * r * SLAB) for r in range(RING)]
        h = sb("h", NT * D)
        xT_at = next_at()
        xT = sb("xT", KD * S)
        xT_parts = parts_of("xT_parts", KD * S, xT_at)
        gain = sb("gain", 2 * D)
        resident = sb("resident", 4 * P + SEATS)
        rows = sb("rows", N_ROWS)
        cols = sb("cols", N_COLS)
        routers = sb("routers", 2 * KD * 36)
        w_fox_f = sb("w_fox_f", KD * 8)
        stat = sb("stat", 176)
        small = sb("small", 512)
        N_ARENA = 18920
        arena_at = next_at()
        arena = sb("arena", N_ARENA)
        banks = [ctx.enter_context(nc.psum_tensor(f"bank{b}", [P, 512], F32)) for b in range(8)]

        ident = resident[:, 0:P]
        ones = resident[:, P:2 * P]
        ones256 = resident[:, P:3 * P]
        seats = resident[:, 3 * P:3 * P + SEATS]
        iota8 = resident[:, 3 * P:3 * P + 8]
        tri = resident[:, 3 * P + SEATS:4 * P + SEATS]
        h3 = h[:, :].rearrange("p (t d) -> p t d", t=NT)
        xT3 = xT[:, :].rearrange("p (k s) -> p k s", k=KD)

        def row(name, n=None):
            at, width = ROWS[name]
            return rows[:, at:at + (n or width)]

        def col(name, i=0, n=1, p=P):
            return cols[0:p, COLS[name][0] + i:COLS[name][0] + i + n]

        def at(start, n):
            assert start + n <= N_ARENA, (start, n)
            return arena[:, start:start + n]

        def parts_at(name, start, n):
            return parts_of(name, n, arena_at + 4 * start)[:, :]

        def over(ap, shape, axis):
            return ap.unsqueeze(axis).to_broadcast(shape)

        bank_full = [sem(f"bank{b}_full") for b in range(8)]
        bank_drained = [sem(f"bank{b}_drained") for b in range(8)]
        slab_loaded = [sem(f"slab{r}_loaded") for r in range(RING)]
        stats_ready = sem("stats_ready")
        std_ready = sem("std_ready")
        normed = sem("normed")
        gain_loaded = [sem("gain0_loaded"), sem("gain1_loaded")]
        vec_step = sem("vec_step")
        act_step = sem("act_step")

        def full(eng, u):
            eng.wait_ge(bank_full[u.bank], u.before + 1)

        def drained(eng, u):
            eng.wait_ge(bank_drained[u.bank], u.before + 1)

        def filling(layer, name, r):
            bank = dict(FILLS)[name]
            base = min(u.before for kind in ("gate", "up", "down") for u in U[f"moe{layer}.{kind}"] if u.bank == bank)
            if isinstance(r, int) and r == -1:
                return Unit(bank, base)
            if isinstance(r, int) and r == 0:
                return Unit(bank, base + fills_before(FIRST_FILLS, name))
            in_first = sum(b == bank for _, b in FIRST_FILLS)
            if isinstance(r, int) and r == PAIRS:
                done = in_first + (PAIRS - 1) * PER_PAIR[bank]
                return Unit(bank, base + done + fills_before(LAST_FILLS, name))
            return Unit(bank, (r - 1) * PER_PAIR[bank] + (base + in_first + fills_before(FILLS, name)))

        def weight_part(name, r, half):
            if isinstance(r, int) and r == 0:
                n = 2 * FIRST_WEIGHTS.index(name) + half
                return n, high[n % 4]
            place = half if isinstance(r, int) and r == PAIRS else 2 * WEIGHTS.index(name) + half
            place += 2 * len(FIRST_WEIGHTS)
            return (r - 1) * (2 * len(WEIGHTS)) + place, high[place % 4]

        def next_weights(name, r, first, last):
            if first and name in ("gate0", "up0"):
                return {"gate0": "gate1", "up0": "up1"}[name], r
            if last and name == "up1":
                return "down1", r + 1
            if last and name == "down0":
                return None
            follower = {"gate0": "down1", "up0": "gate1", "down1": "up1", "gate1": "down0", "up1": "gate0",
                        "down0": "up0"}[name]
            return follower, (r + 1 if name in ("up1", "down0") else r)

        def weight_half(layer, name, half, parts=False):
            slab = slab_ap(K[f"moe{layer}"][0] + SLAB_OF[name], parts)
            if name.startswith("down"):
                return view_k(slab, 4, D)[:, :, half * 512:(half + 1) * 512]
            return view_k(slab, KD, 512)[:, 4 * half:4 * half + 4, :]

        def mlp_part(layer, n):
            w, j, half = MLP_PARTS[n]
            idx = K[f"mlp{layer}.w{w + 1}"][j]
            k, cols_ = (KD, 256) if w == 0 else (4, 512)
            loaded, low = (view_k(slab_ap(idx, x), k, 2 * cols_)[:, :, half * cols_:(half + 1) * cols_]
                           for x in (False, True))
            return idx, loaded, low, high[n % 4].rearrange("p k n -> p (k n)").rearrange("p (k n) -> p k n", k=k)

        def mlp_unit(layer, n):
            w, j, half = MLP_PARTS[n]
            return U[f"mlp{layer}.hidden"][2 * j + half] if w == 0 else U[f"mlp{layer}.out"][4 * j + 2 * half + 1]

        def later(u, i):
            return u.later(i * PER_PAIR[u.bank])

        def short_path(eng, layer):
            eng.wait_ge(sem("counted"), layer + 1)
            most = eng.alloc_register(f"most{layer}")
            eng.reg_load(most, most_tokens[0:1, layer:layer + 1])
            return eng.If_lt(most, SEATS + 1)

        def slab_ap(idx, parts=False):
            r = idx % RING
            return ring_parts[r][:, :] if parts else ring[:, r * SLAB:(r + 1) * SLAB]

        u_buf = at(0, 2048)
        u3 = u_buf.rearrange("p (t d) -> p t d", t=NT)
        scratch = at(2048, 2048)
        even_tables = at(4096, 384 + 640)
        causal = even_tables[:, 0:384]
        level_mask = [even_tables[:, 384 + 128 * i:512 + 128 * i] for i in range(5)]
        EV = 4096 + 1024
        hg_f = at(EV, 1024)
        hg_q = at(EV + 1024, 1024)
        hg_k = at(EV + 2048, 1024)
        hg_cum = at(EV + 3072, 1024)
        hg_i = at(EV + 4096, 1024).rearrange("p (t d) -> p t d", t=NT)
        hg_g = at(EV + 5120, 1024)
        fx_q = at(EV + 6144, 1024)
        fx_k = at(EV + 7168, 1024)
        fx_v = at(EV + 8192, 1024).rearrange("p (t d) -> p t d", t=NT)
        hg_P = at(EV + 9216, 3072).rearrange("p (b c t) -> p b c t", b=6, c=4)
        hg_qh = at(EV + 12288, 1024)
        hg_kh = at(2560, 1024)
        ev_o = at(2048, 2048).rearrange("p (t d) -> p t d", t=NT)
        fq_aug = at(EV, 1056).rearrange("p (t h d) -> p t h d", t=NT, h=8)
        fk_aug = at(EV + 1056, 1056).rearrange("p (t h d) -> p t h d", t=NT, h=8)
        fx_qT = at(EV + 9216, 2048)
        fx_kT = at(EV + 11264, 2048)
        fx_T = at(EV + 5120, 1024)
        fx_L = at(EV + 6144, 1536)
        att_P = at(0, 2048)
        silu_g = at(4096, 1024)
        hidden = at(5120, 1024)
        comb = at(6720, 2 * 34).rearrange("p (t e) -> p t e", t=NT)
        rank = at(6788, 2 * 34).rearrange("p (t e) -> p t e", t=NT)
        routed = at(6856, 64).rearrange("p (t e) -> p t e", t=NT)
        sel = at(6920, 256).rearrange("p (t c) -> p t c", t=NT)
        weighted = at(7176, 512).rearrange("p (t e a c) -> p t e a c", t=NT, e=2, a=2)
        weightedT = at(7688, 512)
        raw = at(8200, 1024).rearrange("p (w f) -> p w f", w=2)
        pair_silu = at(9224, 256)
        pair_h = at(9480, 256)
        hidden2 = parts_at("hidden_parts", 9736, 512).rearrange("p (f a c) -> p f a c", f=4, a=2)
        pair_y = [at(10248 + 1024 * e, 1024) for e in range(2)]
        fold = at(12296, SEATS)
        high = [parts_at(f"high{i}", c, 2048).rearrange("p (k n) -> p k n", k=4)
                for i, c in enumerate((2048, 4096, 14824, 16872))]
        seated2 = xT_parts[:, :].rearrange("p (k e a c) -> p k e a c", k=KD, e=2, a=2)
        route = at(6208, 512)
        mlp_y = at(6208, 2048).rearrange("p (t d) -> p t d", t=NT)
        xT_high = xT_parts[:, :].rearrange("p (k s) -> p k s", k=KD)
        xT_low = parts_at("xT_low", 9280, 2048).rearrange("p (k s) -> p k s", k=KD)
        mlp_hidden = [parts_at(f"mlp_hidden{i}", c, 2048).rearrange("p (a f s) -> p a f s", a=2, f=4)
                      for i, c in enumerate((0, 11328))]
        squares = [at(13376 + 512 * i, 512) for i in range(2)]
        chunk_mask = at(4096, 384)
        od_q = at(4480, 2048)
        od_k = at(6528, 2048)
        od_v = at(8576, 2048).rearrange("p (t d) -> p t d", t=NT)
        od_tab = small[:, 0:256]
        od_qT = at(10624, 4096)
        od_kT = at(14720, 4096)
        od_L = at(2048, 1536)
        od_T = at(4480, 1024)
        od_o = at(6528, 2048).rearrange("p (t d) -> p t d", t=NT)
        c_wide = at(4096, 2048)
        shift, scale = at(6144, 1024), at(7168, 1024)
        shift_c, scale_c = at(8192, 1024), at(9216, 1024)
        ctx_x = at(10240, 2048)
        ctx_u = at(12288, 2048)
        ctxT = at(14336, 2048).rearrange("p (k s) -> p k s", k=KD)
        rope2d = at(6144, 192)
        z_cq = at(6336, 768)
        z_ckv = at(7104, 1024)
        z_kr = at(8128, 128)
        z_gq = at(8256, 1024)
        z_gk = at(9280, 512)
        z_gv = at(9792, 512).rearrange("p (t d) -> p t d", t=4)
        cqT = at(10304, 768).rearrange("p (k s) -> p k s", k=3)
        ckvT = at(11072, 1024).rearrange("p (k s) -> p k s", k=2)
        ml_v = at(16704, 2048).rearrange("p (t h d) -> p t h d", t=4, h=8)
        ml_q = at(12096, 1536)
        ml_k = at(13632, 3072)
        b2_o = at(12096, 2048).rearrange("p (t d) -> p t d", t=NT)
        b2_P = at(14144, 1024)
        b2_T = at(15168, 1024)
        qT2 = xT[:, 0:2048]
        kT2 = at(0, 4096)
        gate = at(14336, 1024)
        two, four = [rows[:, 512 * i:512 * (i + 1)] for i in range(2)], [at(16384 + 512 * i, 512) for i in range(4)]
        partial = {"mod0.pre1": four, "mod0.gate1": two, "mod0.pre2": four, "mod0.gate2": two, "mod1.pre1": four,
                   "mod1.gate1": two, "mod1.pre2": four, "mod1.gate2": two}
        silu_c = small[:, 464:472]
        gate2 = at(8256, 1024)
        dft = at(0, 2048)
        cosT, sinT, icos, isin = [dft[:, 512 * i:512 * (i + 1)].rearrange("p (k f) -> p k f", k=NT) for i in range(4)]
        f_sum = at(2048, 2048)
        window = at(4096, 2048)
        h4 = at(6144, 4096)
        f_norm = rows[:, 0:1024]
        spectra = at(10728, 8192)
        hy_x = [at(2048, 2048), at(4096, 2048), at(8680, 2048)]
        z_pad = at(6144, 2064)
        conv = rows[:, 0:1024]
        y_re = at(6144, 2048)
        y_im = xT[:, 0:2048]
        prod = [rows[:, 0:512], rows[:, 512:1024]]

        def dma_done(eng, name, n=1):
            eng.wait_ge(sem(name), 16 * n)

        s_sum, s_std, s_inv = stat[:, 0:32], stat[:, 32:64], stat[:, 64:96]
        eps_col, lam, neg_lam = stat[:, 96:97], stat[:, 97:98], stat[:, 98:99]
        lb_col, one_less_lb = stat[:, 100:104], stat[:, 104:108]
        neg_max = stat[:, 112:120].rearrange("p (a m g) -> p a m g", a=2, m=2)
        exp_sum = stat[:, 120:136].rearrange("p (a m g) -> p a m g", a=4, m=2)
        exp_inv = stat[:, 136:152].rearrange("p (a m g) -> p a m g", a=4, m=2)

        route_logf = small[:, 448:464]
        pos_tile = ctx.enter_context(nc.sbuf_tensor("pos_tile", [P, NT], I32))
        od_o_flat = at(6528, 2048)
        most_tokens = ctx.enter_context(nc.sbuf_tensor("most_tokens", [P, 2], I32))
        c_kv = z_ckv.rearrange("p (t d) -> p t d", t=4)
        f_h = small[:, 0:256]
        f_diff = h4[:, 0:2048]
        CAUSAL = [(0, 0, P), (1, P, 2 * P)]
        W_IN = A["even_w_in"]

        def view_k(ap, k, n):
            return ap[:, 0:k * n].rearrange("p (k n) -> p k n", k=k)

        def part(w, c0, n):
            return w[:, c0:c0 + n].rearrange("(k p) n -> p k n", p=P)

        SOURCES = {
            "hgrn_f": [part(W_IN, 512, 512)], "hgrn_q": [part(W_IN, 0, 512)], "hgrn_i": [part(W_IN, 1024, 512)],
            "fox_q": [part(W_IN, 2048, 512)], "fox_k": [part(W_IN, 2560, 512)], "fox_v": [part(W_IN, 3072, 512)],
            "hgrn_g": [part(W_IN, 1536, 512)],
            "even_out": [part(A["even_w_out"], 512 * i, 512) for i in range(2)],
            "odd_in": [part(A["odd_w_in"], 512 * i, 512) for i in range(6)],
            "odd_out": [part(A["odd_w_out"], 512 * i, 512) for i in range(2)],
            "mla_cq": [part(A["a_w_in"], 0, 384)], "mla_ckv": [part(A["a_w_in"], 384, 288)],
            "gqa_q": [part(A["a_w_in"], 672, 512)], "gqa_kv": [part(A["a_w_in"], 1184, 256)],
            "mla_q": [part(A["a_w_q_b"], 0, 768)], "mla_kv": [part(A["a_w_kv_b"], 0, 1024)],
            "a_out": [part(A["a_w_out"], 512 * i, 512) for i in range(2)],
            "hyena_out": [part(A["h_w_out"], 512 * i, 512) for i in range(2)],
            "filter_w4": [A["h_f_w4"]],
        }
        for l in range(2):
            wm = A["w_mod"][l]
            SOURCES[f"mod{l}.pre1"] = [part(wm, 512 * i, 512) for i in range(4)]
            SOURCES[f"mod{l}.gate1"] = [part(wm, 2048 + 512 * i, 512) for i in range(2)]
            SOURCES[f"mod{l}.pre2"] = [part(wm, 3072 + 512 * i, 512) for i in range(4)]
            SOURCES[f"mod{l}.gate2"] = [part(wm, 5120 + 512 * i, 512) for i in range(2)]

        block = ctx.enter_context(nc.Block())

        @block.sync
        def _(sp):
            def load(idx, src):
                r = idx % RING
                if idx >= RING:
                    reader = plan.last_reader[idx - RING]
                    sp.wait_ge(bank_full[reader.bank], reader.before + 1)
                dst = slab_ap(idx)
                if len(src.shape) == 3:
                    dst = view_k(dst, src.shape[1], src.shape[2])
                    sp.dma_start(dst, src).then_inc(slab_loaded[r], 16)
                else:
                    sp.dma_start(dst[0:src.shape[0], 0:src.shape[1]], src).then_inc(slab_loaded[r], 16)

            def stream(name):
                for idx, src in zip(K[name], SOURCES[name], strict=True):
                    load(idx, src)

            def expert_source(layer, e, which):
                w = (A["moe_w_gate"], A["moe_w_up"], A["moe_w_down"])[which]
                k = KD if which < 2 else 4
                return w[bass.ds(layer * N_EXPERTS + e, 1)].rearrange("a (k p) n -> p (a k) n", p=P)

            def experts(layer):
                name = f"moe{layer}"
                first = K[name][0]
                for j in range(RING):
                    load(first + j, expert_source(layer, j // EXPERT_SLABS, j % EXPERT_SLABS))

                def next_pair(i, j):
                    dst = slab_ap(first + j)
                    src = expert_source(layer, i * 2 + j // EXPERT_SLABS, j % EXPERT_SLABS)
                    sp.dma_start(view_k(dst, src.shape[1], src.shape[2]), src)\
                        .then_inc(slab_loaded[(first + j) % RING], 16)

                def refill_short(i):
                    for name in ("gate0", "up0", "gate1", "up1", "down0", "down1"):
                        if name == "down1":
                            reader = filling(layer, "down1.1", i)
                        else:
                            reader = filling(layer, "down0.1" if name == "down0" else name, i - 1)
                        sp.wait_ge(bank_full[reader.bank], reader.before + 1)
                        next_pair(i, SLAB_OF[name])

                with short_path(sp, layer):
                    refill_short(1)
                    with sp.Fori(2, PAIRS) as i:
                        refill_short(i)
                with sp.Else():
                    with sp.Fori(1, PAIRS) as i:
                        for j in range(RING):
                            reader = plan.last_reader[first + j]
                            sp.wait_ge(bank_full[reader.bank], (i - 1) * PER_PAIR[reader.bank] + (reader.before + 1))
                            next_pair(i, j)

            def mlp(layer):
                w1, w2 = A["mlp_w1"][layer], A["mlp_w2"][layer]
                gate_name = f"mod{layer}.gate2"
                for w, j, half in MLP_PARTS:
                    if half == 0:
                        load(K[f"mlp{layer}.w{w + 1}"][j], part(w1, 512 * j, 512) if w == 0 else
                             w2[512 * j:512 * (j + 1), :].rearrange("(k p) n -> p k n", p=P))
                    elif w == 1 and j + 3 in GATE_SUMS:
                        i = GATE_SUMS.index(j + 3)
                        load(K[gate_name][i], SOURCES[gate_name][i])

            sp.dma_start(h3, A["x"].rearrange("(t p) d -> p t d", p=P)).then_inc(sem("x_loaded"), 16)
            sp.dma_start(gain[:, 0:D], A["gains"][0].partition_broadcast(P)).then_inc(sem("first_gain_loaded"), 16)
            sp.dma_start(resident[:, :], A["resident"]).then_inc(sem("resident_loaded"), 16)
            for name in ("hgrn_f", "hgrn_q", "hgrn_i", "fox_q", "fox_k", "fox_v", "hgrn_g", "even_out"):
                stream(name)
            experts(0)
            stream("odd_in")
            stream("odd_out")
            experts(1)
            for name in ("mod0.pre1", "mla_cq", "mla_ckv", "gqa_q", "gqa_kv", "mla_q", "mla_kv", "mod0.gate1",
                         "a_out", "mod0.pre2"):
                stream(name)
            mlp(0)
            stream("mod1.pre1")
            stream("filter_w4")
            for i in range(6):
                load(K["hyena_in"][i], part(A["h_w_in"], 512 * i, 512))
            for name in ("mod1.gate1", "hyena_out", "mod1.pre2"):
                stream(name)
            mlp(1)
            sp.wait_ge(sem("result_ready"), 1)
            sp.dma_start(out.rearrange("(t p) d -> p t d", p=P), u3).then_inc(sem("stored"), 16)
            sp.wait_ge(sem("stored"), 16)

        @block.gpsimd
        def _(pool):
            def load(name, dst, src):
                pool.dma_start(dst, src).then_inc(sem(name), 16)


            def gain_row(n):
                if n >= 2:
                    pool.wait_ge(sem("gain_used"), n - 1)
                pool.dma_start(gain[:, (n % 2) * D:(n % 2 + 1) * D], A["gains"][n].partition_broadcast(P))\
                    .then_inc(gain_loaded[n % 2], 16)

            load("rows_loaded", rows[:, :], A["rows"].partition_broadcast(P))
            load("cols_loaded", cols[:, :], A["cols"])
            load("fox_f_loaded", w_fox_f[:, :].rearrange("p (k n) -> p k n", k=KD), part(W_IN, 3584, 8))
            load("cols_loaded", pos_tile[:, :], A["positions"])
            load("even_tables_loaded", even_tables, A["even_tables"])
            for l in range(2):
                load("routers_loaded", routers[:, l * 288:(l + 1) * 288].rearrange("p (k n) -> p k n", k=KD),
                     A["routers"][l].rearrange("(k p) n -> p k n", p=P))
            gain_row(1)
            gain_row(2)
            gain_row(3)
            pool.wait_ge(normed, 3)
            load("chunk_loaded", chunk_mask, A["chunk_mask"])
            gain_row(4)
            pool.wait_ge(sem("moe_done"), 2)
            for dst, k, c in ((shift, 0, 0), (scale, 0, 1), (shift_c, 0, 0), (scale_c, 0, 1)):
                load("bias0_pre1", dst, A["b_mod"][k, c * D:(c + 1) * D].partition_broadcast(P))
            load("ctx_loaded", ctx_x.rearrange("p (t d) -> p t d", t=NT), A["ctx"].rearrange("(t p) d -> p t d", p=P))
            gain_row(5)
            pool.wait_ge(normed, 5)
            load("rope2d_loaded", rope2d, A["rope2d"])
            pool.wait_ge(sem("gqa_o"), 16)
            load("bias0_gate1", gate, A["b_mod"][0, 2 * D:3 * D].partition_broadcast(P))
            load("bias0_pre2", shift, A["b_mod"][0, 3 * D:4 * D].partition_broadcast(P))
            load("bias0_pre2", scale, A["b_mod"][0, 4 * D:5 * D].partition_broadcast(P))
            gain_row(6)
            pool.wait_ge(sem("gate_used"), 1)
            load("bias0_gate2", gate2, A["b_mod"][0, 5 * D:6 * D].partition_broadcast(P))
            gain_row(7)
            pool.wait_ge(sem("mlp_done"), 1)
            load("bias1_pre1", shift, A["b_mod"][1, 0:D].partition_broadcast(P))
            load("bias1_pre1", scale, A["b_mod"][1, D:2 * D].partition_broadcast(P))
            pool.wait_ge(normed, 7)
            load("filter_loaded", small[:, 0:256], A["feats"])
            load("filter_loaded", small[0:17, 256:320], A["h_f_w1"])
            load("filter_loaded", small[0:64, 320:384], A["h_f_w2"])
            load("filter_loaded", small[0:64, 384:448], A["h_f_w3"])
            load("window_loaded", window.rearrange("p (t d) -> p t d", t=NT),
                 A["window"].rearrange("(t p) d -> p t d", p=P))
            turned = U["turn.n1_1"][-1]
            pool.wait_ge(bank_full[turned.bank], turned.before + 1)
            load("dft_loaded", dft, A["dft"])
            gain_row(8)
            gain_row(9)
            gain_row(10)
            pool.wait_ge(sem("hyena_y"), 8)
            load("bias1_gate1", gate, A["b_mod"][1, 2 * D:3 * D].partition_broadcast(P))
            load("bias1_pre2", shift, A["b_mod"][1, 3 * D:4 * D].partition_broadcast(P))
            load("bias1_pre2", scale, A["b_mod"][1, 4 * D:5 * D].partition_broadcast(P))
            pool.wait_ge(sem("gate_used"), 2)
            load("bias1_gate2", gate2, A["b_mod"][1, 5 * D:6 * D].partition_broadcast(P))

        @block.tensor
        def _(pe):
            mm = nc.tensor.matmul

            def claim(u):
                if u.before:
                    pe.wait_ge(bank_drained[u.bank], u.before)

            def tell(ins, u):
                ins.then_inc(bank_full[u.bank], 1)

            def slab_in(idx):
                pe.wait_ge(slab_loaded[idx % RING], 16 * (idx // RING + 1))

            def turn(name, src):
                for j, u in enumerate(U[name]):
                    claim(u)
                    for i in range(4):
                        k = 4 * (j % 2) + i
                        last = nc.tensor.transpose(banks[u.bank][:, i * P:(i + 1) * P],
                                                   src[:, j // 2, k * P:(k + 1) * P], ident)
                    tell(last, u)

            def turned(name):
                for u in U[name]:
                    drained(pe, u)

            def project(units, idx, n, lhs, k_tiles=KD, c0=0, width=None):
                w = view_k(slab_ap(idx), k_tiles, width or n)
                for tile, u in enumerate(units):
                    claim(u)
                    for k in range(k_tiles):
                        last = mm(banks[u.bank][:, 0:n], lhs(k, tile), w[:, k, c0:c0 + n],
                                  start=(k == 0), stop=(k == k_tiles - 1))
                    tell(last, u)

            def project_cols(units, idx, rhs):
                w = view_k(slab_ap(idx), KD, 512)
                for j, u in enumerate(units):
                    claim(u)
                    for i in range(2):
                        f0 = (2 * j + i) * P
                        for k in range(KD):
                            last = mm(banks[u.bank][:, i * S:(i + 1) * S], w[:, k, f0:f0 + P], rhs[:, k, :],
                                      start=(k == 0), stop=(k == KD - 1))
                    tell(last, u)

            def tokens(k, tile):
                return xT3[:, k, tile * P:(tile + 1) * P]

            def turn_heads(name, n, src, dk, tiles=NT):
                blocks = [(hh, t) for hh in range(n) for t in range(tiles)]
                for j, u in enumerate(U[name]):
                    claim(u)
                    for i, (hh, t) in enumerate(blocks[4 * j:4 * j + 4]):
                        last = nc.tensor.transpose(banks[u.bank][0:dk, i * P:(i + 1) * P], src(hh, t), ident)
                    tell(last, u)

            def attend(name, steps, maps, logits, n_blocks, probs, ready, pT, values):
                for s in range(steps + 2):
                    if s < steps:
                        for m in range(maps):
                            u = U[name + ".logits"][s * maps + m]
                            claim(u)
                            for c0, n, lhsT, rhs in logits(s, m):
                                last = mm(banks[u.bank][:, c0:c0 + n], lhsT, rhs, start=True, stop=True)
                            tell(last, u)
                    if 1 <= s <= steps:
                        u = U[name + ".turn"][s - 1]
                        claim(u)
                        ready(s - 1)
                        for b in range(n_blocks):
                            last = nc.tensor.transpose(banks[u.bank][:, b * P:(b + 1) * P],
                                                       probs(s - 1)[:, b * P:(b + 1) * P], ident)
                        tell(last, u)
                    if s >= 2:
                        u = U[name + ".out"][s - 2]
                        claim(u)
                        drained(pe, U[name + ".turn"][s - 2])
                        for c0, n, terms in values(s - 2):
                            for i, (b, v) in enumerate(terms):
                                last = mm(banks[u.bank][:, c0:c0 + n], pT(s - 2)[:, b * P:(b + 1) * P], v,
                                          start=(i == 0), stop=(i == len(terms) - 1))
                        tell(last, u)

            def c_product(u, idx, source):
                slab_in(idx)
                project([u], idx, 512, lambda k, tile: c_wide[:, (source * KD + k) * P:(source * KD + k + 1) * P])

            def sum_up(u, name, i):
                pe.wait_ge(sem(name + ".partial"), i + 1)
                claim(u)
                tell(mm(banks[u.bank][:, :], ones, partial[name][i], start=True, stop=True), u)

            pe.wait_ge(sem("resident_loaded"), 16)

            pe.wait_ge(normed, 1)
            turn("turn.mix0", u3)
            turned("turn.mix0")
            for name in ("hgrn_f", "hgrn_q"):
                slab_in(K[name][0])
                project_cols(U[name], K[name][0], xT3)
            u = U["fox_f"][0]
            pe.wait_ge(sem("fox_f_loaded"), 16)
            for tile in range(NT):
                for k in range(KD):
                    last = mm(banks[u.bank][:, tile * 8:(tile + 1) * 8], tokens(k, tile),
                              w_fox_f[:, k * 8:(k + 1) * 8], start=(k == 0), stop=(k == KD - 1))
            tell(last, u)
            for name in ("hgrn_i", "fox_q", "fox_k", "fox_v", "hgrn_g"):
                slab_in(K[name][0])
                project(U[name], K[name][0], 512, tokens)
            u = U["fox_cum"][0]
            claim(u)
            pe.wait_ge(sem("fox_logf"), 1)
            pe.wait_ge(sem("even_tables_loaded"), 16)
            logf = route_logf
            mm(banks[u.bank][:, 0:8], tri, logf[:, 0:8], start=True, stop=True)
            mm(banks[u.bank][:, 8:16], ones, logf[:, 0:8], start=True, stop=False)
            tell(mm(banks[u.bank][:, 8:16], tri, logf[:, 8:16], start=False, stop=True), u)
            for n, name in enumerate([f"level{L}" for L in HGRN_LEVELS] + ["diagonal", "level128"]):
                pe.wait_ge(sem("hgrn_factors"), n + 1)
                for j, u in enumerate(U[name]):
                    claim(u)
                    half, tile = j % 2, j // 2
                    s0, t0 = (tile, tile) if name != "level128" else (0, 1)
                    for c in range(4):
                        lo = half * 64
                        kh = hg_kh[lo:lo + 64, c * S + s0 * P:c * S + (s0 + 1) * P]
                        qh = hg_qh[lo:lo + 64, c * S + t0 * P:c * S + (t0 + 1) * P]
                        last = mm(banks[u.bank][:, c * P:(c + 1) * P], kh, qh, start=True, stop=True)
                    tell(last, u)
            for u in U["level128"]:
                drained(pe, u)
            for tile in range(NT):
                u = U["hgrn_o"][tile]
                claim(u)
                for hh in range(8):
                    c, half = hh // 2, hh % 2
                    dst = banks[u.bank][:, hh * 64:(hh + 1) * 64]
                    own = hg_P[:, 2 * tile + half, c, :]
                    last = mm(dst, own, hg_i[:, tile, hh * 64:(hh + 1) * 64], start=True, stop=(tile == 0))
                    if tile == 1:
                        last = mm(dst, hg_P[:, 4 + half, c, :], hg_i[:, 0, hh * 64:(hh + 1) * 64],
                                  start=False, stop=True)
                tell(last, u)
            pe.wait_ge(sem("fox_aug"), 1)
            turn_heads("fox_qT", 8, lambda hh, t: fq_aug[:, t, hh, :], 66)
            turn_heads("fox_kT", 8, lambda hh, t: fk_aug[:, t, hh, :], 66)
            turned("fox_qT")
            turned("fox_kT")

            def fox_logits(s, m):
                return [(c0, n, fx_qT[0:66, s * S + t * P:s * S + (t + 1) * P], fx_kT[0:66, s * S:s * S + n])
                        for t, c0, n in CAUSAL]

            attend("fox", 8, 1, fox_logits, 3, lambda s: att_P[:, (s % 2) * 1024:(s % 2) * 1024 + 384],
                   lambda s: pe.wait_ge(sem("fox_exp"), 2 * s + 2),
                   lambda s: fx_T[:, (s % 2) * 512:(s % 2) * 512 + 384],
                   lambda s: [(0, 64, [(0, fx_v[:, 0, s * 64:(s + 1) * 64])]),
                              (64, 64, [(1, fx_v[:, 0, s * 64:(s + 1) * 64]), (2, fx_v[:, 1, s * 64:(s + 1) * 64])])])
            pe.wait_ge(sem("fox_o"), 8)
            turn("turn.even_out", ev_o)
            turned("turn.even_out")
            for i, idx in enumerate(K["even_out"]):
                slab_in(idx)
                project(U["even_out"][2 * i:2 * i + 2], idx, 512, tokens)

            def moe(layer):
                name = f"moe{layer}"
                pe.wait_ge(normed, 2 * layer + 2)
                turn(f"turn.ffn{layer}", u3)
                turned(f"turn.ffn{layer}")
                u = U[f"router{layer}"][0]
                claim(u)
                pe.wait_ge(sem("routers_loaded"), 32)
                for tile in range(NT):
                    for k in range(KD):
                        at_k = layer * 288 + k * 36
                        last = mm(banks[u.bank][:, tile * 36:(tile + 1) * 36], tokens(k, tile),
                                  routers[:, at_k:at_k + 36], start=(k == 0), stop=(k == KD - 1))
                tell(last, u)
                u = U[f"rank{layer}"][0]
                claim(u)
                pe.wait_ge(sem("routed"), layer + 1)
                dst = banks[u.bank]
                mm(dst[:, 0:32], tri, routed[:, 0], start=True, stop=True)
                mm(dst[:, 32:64], ones, routed[:, 0], start=True, stop=False)
                mm(dst[:, 32:64], tri, routed[:, 1], start=False, stop=True)
                mm(dst[:, 64:96], ones, routed[:, 0], start=True, stop=False)
                tell(mm(dst[:, 64:96], ones, routed[:, 1], start=False, stop=True), u)
                with short_path(pe, layer):
                    moe_short(layer)
                with pe.Else():
                    moe_dense(layer)

            def moe_short(layer):
                def enter(name, r):
                    u = filling(layer, name, r)
                    pe.wait_ge(bank_drained[u.bank], u.before)
                    return u, banks[u.bank]

                def wait_drained(name, r):
                    drained(pe, filling(layer, name, r))

                def wait_low(name, r, half):
                    n, hi = weight_part(name, r, half)
                    pe.wait_ge(sem(f"low{layer}"), n + 1)
                    return hi, weight_half(layer, name, half, True)

                def gather(r):
                    pe.wait_ge(sem(f"seats{layer}"), r + 2)
                    for j in range(2):
                        u, dst = enter(f"gather{j}", r)
                        for c in range(4):
                            k = 4 * j + c
                            for t in range(NT):
                                last = mm(dst[:, c * P:(c + 1) * P], u3[:, t, k * P:(k + 1) * P], sel[:, t, :],
                                          start=(t == 0), stop=(t == 1))
                        tell(last, u)

                def into(name, r, e):
                    u, dst = enter(name, r)
                    for half in range(2):
                        parts = wait_low(name, r, half)
                        for a, part_ in enumerate(parts):
                            for k in range(4):
                                last = mm(dst[:, :], seated2[:, 4 * half + k, e], part_[:, k, :],
                                          start=(half == a == k == 0), stop=(half == a == 1 and k == 3))
                        if half == 0:
                            last.then_inc(sem(f"half_used{layer}"), 1)
                        else:
                            tell(last, u)

                def add_parts(e, r):
                    wait_drained(f"gate{e}", r)
                    wait_drained(f"up{e}", r)
                    u, dst = enter(f"fold{e}", r)
                    for w in range(2):
                        for f in range(4):
                            last = mm(dst[:, (4 * w + f) * SEATS:(4 * w + f + 1) * SEATS], raw[:, w, f * P:(f + 1) * P],
                                      fold, start=True, stop=True)
                    tell(last, u)

                def down(e, r):
                    pe.wait_ge(sem(f"hidden{layer}"), r * 2 + 1 - e)
                    for half in range(2):
                        u, dst = enter(f"down{e}.{half}", r)
                        for a, part_ in enumerate(wait_low(f"down{e}", r, half)):
                            for f in range(4):
                                last = mm(dst[:, :], hidden2[:, f], part_[:, f, :],
                                          start=(a == f == 0), stop=(a == 1 and f == 3))
                        tell(last, u)

                def turn_weights(r):
                    pe.wait_ge(sem(f"weights{layer}"), r)
                    u, dst = enter("turn", r)
                    for e in range(2):
                        for t in range(NT):
                            c = (e * NT + t) * P
                            last = nc.tensor.transpose(dst[:, c:c + P], weighted[:, t, e].rearrange("p a c -> p (a c)"),
                                                       ident)
                    tell(last, u)

                def scatter(r):
                    wait_drained("turn", r)
                    for half in range(2):
                        wait_drained(f"down0.{half}", r - 1)
                        wait_drained(f"down1.{half}", r)
                    for j in range(4):
                        u, dst = enter(f"out{j}", r)
                        for e in range(2):
                            c = (e * NT + j // 2) * P
                            last = mm(dst[:, :], weightedT[:, c:c + P], pair_y[e][:, (j % 2) * 512:(j % 2 + 1) * 512],
                                      start=(e == 0), stop=(e == 1))
                        tell(last, u)

                def round_(r, first=False, last=False):
                    for j in range(2):
                        wait_drained(f"gather{j}", r - 1)
                    into("gate0", r, 0)
                    into("up0", r, 0)
                    if not first:
                        down(1, r)
                    add_parts(0, r)
                    if not first:
                        turn_weights(r)
                    into("gate1", r, 1)
                    into("up1", r, 1)
                    if not first:
                        scatter(r)
                    down(0, r)
                    if not last:
                        gather(r)
                    add_parts(1, r)

                gather(-1)
                round_(0, first=True)
                round_(1)
                with pe.Fori(2, PAIRS - 1) as r:
                    round_(r)
                round_(PAIRS - 1, last=True)
                down(1, PAIRS)
                turn_weights(PAIRS)
                scatter(PAIRS)

            def moe_dense(layer):
                name = f"moe{layer}"
                first = K[name][0]
                with pe.Fori(0, PAIRS) as i:
                    for e in range(2):
                        ups = [[later(x, i) for x in U[name + kind][2 * e:2 * e + 2]] for kind in (".gate", ".up")]
                        for w, units in enumerate(ups):
                            idx = first + EXPERT_SLABS * e + w
                            pe.wait_ge(slab_loaded[idx % RING], i * 16 + 16 * (idx // RING + 1))
                            slab = view_k(slab_ap(idx), KD, 512)
                            for j, u in enumerate(units):
                                pe.wait_ge(bank_drained[u.bank], u.before)
                                for c in range(2):
                                    f0 = (2 * j + c) * P
                                    for k in range(KD):
                                        last = mm(banks[u.bank][:, c * S:(c + 1) * S], slab[:, k, f0:f0 + P],
                                                  xT3[:, k, :], start=(k == 0), stop=(k == KD - 1))
                                tell(last, u)
                        idx = first + EXPERT_SLABS * e + 2
                        pe.wait_ge(slab_loaded[idx % RING], i * 16 + 16 * (idx // RING + 1))
                        for u in ups[1]:
                            pe.wait_ge(bank_drained[u.bank], u.before + 1)
                        slab = view_k(slab_ap(idx), 4, D)
                        for j in range(4):
                            u = later(U[name + ".down"][4 * e + j], i)
                            pe.wait_ge(bank_drained[u.bank], u.before)
                            for f in range(4):
                                last = mm(banks[u.bank][:, :], hidden[:, f * S + (j // 2) * P:f * S + (j // 2 + 1) * P],
                                          slab[:, f, (j % 2) * 512:(j % 2 + 1) * 512], start=(f == 0), stop=(f == 3))
                            tell(last, u)
                    u = later(U[name + ".even"][0], i)
                    pe.wait_ge(bank_drained[u.bank], u.before)
                    tell(nc.tensor.transpose(banks[u.bank][:, 0:P], ident, ident), u)

            moe(0)

            pe.wait_ge(normed, 3)
            turn("turn.mix1", u3)
            turned("turn.mix1")
            for i, idx in enumerate(K["odd_in"]):
                slab_in(idx)
                project(U["odd_in"][2 * i:2 * i + 2], idx, 512, tokens)
            pe.wait_ge(sem("odd_qk"), 1)
            turn_heads("diff_qT", 16, lambda hh, t: od_q[:, t * D + hh * 64:t * D + (hh + 1) * 64], 64)
            pe.wait_ge(sem("odd_qk"), 2)
            turn_heads("diff_kT", 16, lambda hh, t: od_k[:, t * D + hh * 64:t * D + (hh + 1) * 64], 64)
            turned("diff_qT")
            turned("diff_kT")

            def diff_logits(s, m):
                c = (2 * s + m) * S
                return [(c0, n, od_qT[0:64, c + t * P:c + (t + 1) * P], od_kT[0:64, c:c + n]) for t, c0, n in CAUSAL]

            attend("diff", 8, 2, diff_logits, 3, lambda s: att_P[:, (s % 2) * 1024:(s % 2) * 1024 + 384],
                   lambda s: pe.wait_ge(sem("diff_probs"), s + 1),
                   lambda s: od_T[:, (s % 2) * 512:(s % 2) * 512 + 384],
                   lambda s: [(0, P, [(0, od_v[:, 0, s * P:(s + 1) * P])]),
                              (P, P, [(1, od_v[:, 0, s * P:(s + 1) * P]), (2, od_v[:, 1, s * P:(s + 1) * P])])])
            pe.wait_ge(sem("diff_o"), 1)
            turn("turn.odd_out", od_o)
            turned("turn.odd_out")
            for i, idx in enumerate(K["odd_out"]):
                slab_in(idx)
                project(U["odd_out"][2 * i:2 * i + 2], idx, 512, tokens)
            moe(1)

            pe.wait_ge(sem("c_wide_ready"), 1)
            for i, idx in enumerate(K["mod0.pre1"]):
                for_c, for_ctx = U["mod0.pre1"][2 * i:2 * i + 2]
                c_product(for_ctx, idx, 1)
                sum_up(for_c, "mod0.pre1", i)
            pe.wait_ge(sem("ctx_normed"), 1)
            turn("turn.n1_0", ctx_u.rearrange("p (t d) -> p t d", t=NT))
            pe.wait_ge(normed, 5)
            turn("turn.ctx", u3)
            turned("turn.n1_0")
            turned("turn.ctx")

            def all_tokens(k, tile):
                return tokens(k, tile) if tile < 2 else ctxT[:, k, (tile - 2) * P:(tile - 1) * P]

            for name, n in (("mla_cq", 384), ("mla_ckv", 288), ("gqa_q", 512), ("gqa_kv", 256)):
                slab_in(K[name][0])
                project(U[name], K[name][0], n, all_tokens)
            pe.wait_ge(sem("lora_ready"), 1)
            for t, u in enumerate(U["turn.cq"]):
                claim(u)
                for k in range(3):
                    c0 = t * 384 + k * P
                    last = nc.tensor.transpose(banks[u.bank][:, k * P:(k + 1) * P], z_cq[:, c0:c0 + P], ident)
                tell(last, u)
            for k, u in enumerate(U["turn.ckv"]):
                claim(u)
                for t in range(4):
                    last = nc.tensor.transpose(banks[u.bank][:, t * P:(t + 1) * P],
                                               c_kv[:, t, k * P:(k + 1) * P], ident)
                tell(last, u)
            turned("turn.cq")
            turned("turn.ckv")
            slab_in(K["mla_q"][0])
            for half in range(2):
                project(U["mla_q"][2 * half:2 * half + 2], K["mla_q"][0], 384,
                        lambda k, tile: cqT[:, k, tile * P:(tile + 1) * P], 3, 384 * half, 768)
            slab_in(K["mla_kv"][0])
            for half in range(2):
                project(U["mla_kv"][4 * half:4 * half + 4], K["mla_kv"][0], 512,
                        lambda k, tile: ckvT[:, k, tile * P:(tile + 1) * P], 2, 512 * half, D)
            pe.wait_ge(sem("mla_qk"), 1)
            turn_heads("mla_qT", 8, lambda hh, t: ml_q[:, t * 768 + hh * 96:t * 768 + (hh + 1) * 96], 96)
            turn_heads("mla_kT", 8, lambda hh, t: ml_k[:, t * 768 + hh * 96:t * 768 + (hh + 1) * 96], 96, 4)
            turned("mla_qT")
            turned("mla_kT")

            def full_logits(dk, group):
                def logits(s, m):
                    hh, t = s // 2, s % 2
                    kv = hh // group
                    return [(0, 512, qT2[0:dk, hh * S + t * P:hh * S + (t + 1) * P], kT2[0:dk, kv * 512:(kv + 1) * 512])]
                return logits

            def b2_probs(s):
                return b2_P[:, (s % 2) * 512:(s % 2 + 1) * 512]

            def b2_turned(s):
                return b2_T[:, (s % 2) * 512:(s % 2 + 1) * 512]

            attend("mla", 16, 1, full_logits(96, 1), 4, b2_probs,
                   lambda s: drained(pe, U["mla.logits"][s]), b2_turned,
                   lambda s: [(0, 64, [(t, ml_v[:, t, s // 2, :]) for t in range(4)])])
            pe.wait_ge(sem("gqa_qk"), 1)
            turn_heads("gqa_qT", 8, lambda hh, t: z_gq[:, t * 512 + hh * 64:t * 512 + (hh + 1) * 64], 64)
            turn_heads("gqa_kT", 2, lambda hh, t: z_gk[:, t * P + hh * 64:t * P + (hh + 1) * 64], 64, 4)
            turned("gqa_qT")
            turned("gqa_kT")
            attend("gqa", 16, 1, full_logits(64, 4), 4, b2_probs,
                   lambda s: drained(pe, U["gqa.logits"][s]), b2_turned,
                   lambda s: [(0, 64, [(t, z_gv[:, t, s // 8 * 64:(s // 8 + 1) * 64]) for t in range(4)])])
            pe.wait_ge(sem("gqa_o"), 16)
            turn("turn.a_out", b2_o)
            turned("turn.a_out")
            for i, idx in enumerate(K["a_out"]):
                slab_in(idx)
                project(U["a_out"][2 * i:2 * i + 2], idx, 512, tokens)
                if i == 0:
                    for k in range(2):
                        sum_up(U["mod0.gate1"][k], "mod0.gate1", k)
            for k in range(4):
                sum_up(U["mod0.pre2"][k], "mod0.pre2", k)

            def mlp(layer):
                for n, (w, j, half) in enumerate(MLP_PARTS):
                    _, _, w_low, w_high = mlp_part(layer, n)
                    if w == half == 0 and j in GATE_SUMS:
                        i = GATE_SUMS.index(j)
                        sum_up(U[f"mod{layer}.gate2"][i], f"mod{layer}.gate2", i)
                    pe.wait_ge(sem("mlp_low"), len(MLP_PARTS) * layer + n + 1)
                    if w == 0:
                        u = U[f"mlp{layer}.hidden"][2 * j + half]
                        claim(u)
                        for c in range(2):
                            dst, fs = banks[u.bank][:, c * S:(c + 1) * S], slice(c * P, (c + 1) * P)
                            for k in range(KD):
                                mm(dst, w_high[:, k, fs], xT_high[:, k, :], start=(k == 0), stop=False)
                                mm(dst, w_high[:, k, fs], xT_low[:, k, :], start=False, stop=False)
                                last = mm(dst, w_low[:, k, fs], xT_high[:, k, :], start=False, stop=(k == KD - 1))
                        tell(last, u)
                        continue
                    if half == 0:
                        pe.wait_ge(sem("mlp_hidden"), 2 * MLP_STEPS * layer + 2 * (j + 1))
                    for tile in range(NT):
                        u = U[f"mlp{layer}.out"][4 * j + 2 * half + tile]
                        claim(u)
                        dst = banks[u.bank][:, :]
                        for f in range(4):
                            h_high, h_low = (mlp_hidden[j % 2][:, a, f, tile * P:(tile + 1) * P] for a in range(2))
                            mm(dst, h_high, w_high[:, f, :], start=(f == 0), stop=False)
                            mm(dst, h_high, w_low[:, f, :], start=False, stop=False)
                            last = mm(dst, h_low, w_high[:, f, :], start=False, stop=(f == 3))
                        tell(last, u)

            pe.wait_ge(normed, 6)
            turn("turn.n2_0", u3)
            turned("turn.n2_0")
            mlp(0)

            pe.wait_ge(sem("c_wide_ready"), 2)
            for i in range(2):
                c_product(U["mod1.pre1"][i], K["mod1.pre1"][i], 0)
            for i in range(2, 4):
                sum_up(U["mod1.pre1"][i], "mod1.pre1", i - 2)
            pe.wait_ge(normed, 7)
            turn("turn.n1_1", u3)
            turned("turn.n1_1")
            pe.wait_ge(sem("filter_loaded"), 64)
            for i, u in enumerate(U["filter_mlp"]):
                claim(u)
                if i == 0:
                    last = mm(banks[u.bank][0:64, 0:S], small[0:17, 256:320], small[0:17, 0:256], start=True, stop=True)
                else:
                    pe.wait_ge(sem("filter_h"), i)
                    last = mm(banks[u.bank][0:64, 0:S], small[0:64, 256 + 64 * i:320 + 64 * i], f_h[0:64, :],
                              start=True, stop=True)
                tell(last, u)
            pe.wait_ge(sem("filter_h"), 3)
            idx = K["filter_w4"][0]
            slab_in(idx)
            pe.wait_ge(sem("dft_loaded"), 16)
            for n in range(2):
                for j, u in enumerate(U[f"filter{n}"]):
                    direction, tile, half = j // 4, j // 2 % 2, j % 2
                    claim(u)
                    c0 = direction * 2048 + n * D + half * 512
                    tell(mm(banks[u.bank][:, :], f_h[0:64, tile * P:(tile + 1) * P], slab_ap(idx)[0:64, c0:c0 + 512],
                            start=True, stop=True), u)
                for half, u in enumerate(U[f"filter_norm{n}"]):
                    claim(u)
                    pe.wait_ge(sem("filter_squares"), 2 * n + half + 1)
                    for i in range(4):
                        last = mm(banks[u.bank][:, :], ones, f_sum[:, i * 512:(i + 1) * 512], start=(i == 0), stop=(i == 3))
                    tell(last, u)
                for j, u in enumerate(U[f"filter_dft{n}"]):
                    kind, ft, half = j // 4, j // 2 % 2, j % 2
                    claim(u)
                    pe.wait_ge(sem("filter_sums"), 2 * n + kind + 1)
                    table, src = ((cosT, f_sum), (sinT, f_diff))[kind]
                    for k in range(NT):
                        last = mm(banks[u.bank][:, :], table[:, k, ft * P:(ft + 1) * P],
                                  src[:, k * D + half * 512:k * D + (half + 1) * 512], start=(k == 0), stop=(k == 1))
                    tell(last, u)
            for i in range(7):
                if i < 6:
                    idx = K["hyena_in"][i]
                    slab_in(idx)
                    project_cols(U["hyena_in"][2 * i:2 * i + 2], idx, xT3)
                if i == 0:
                    continue
                pe.wait_ge(sem("conv_ready"), i)
                for tile in range(NT):
                    u = U["hyena_turn"][2 * (i - 1) + tile]
                    claim(u)
                    for c in range(4):
                        last = nc.tensor.transpose(banks[u.bank][:, c * P:(c + 1) * P],
                                                   conv[:, c * S + tile * P:c * S + (tile + 1) * P], ident)
                    tell(last, u)
            for u in U["hyena_turn"]:
                drained(pe, u)
            for n in range(2):
                if n == 1:
                    pe.wait_ge(sem("hyena_y"), 4)
                for j, u in enumerate(U[f"dft{n}"]):
                    ft, half, kind = j // 4, j // 2 % 2, j % 2
                    claim(u)
                    table = (cosT, sinT)[kind]
                    for k in range(NT):
                        last = mm(banks[u.bank][:, :], table[:, k, ft * P:(ft + 1) * P],
                                  hy_x[2][:, k * D + half * 512:k * D + (half + 1) * 512], start=(k == 0), stop=(k == 1))
                    tell(last, u)
                pe.wait_ge(sem("spectrum_ready"), 4 * (n + 1))
                for j, u in enumerate(U[f"idft{n}"]):
                    tile, half = j // 2, j % 2
                    claim(u)
                    for i, (table, src) in enumerate(((icos, y_re), (isin, y_im))):
                        for k in range(NT):
                            last = mm(banks[u.bank][:, :], table[:, k, tile * P:(tile + 1) * P],
                                      src[:, k * D + half * 512:k * D + (half + 1) * 512],
                                      start=(i == 0 and k == 0), stop=(i == 1 and k == 1))
                    tell(last, u)
            pe.wait_ge(sem("hyena_y"), 8)
            turn("turn.hyena_out", hy_x[2].rearrange("p (t d) -> p t d", t=NT))
            turned("turn.hyena_out")
            for i, idx in enumerate(K["hyena_out"]):
                slab_in(idx)
                project(U["hyena_out"][2 * i:2 * i + 2], idx, 512, tokens)
                if i == 0:
                    for k in range(2):
                        sum_up(U["mod1.gate1"][k], "mod1.gate1", k)
            for k in range(4):
                sum_up(U["mod1.pre2"][k], "mod1.pre2", k)
            pe.wait_ge(normed, 8)
            turn("turn.n2_1", u3)
            turned("turn.n2_1")
            mlp(1)

        @block.scalar
        def _(act):
            act_fn = nc.scalar.activation
            calls = [0]
            steps = [0]

            def link(ins):
                steps[0] += 1
                ins.then_inc(act_step, 1)
                act.wait_ge(act_step, steps[0])

            def root(n, groups, src=None):
                calls[0] += 1
                act.wait_ge(stats_ready, calls[0])
                act_fn(s_std[:, 0:groups], s_sum[:, 0:groups], ACT.Sqrt, bias=eps_col, scale=1.0 / n)\
                    .then_inc(std_ready, 1)

            def copy_out(u, dst, src, func=ACT.Copy):
                full(act, u)
                act_fn(dst, src, func).then_inc(bank_drained[u.bank], 1)

            def turn(name, dst):
                for j in (1, 3):
                    u = U[name][j]
                    copy_out(u, dst[:, 4:8, (j // 2) * P:(j // 2 + 1) * P],
                             banks[u.bank][:, :].rearrange("p (k s) -> p k s", k=4))

            def turn_high(name, layer):
                for j, u in enumerate(U[name]):
                    full(act, u)
                    act_fn(xT_high[:, 4 * (j % 2):4 * (j % 2) + 4, (j // 2) * P:(j // 2 + 1) * P],
                           banks[u.bank][:, :].rearrange("p (k s) -> p k s", k=4), ACT.Copy)\
                        .then_inc(sem("turned_high"), 1)

            def mlp(layer):
                def make_high(n):
                    idx, loaded, _, w_high = mlp_part(layer, n)
                    act.wait_ge(slab_loaded[idx % RING], 16 * (idx // RING + 1))
                    act_fn(w_high, loaded, ACT.Copy).then_inc(sem("mlp_high"), 1)

                for n in range(4):
                    make_high(n)
                for n, (w, j, half) in enumerate(MLP_PARTS):
                    u = mlp_unit(layer, n)
                    full(act, u)
                    if w == 0:
                        if j > 0:
                            act.wait_ge(sem("mlp_hidden"), 2 * MLP_STEPS * layer + 2 * (j - 1) + half + 1)
                        act_fn(squares[half], banks[u.bank][:, :], ACT.Relu).then_inc(bank_drained[u.bank], 1)
                    if n + 4 < len(MLP_PARTS):
                        make_high(n + 4)

            def copies(name, dst, p=P):
                for j, u in enumerate(U[name]):
                    copy_out(u, dst[0:p, j * 512:(j + 1) * 512], banks[u.bank][0:p, :])

            act.wait_ge(sem("eps_ready"), 1)
            root(D, NT)
            turn("turn.mix0", xT3)
            act.wait_ge(sem("lb_diff"), 1)
            act_fn(lb_col, s_inv[:, 0:4], ACT.Sigmoid).then_inc(sem("lb_ready"), 1)
            for j, u in enumerate(U["hgrn_f"]):
                copy_out(u, hg_f[:, j * 512:(j + 1) * 512], banks[u.bank][:, :], ACT.Sigmoid)
            for j, u in enumerate(U["hgrn_q"]):
                copy_out(u, hg_q[:, j * 512:(j + 1) * 512], banks[u.bank][:, :], ACT.Silu)
            for j, u in enumerate(U["hgrn_i"]):
                copy_out(u, hg_i[:, j, :], banks[u.bank][:, :])
            for j, u in enumerate(U["fox_v"]):
                copy_out(u, fx_v[:, j, :], banks[u.bank][:, :])
            for j, u in enumerate(U["hgrn_g"]):
                copy_out(u, hg_g[:, j * 512:(j + 1) * 512], banks[u.bank][:, :], ACT.Silu)
            act.wait_ge(sem("hgrn_forget"), 1)
            act_fn(hg_qh, hg_f, ACT.Ln).then_inc(sem("hgrn_logf"), 1)
            act.wait_ge(sem("fox_absf"), 1)
            link(act_fn(small[:, 464:480], small[:, 464:480], ACT.Exp))
            act_fn(small[:, 464:480], small[:, 464:480], ACT.Ln, bias=1.0).then_inc(sem("fox_softplus"), 1)
            for n in range(6):
                act.wait_ge(sem("hgrn_exponents"), n + 1)
                src, dst = at(0, 1024), at(1024, 1024)
                if n == len(HGRN_LEVELS):
                    act_fn(hg_kh, src, ACT.Exp, scale=-1.0).then_inc(sem("hgrn_exps"), 1)
                    act_fn(dst, src, ACT.Exp).then_inc(sem("hgrn_exps"), 1)
                else:
                    act_fn(dst, src, ACT.Exp).then_inc(sem("hgrn_exps"), 1)
            root(64, 16)
            root(64, 16)
            root(64, 16)
            copies("fox_qT", fx_qT, 66)
            copies("fox_kT", fx_kT, 66)
            SEG = [(0, P), (P, 2 * P)]

            def masked_attend(name, maps, L, pT, done):
                for s in range(9):
                    if s < 8:
                        for m in range(maps):
                            act.wait_ge(sem(name + "_max"), s * maps + m + 1)
                            if s >= 2 and m == 0:
                                full(act, U[name + ".turn"][s - 2])
                            P_m = att_P[:, (s % 2) * 1024 + m * 384:(s % 2) * 1024 + (m + 1) * 384]
                            L_m = L[:, (s % 2) * 768 + m * 384:(s % 2) * 768 + (m + 1) * 384]
                            for g, (c0, n) in enumerate(SEG):
                                ins = act_fn(P_m[:, c0:c0 + n], L_m[:, c0:c0 + n], ACT.Exp,
                                             bias=neg_max[:, s % 2, m, g:g + 1],
                                             accum_out=exp_sum[:, s % 4, m, g:g + 1])
                                ins.then_inc(sem(done), 1)
                    if s >= 1:
                        u = U[name + ".turn"][s - 1]
                        if s >= 3:
                            full(act, U[name + ".out"][s - 3])
                        T = pT[:, ((s - 1) % 2) * 512:((s - 1) % 2) * 512 + 384]
                        copy_out(u, T, banks[u.bank][:, 0:384])

            def full_attend(name):
                for s in range(17):
                    if s < 16:
                        u = U[name + ".logits"][s]
                        act.wait_ge(sem(name + "_max"), s + 1)
                        if s >= 2:
                            full(act, U[name + ".turn"][s - 2])
                        act_fn(b2_P[:, (s % 2) * 512:(s % 2 + 1) * 512], banks[u.bank][:, :], ACT.Exp,
                               bias=neg_max[:, s % 2, 0, 0:1],
                               accum_out=exp_sum[:, s % 4, 0, 0:1]).then_inc(bank_drained[u.bank], 1)
                    if s >= 1:
                        u = U[name + ".turn"][s - 1]
                        if s >= 3:
                            full(act, U[name + ".out"][s - 3])
                        copy_out(u, b2_T[:, ((s - 1) % 2) * 512:((s - 1) % 2 + 1) * 512], banks[u.bank][:, :])

            masked_attend("fox", 1, fx_L, fx_T, "fox_exp")
            turn("turn.even_out", xT3)

            def moe(layer):
                name = f"moe{layer}"
                root(D, NT)
                turn(f"turn.ffn{layer}", xT3)
                act.wait_ge(sem("routed"), layer + 1)
                act_fn(route[:, 64:64 + 2 * 8], route[:, 64:64 + 2 * 8], ACT.Exp).then_inc(sem("route_exp_out"), 1)
                with short_path(act, layer):
                    moe_short(layer)
                with act.Else():
                    moe_dense(layer)

            def moe_short(layer):
                def out_of(name, r, dst, src, func=ACT.Copy, done=None):
                    u = filling(layer, name, r)
                    act.wait_ge(bank_full[u.bank], u.before + 1)
                    act_fn(dst, src(banks[u.bank]), func).then_inc(done or bank_drained[u.bank], 1)

                def make_high(name, r, half):
                    n, hi = weight_part(name, r, half)
                    if half == 0:
                        pair = r - 1 if name == "down1" else r
                        idx = K[f"moe{layer}"][0] + SLAB_OF[name]
                        act.wait_ge(slab_loaded[idx % RING], pair * 16 + 16 * (idx // RING + 1))
                    act_fn(hi, weight_half(layer, name, half), ACT.Copy).then_inc(sem(f"high{layer}"), 1)

                def refill(name, r, half, first, last):
                    follower = next_weights(name, r, first, last)
                    if follower is None:
                        return
                    if name.startswith("down"):
                        u = filling(layer, f"{name}.{half}", r)
                        act.wait_ge(bank_full[u.bank], u.before + 1)
                    elif half == 0:
                        order = ("gate0", "up0", "gate1", "up1").index(name)
                        act.wait_ge(sem(f"half_used{layer}"), r * 4 + (order + 1))
                    else:
                        u = filling(layer, name, r)
                        act.wait_ge(bank_full[u.bank], u.before + 1)
                    make_high(*follower, half)

                def into(name, w, r, first, last):
                    refill(name, r, 0, first, last)
                    out_of(name, r, raw[:, w, :], lambda ps: ps[:, :])
                    refill(name, r, 1, first, last)

                def down(e, r, first, last):
                    for half in range(2):
                        out_of(f"down{e}.{half}", r, pair_y[e][:, half * 512:(half + 1) * 512], lambda ps: ps[:, :])
                        if not (isinstance(r, int) and r == PAIRS):
                            refill(f"down{e}", r, half, first, last)

                def silu(e, r):
                    out_of(f"fold{e}", r, pair_silu, lambda ps: ps[:, 0:4 * SEATS], ACT.Silu, sem(f"silu{layer}"))

                def gather(r):
                    for j in range(2):
                        out_of(f"gather{j}", r, seated2[:, 4 * j:4 * j + 4, :, 0],
                               lambda ps: ps[:, :].rearrange("p (k e c) -> p k e c", k=4, e=2),
                               done=sem(f"seated_high{layer}"))

                def turn_weights(r):
                    out_of("turn", r, weightedT, lambda ps: ps[:, :])

                def round_(r, first=False, last=False):
                    into("gate0", 0, r, first, last)
                    into("up0", 1, r, first, last)
                    if not first:
                        down(1, r, first, last)
                    silu(0, r)
                    if not first:
                        turn_weights(r)
                    into("gate1", 0, r, first, last)
                    into("up1", 1, r, first, last)
                    down(0, r, first, last)
                    if not last:
                        gather(r)
                    silu(1, r)

                for name in ("gate0", "up0"):
                    for half in range(2):
                        make_high(name, 0, half)
                gather(-1)
                round_(0, first=True)
                round_(1)
                with act.Fori(2, PAIRS - 1) as r:
                    round_(r)
                round_(PAIRS - 1, last=True)
                down(1, PAIRS, False, True)
                turn_weights(PAIRS)

            def moe_dense(layer):
                name = f"moe{layer}"
                with act.Fori(0, PAIRS) as i:
                    for e in range(2):
                        for j in range(2):
                            u = later(U[name + ".gate"][2 * e + j], i)
                            up = later(U[name + ".up"][2 * e + j], i)
                            act.wait_ge(bank_drained[up.bank], up.before)
                            act.wait_ge(bank_full[u.bank], u.before + 1)
                            act_fn(silu_g[:, j * 512:(j + 1) * 512], banks[u.bank][:, :], ACT.Silu)\
                                .then_inc(bank_drained[u.bank], 1)
                    u = later(U[name + ".even"][0], i)
                    act.wait_ge(bank_full[u.bank], u.before + 1)
                    act_fn(stat[:, 174:175], banks[u.bank][:, 0:1], ACT.Copy).then_inc(bank_drained[u.bank], 1)

            moe(0)
            root(D, NT)
            turn("turn.mix1", xT3)
            act.wait_ge(sem("angles_ready"), 1)
            act_fn(od_tab[:, 0:128], od_tab[:, 0:128], ACT.Sin).then_inc(sem("rope_ready"), 1)
            act.wait_ge(sem("lam_sums"), 1)
            act_fn(small[:, 480:482], small[:, 480:482], ACT.Exp).then_inc(sem("lam_exps"), 1)
            for j, u in enumerate(U["odd_in"]):
                dst = (od_q.rearrange("p (t d) -> p t d", t=NT), od_k.rearrange("p (t d) -> p t d", t=NT), od_v)[j // 4]
                copy_out(u, dst[:, j % 2, (j // 2 % 2) * 512:(j // 2 % 2 + 1) * 512], banks[u.bank][:, :])
                if j in (3, 7):
                    root(64, 32)
            copies("diff_qT", od_qT, 64)
            copies("diff_kT", od_kT, 64)
            masked_attend("diff", 2, od_L, od_T, "diff_exp")
            root(P, 16)
            turn("turn.odd_out", xT3)
            moe(1)
            act.wait_ge(sem("c_copied"), 1)
            act_fn(small[:, 464:480], small[:, 464:480], ACT.Silu).then_inc(sem("c_silu"), 1)
            root(D, NT)
            turn("turn.n1_0", ctxT)
            root(D, NT)
            turn("turn.ctx", xT3)
            for j, u in enumerate(U["mla_cq"]):
                copy_out(u, z_cq[:, j * 384:(j + 1) * 384], banks[u.bank][:, 0:384])
            for j, u in enumerate(U["mla_ckv"]):
                full(act, u)
                link(act_fn(z_kr[:, j * 32:(j + 1) * 32], banks[u.bank][:, 256:288], ACT.Copy))
                act_fn(c_kv[:, j, :], banks[u.bank][:, 0:256], ACT.Copy).then_inc(bank_drained[u.bank], 1)
            for j, u in enumerate(U["gqa_q"]):
                copy_out(u, z_gq[:, j * 512:(j + 1) * 512], banks[u.bank][:, :])
            for j, u in enumerate(U["gqa_kv"]):
                full(act, u)
                link(act_fn(z_gk[:, j * P:(j + 1) * P], banks[u.bank][:, 0:P], ACT.Copy))
                act_fn(z_gv[:, j, :], banks[u.bank][:, P:2 * P], ACT.Copy).then_inc(bank_drained[u.bank], 1)
            root(384, 2)
            root(256, 4)
            for t, u in enumerate(U["turn.cq"]):
                copy_out(u, cqT[:, :, t * P:(t + 1) * P], banks[u.bank][:, 0:384].rearrange("p (k s) -> p k s", k=3))
            for k, u in enumerate(U["turn.ckv"]):
                copy_out(u, ckvT[:, k, :], banks[u.bank][:, :])
            root(64, 16)
            root(64, 8)
            for j, u in enumerate(U["mla_q"]):
                half, t = j // 2, j % 2
                c0 = t * 768 + half * 384
                copy_out(u, ml_q[:, c0:c0 + 384], banks[u.bank][:, 0:384])
            ml_k4 = ml_k.rearrange("p (t h d) -> p t h d", t=4, h=8)
            for j, u in enumerate(U["mla_kv"]):
                half, t = j // 4, j % 4
                src = banks[u.bank][:, :].rearrange("p (h d) -> p h d", h=4)
                full(act, u)
                link(act_fn(ml_k4[:, t, 4 * half:4 * half + 4, 0:64], src[:, :, 0:64], ACT.Copy))
                act_fn(ml_v[:, t, 4 * half:4 * half + 4, :], src[:, :, 64:P], ACT.Copy)\
                    .then_inc(bank_drained[u.bank], 1)
            copies("mla_qT", qT2, 96)
            copies("mla_kT", kT2, 96)
            full_attend("mla")
            copies("gqa_qT", qT2, 64)
            copies("gqa_kT", kT2, 64)
            full_attend("gqa")
            turn("turn.a_out", xT3)
            root(D, NT)
            turn_high("turn.n2_0", 0)
            mlp(0)
            root(D, NT)
            turn("turn.n1_1", xT3)
            for i in range(3):
                act.wait_ge(sem("filter_angle"), i + 1)
                act_fn(f_h[0:64, :], at(10240, 256)[0:64, :], ACT.Sin).then_inc(sem("filter_h"), 1)
            for n in range(2):
                for half, u in enumerate(U[f"filter_norm{n}"]):
                    full(act, u)
                    if n:
                        act.wait_ge(sem("filter_sums"), 2)
                    act_fn(f_norm[:, half * 512:(half + 1) * 512], banks[u.bank][:, :], ACT.Sqrt, bias=eps_col)\
                        .then_inc(bank_drained[u.bank], 1)
                for j, u in enumerate(U[f"filter_dft{n}"]):
                    c0 = n * 4096 + j * 512
                    copy_out(u, spectra[:, c0:c0 + 512], banks[u.bank][:, :])
            for i in range(7):
                for j in range(2 if i < 6 else 0):
                    u = U["hyena_in"][2 * i + j]
                    z4 = z_pad[:, (i % 2) * 1032:(i % 2 + 1) * 1032].rearrange("p (c s) -> p c s", c=4)
                    if i < 2:
                        act.wait_ge(sem("pad_ready"), 1)
                    else:
                        act.wait_ge(sem("conv_ready"), i - 1)
                    copy_out(u, z4[:, 2 * j:2 * j + 2, 1:S + 1],
                             banks[u.bank][:, :].rearrange("p (c s) -> p c s", c=2))
                for tile in range(NT if i > 0 else 0):
                    u = U["hyena_turn"][2 * (i - 1) + tile]
                    c0 = tile * D + ((i - 1) % 2) * 512
                    copy_out(u, hy_x[(i - 1) // 2][:, c0:c0 + 512], banks[u.bank][:, :])
            turn("turn.hyena_out", xT3)
            root(D, NT)
            turn_high("turn.n2_1", 1)
            mlp(1)
            root(D, NT)

        @block.vector
        def _(dve):
            v = nc.vector
            steps = [0]
            calls = [0]
            norms = [0]
            rows_used = [0]

            def link(ins):
                steps[0] += 1
                ins.then_inc(vec_step, 1)
                dve.wait_ge(vec_step, steps[0])

            def drain(ins, u):
                ins.then_inc(bank_drained[u.bank], 1)
                dve.wait_ge(bank_drained[u.bank], u.before + 1)

            def tell(ins, name, count=None):
                told[name] = told.get(name, 0) + 1
                ins.then_inc(sem(name), 1)
                dve.wait_ge(sem(name), told[name])

            told = {}

            def inverse_rms(squares, groups):
                link(v.tensor_reduce(s_sum[:, 0:groups], squares, AX_X, ALU.add))
                calls[0] += 1
                v.tensor_copy(s_sum[:, 0:1], s_sum[:, 0:1]).then_inc(stats_ready, 1)
                dve.wait_ge(std_ready, calls[0])
                link(v.reciprocal(s_inv[:, 0:groups], s_std[:, 0:groups]))

            def group_norm(x, groups, n, squares, gain_ap, outs=None):
                x3 = x.rearrange("p (g n) -> p g n", g=groups)
                sq3 = squares.rearrange("p (g n) -> p g n", g=groups)
                link(v.tensor_tensor(sq3, x3, x3, ALU.mult))
                inverse_rms(sq3, groups)
                link(v.tensor_tensor(sq3, x3, over(s_inv[:, 0:groups], [P, groups, n], 2), ALU.mult))
                dst = x3 if outs is None else outs
                return v.tensor_tensor(dst, sq3 if len(dst.shape) == 3 else sq3.rearrange("p (a g) n -> p a g n", a=2),
                                       over(gain_ap, [P, groups, n], 1) if len(dst.shape) == 3 else
                                       gain_ap.unsqueeze(1).unsqueeze(1).to_broadcast([P, 2, groups // 2, n]), ALU.mult)

            def gain_row():
                n = rows_used[0]
                rows_used[0] += 1
                if n == 0:
                    dma_done(dve, "first_gain_loaded")
                else:
                    dve.wait_ge(gain_loaded[n % 2], 16 * ((n + 1) // 2))
                return gain[:, (n % 2) * D:(n % 2 + 1) * D]

            def norm(src, dst, g):
                s3 = src.rearrange("p (t d) -> p t d", t=NT)
                d3 = dst.rearrange("p (t d) -> p t d", t=NT)
                link(v.tensor_tensor(d3, s3, s3, ALU.mult))
                inverse_rms(d3, NT)
                for t in range(NT):
                    ins = v.scalar_tensor_tensor(d3[:, t], s3[:, t], s_inv[:, t:t + 1], g, ALU.mult, ALU.mult)
                    if t == 0:
                        link(ins)
                return ins

            def norm_input():
                g = gain_row()
                link(norm(h[:, :], u_buf, g))
                v.tensor_copy(stat[:, 160:161], g[:, 0:1]).then_inc(sem("gain_used"), 1)
                v.tensor_copy(stat[:, 161:162], u_buf[:, 0:1]).then_inc(normed, 1)

            def modulated(src, dst, g, sc, sh):
                d3 = dst.rearrange("p (t d) -> p t d", t=NT)
                link(v.scalar_tensor_tensor(sc, sc, 1.0, g, ALU.add, ALU.mult))
                link(norm(src, dst, sc))
                return v.tensor_tensor(d3, d3, over(sh, [P, NT, D], 1), ALU.add)

            def modulated_input():
                g = gain_row()
                link(modulated(h[:, :], u_buf, g, scale, shift))
                v.tensor_copy(stat[:, 160:161], g[:, 0:1]).then_inc(sem("gain_used"), 1)
                v.tensor_copy(stat[:, 161:162], u_buf[:, 0:1]).then_inc(normed, 1)

            def turn(name, dst):
                for j in (0, 2):
                    u = U[name][j]
                    full(dve, u)
                    drain(v.tensor_copy(dst[:, 0:4, (j // 2) * P:(j // 2 + 1) * P],
                                        banks[u.bank][:, :].rearrange("p (k s) -> p k s", k=4)), u)

            def turn_low(name, layer):
                for j, u in enumerate(U[name]):
                    dve.wait_ge(sem("turned_high"), 4 * layer + j + 1)
                    c = (slice(None), slice(4 * (j % 2), 4 * (j % 2) + 4), slice((j // 2) * P, (j // 2 + 1) * P))
                    drain(v.tensor_tensor(xT_low[c], banks[u.bank][:, :].rearrange("p (k s) -> p k s", k=4),
                                          xT_high[c].bitcast(F32), ALU.subtract), u)

            def add_to_h(name):
                for j, u in enumerate(U[name]):
                    full(dve, u)
                    dst = h3[:, j % 2, (j // 2) * 512:(j // 2 + 1) * 512]
                    drain(v.tensor_tensor(dst, dst, banks[u.bank][:, :], ALU.add), u)

            def add_gated(name, g):
                for j, u in enumerate(U[name]):
                    full(dve, u)
                    half = slice((j // 2) * 512, (j // 2 + 1) * 512)
                    tmp = scratch[:, 0:512]
                    drain(v.tensor_tensor(tmp, banks[u.bank][:, :], g[:, half], ALU.mult), u)
                    dst = h3[:, j % 2, half]
                    link(v.tensor_tensor(dst, dst, tmp, ALU.add))

            def add_bias(name, dsts, bias, loads):
                dma_done(dve, bias, loads)
                per = len(U[name]) // len(K[name])
                for j, u in enumerate(U[name]):
                    i, c = j // per, j % per
                    dst = dsts[2 * c + i // 2][:, (i % 2) * 512:(i % 2 + 1) * 512]
                    full(dve, u)
                    drain(v.tensor_tensor(dst, dst, banks[u.bank][:, :], ALU.add), u)

            def widen_c():
                tell(v.tensor_copy(c_wide.rearrange("p (k n) -> p k n", k=16),
                                   over(small[:, 464:480], [P, 16, P], 2)), "c_wide_ready")

            def multiply_c(name, i, buffer, tiles=(0, KD)):
                idx = K[name][i]
                dve.wait_ge(slab_loaded[idx % RING], 16 * (idx // RING + 1))
                w, dst = view_k(slab_ap(idx), KD, 512), partial[name][buffer]
                for k in range(*tiles):
                    c = silu_c[:, k:k + 1]
                    if k == 0:
                        link(v.tensor_scalar(dst, w[:, k], c, None, ALU.mult))
                    elif k < KD - 1:
                        link(v.scalar_tensor_tensor(dst, w[:, k], c, dst, ALU.mult, ALU.add))
                    else:
                        tell(v.scalar_tensor_tensor(dst, w[:, k], c, dst, ALU.mult, ALU.add), name + ".partial")

            def rotate(x, groups, axes, nf, cos, sin, tmp):
                shape = [P, groups, axes, nf] if axes > 1 else [P, groups, nf]

                def half(a):
                    return x[:, :, :, a, :] if axes > 1 else x[:, :, a, :]

                def table(c):
                    return c.unsqueeze(1).to_broadcast(shape)

                n = groups * axes * nf
                pat = "p (g a n) -> p g a n" if axes > 1 else "p (g n) -> p g n"
                t = [tmp[:, i * n:(i + 1) * n].rearrange(pat, **({"g": groups, "a": axes} if axes > 1 else {"g": groups}))
                     for i in range(4)]
                link(v.tensor_tensor(t[0], half(0), table(cos), ALU.mult))
                link(v.tensor_tensor(t[1], half(1), table(sin), ALU.mult))
                link(v.tensor_tensor(t[2], half(0), table(sin), ALU.mult))
                link(v.tensor_tensor(t[3], half(1), table(cos), ALU.mult))
                link(v.tensor_tensor(half(0), t[0], t[1], ALU.subtract))
                link(v.tensor_tensor(half(1), t[2], t[3], ALU.add))

            def wrap_angle(x, turns, shift_turns=0.0, p=P):
                link(v.tensor_scalar(turns, x, 1.0 / (2 * np.pi), shift_turns, ALU.mult, ALU.add))
                link(v.tensor_scalar(turns, turns, ROUNDER, None, ALU.add))
                link(v.tensor_scalar(turns, turns, ROUNDER, None, ALU.subtract))
                link(v.scalar_tensor_tensor(x, turns, -TWO_PI_HI, x, ALU.mult, ALU.add))
                link(v.scalar_tensor_tensor(x, turns, -TWO_PI_LO, x, ALU.mult, ALU.add))
                link(v.tensor_scalar(x, x, 2 * np.pi * shift_turns, 3.1415925, ALU.add, ALU.min))
                link(v.tensor_scalar(x, x, -3.1415925, None, ALU.max))

            def masked_attend(name, maps, mask, L, dv, o, done, combine=None):
                for s in range(10):
                    if s < 8:
                        for m in range(maps):
                            u = U[name + ".logits"][s * maps + m]
                            full(dve, u)
                            if s >= 2:
                                dve.wait_ge(sem(done), (s - 2) * maps * 2 + 2 * m + 2)
                            L_m = L[:, (s % 2) * 768 + m * 384:(s % 2) * 768 + (m + 1) * 384]
                            drain(v.tensor_tensor(L_m, banks[u.bank][:, 0:384], mask, ALU.add), u)
                            for g, (c0, n) in enumerate(((0, P), (P, 2 * P))):
                                ins = v.tensor_reduce(neg_max[:, s % 2, m, g:g + 1], L_m[:, c0:c0 + n], AX_X, ALU.max,
                                                      negate=True)
                                if g == 0:
                                    link(ins)
                            tell(ins, name + "_max")
                    if combine and 1 <= s <= 8:
                        combine(s - 1)
                    if s >= 2:
                        a = s - 2
                        u = U[name + ".out"][a]
                        full(dve, u)
                        if not combine:
                            dve.wait_ge(sem(done), a * maps * 2 + 2)
                            link(v.reciprocal(exp_inv[:, a % 4, 0, :], exp_sum[:, a % 4, 0, :]))
                        for t in range(NT):
                            dst = o[:, t, a * dv:(a + 1) * dv]
                            src = banks[u.bank][:, t * dv:(t + 1) * dv]
                            if combine:
                                ins = v.tensor_copy(dst, src)
                            else:
                                ins = v.tensor_scalar(dst, src, exp_inv[:, a % 4, 0, t:t + 1], None, ALU.mult)
                            if t == 0:
                                link(ins)
                        drain(ins, u)
                        if not combine:
                            v.tensor_copy(stat[:, 162:163], stat[:, 163:164]).then_inc(sem(name + "_o"), 1)

            def full_attend(name, o):
                for s in range(18):
                    if s < 16:
                        u = U[name + ".logits"][s]
                        full(dve, u)
                        if s >= 2:
                            before = U[name + ".logits"][s - 2]
                            drained(dve, before)
                        tell(v.tensor_reduce(neg_max[:, s % 2, 0, 0:1], banks[u.bank][:, :], AX_X, ALU.max,
                                             negate=True), name + "_max")
                    if s >= 2:
                        a = s - 2
                        u = U[name + ".out"][a]
                        full(dve, u)
                        drained(dve, U[name + ".logits"][a])
                        link(v.reciprocal(exp_inv[:, a % 4, 0, 0:1], exp_sum[:, a % 4, 0, 0:1]))
                        hh, t = a // 2, a % 2
                        drain(v.tensor_scalar(o[:, t, hh * 64:(hh + 1) * 64], banks[u.bank][:, 0:64],
                                              exp_inv[:, a % 4, 0, 0:1], None, ALU.mult), u)
                        v.tensor_copy(stat[:, 162:163], stat[:, 163:164]).then_inc(sem(name + "_o"), 1)

            link(v.memset(stat[:, :], 0.0))
            tell(v.memset(eps_col, EPS), "eps_ready")

            dma_done(dve, "x_loaded")
            norm_input()
            turn("turn.mix0", xT3)
            dma_done(dve, "cols_loaded", 2)
            tell(v.tensor_tensor(s_inv[:, 0:4], col("lb0", 0, 4), col("lb1", 0, 4), ALU.subtract), "lb_diff")
            dve.wait_ge(sem("lb_ready"), 1)
            link(v.tensor_scalar(one_less_lb, lb_col, -1.0, 1.0, ALU.mult, ALU.add))
            for u in U["hgrn_f"]:
                drained(dve, u)
            for c in range(4):
                f_c = hg_f[:, c * S:(c + 1) * S]
                link(v.tensor_scalar(f_c, f_c, one_less_lb[:, c:c + 1], lb_col[:, c:c + 1], ALU.mult, ALU.add))
            tell(v.tensor_scalar(hg_k, hg_f, -1.0, 1.0, ALU.mult, ALU.add), "hgrn_forget")
            u = U["fox_f"][0]
            full(dve, u)
            dma_done(dve, "rows_loaded")
            dma_done(dve, "resident_loaded")
            xf = route_logf
            drain(v.tensor_tensor(xf.rearrange("p (t n) -> p t n", t=NT),
                                  banks[u.bank][:, 0:16].rearrange("p (t n) -> p t n", t=NT),
                                  over(row("fox_bias"), [P, NT, 8], 1), ALU.add), u)
            link(v.tensor_scalar(small[:, 464:480], xf, -1.0, None, ALU.mult))
            tell(v.tensor_tensor(small[:, 464:480], small[:, 464:480], xf, ALU.min), "fox_absf")
            for j, u in enumerate(U["fox_q"]):
                full(dve, u)
                drain(v.tensor_copy(fx_q[:, j * 512:(j + 1) * 512], banks[u.bank][:, :]), u)
            for j, u in enumerate(U["fox_k"]):
                full(dve, u)
                drain(v.tensor_copy(fx_k[:, j * 512:(j + 1) * 512], banks[u.bank][:, :]), u)
            dve.wait_ge(sem("fox_softplus"), 1)
            link(v.tensor_scalar(xf, xf, 0.0, None, ALU.min))
            tell(v.tensor_tensor(xf, xf, small[:, 464:480], ALU.subtract), "fox_logf")
            dve.wait_ge(sem("hgrn_logf"), 1)
            for c in range(4):
                cs = slice(c * S, (c + 1) * S)
                link(v.tensor_tensor_scan(hg_cum[:, cs], ones256, hg_qh[:, cs], 0.0, ALU.mult, ALU.add))
            u = U["fox_cum"][0]
            full(dve, u)
            drain(v.tensor_copy(small[:, 480:496], banks[u.bank][:, 0:16]), u)
            link(v.memset(hg_qh, 0.0))
            link(v.memset(hg_kh, 0.0))
            for u in U["hgrn_q"]:
                drained(dve, u)
            dma_done(dve, "even_tables_loaded")
            expo, exps = at(0, 1024), at(1024, 1024)
            tmp = at(2048, 512)
            exps_done = 0
            for n, L in enumerate(list(HGRN_LEVELS) + [None, P]):
                name = f"level{L}" if L else "diagonal"
                if n:
                    prev = f"level{HGRN_LEVELS[n - 1]}" if n <= 4 else "diagonal"
                    full(dve, U[prev][-1])
                if L:
                    blocks = lambda a: a.rearrange("p (b w l) -> p b w l", w=2, l=L)
                    first, second = (lambda a: blocks(a)[:, :, 0, :]), (lambda a: blocks(a)[:, :, 1, :])
                    nb = 1024 // (2 * L)
                    ref = first(hg_cum)[:, :, L - 1:L].to_broadcast([P, nb, L])
                    link(v.tensor_tensor(second(expo), second(hg_cum), ref, ALU.subtract))
                    tell(v.tensor_tensor(first(expo), ref, first(hg_cum), ALU.subtract), "hgrn_exponents")
                    exps_done += 1
                    dve.wait_ge(sem("hgrn_exps"), exps_done)
                    link(v.tensor_tensor(second(hg_qh), second(hg_q), second(exps), ALU.mult))
                    tell(v.tensor_tensor(first(hg_kh), first(hg_k), first(exps), ALU.mult), "hgrn_factors")
                else:
                    b3 = lambda a: a.rearrange("p (b l) -> p b l", l=LAST_BLOCK)
                    mid = b3(hg_cum)[:, :, LAST_BLOCK // 2 - 1:LAST_BLOCK // 2].to_broadcast([P, 1024 // 8, 8])
                    tell(v.tensor_tensor(b3(expo), b3(hg_cum), mid, ALU.subtract), "hgrn_exponents")
                    exps_done += 2
                    dve.wait_ge(sem("hgrn_exps"), exps_done)
                    link(v.tensor_tensor(hg_qh, hg_q, exps, ALU.mult))
                    tell(v.tensor_tensor(hg_kh, hg_k, hg_kh, ALU.mult), "hgrn_factors")
                for j, u in enumerate(U[name]):
                    full(dve, u)
                    src = banks[u.bank][:, :].rearrange("p (c t) -> p c t", c=4)
                    if L == P:
                        drain(v.tensor_copy(hg_P[:, 4 + j], src), u)
                        continue
                    mask = over(level_mask[n], [P, 4, P], 1)
                    t3 = tmp.rearrange("p (c t) -> p c t", c=4)
                    dst = hg_P[:, j]
                    if n == 0:
                        drain(v.tensor_tensor(dst, src, mask, ALU.mult), u)
                    else:
                        drain(v.scalar_tensor_tensor(t3, src, 3e38, mask, ALU.min, ALU.mult), u)
                        link(v.tensor_tensor(dst, dst, t3, ALU.add))
            for u in U["hgrn_g"]:
                drained(dve, u)
            for t, u in enumerate(U["hgrn_o"]):
                full(dve, u)
                drain(v.tensor_copy(expo[:, t * 512:(t + 1) * 512], banks[u.bank][:, :]), u)
            link(group_norm(expo, 16, 64, exps, row("hgrn_out")))
            link(v.tensor_tensor(ev_o[:, :, 0:512], expo.rearrange("p (t d) -> p t d", t=NT),
                                 hg_g.rearrange("p (t d) -> p t d", t=NT), ALU.mult))
            link(v.tensor_scalar(row("fox_q"), row("fox_q"), 0.125, None, ALU.mult))
            link(group_norm(fx_q, 16, 64, exps, row("fox_q"), fq_aug[:, :, :, 0:64]))
            link(group_norm(fx_k, 16, 64, exps, row("fox_k"), fk_aug[:, :, :, 0:64]))
            cum4 = small[:, 480:496].rearrange("p (t h d) -> p t h d", t=NT, h=8)
            link(v.memset(fq_aug[:, :, :, 64:65], 1.0))
            link(v.tensor_copy(fq_aug[:, :, :, 65:66], cum4))
            link(v.tensor_scalar(fk_aug[:, :, :, 64:65], cum4, -1.0, None, ALU.mult))
            tell(v.memset(fk_aug[:, :, :, 65:66], 1.0), "fox_aug")
            masked_attend("fox", 1, causal, fx_L, 64, ev_o[:, :, 512:1024], "fox_exp")
            turn("turn.even_out", xT3)
            add_to_h("even_out")

            def moe(layer):
                name = f"moe{layer}"
                norm_input()
                turn(f"turn.ffn{layer}", xT3)
                u = U[f"router{layer}"][0]
                full(dve, u)
                lg = route[:, 256:328]
                drain(v.tensor_copy(lg, banks[u.bank][:, 0:72]), u)
                best, place = route[:, 0:8], route[:, 16:24].bitcast(U32)
                padded, picked = route[:, 32:40], route[:, 40:48]
                ex = route[:, 64:80].rearrange("p (t n) -> p t n", t=NT)
                keep = [route[:, 336 + 32 * t:368 + 32 * t] for t in range(NT)]
                both = route[:, 400:408]
                link(v.memset(padded, -1e30))
                link(v.memset(route[:, 64:80], 0.0))
                link(v.memset(comb[:, :, 32:34], 0.0))
                link(v.memset(rank[:, :, 32:34], -1.0))
                for t in range(NT):
                    g4 = lg[:, t * 36:t * 36 + 4]
                    link(v.tensor_copy(padded[:, 0:4], g4))
                    link(v.max(best, padded))
                    link(v.max_index(place, best, padded))
                    link(v.tensor_copy(route[:, 24:32], place))
                    hot = keep[t][:, 0:4]
                    link(v.tensor_scalar(hot, iota8[:, 0:4], route[:, 24:25], None, ALU.is_equal))
                    link(v.tensor_scalar(ex[:, t, 0:4], g4, best[:, 0:1], None, ALU.subtract))
                    e3 = lg[:, t * 36 + 4:t * 36 + 36].rearrange("p (g e) -> p g e", g=4)
                    link(v.tensor_scalar(picked, e3[:, 0], hot[:, 0:1], None, ALU.mult))
                    for g in range(1, 4):
                        link(v.scalar_tensor_tensor(picked, e3[:, g], hot[:, g:g + 1], picked, ALU.mult, ALU.add))
                    link(v.max(best, picked))
                    link(v.max_index(place, best, picked))
                    link(v.tensor_copy(route[:, 24:32], place))
                    link(v.tensor_tensor(ex[:, t, 4:5], best[:, 1:2], best[:, 0:1], ALU.subtract))
                    for r in range(2):
                        link(v.tensor_scalar(keep[t][:, 8 + 8 * r:16 + 8 * r], iota8, route[:, 24 + r:25 + r], None,
                                             ALU.is_equal))
                    link(v.tensor_tensor(both, keep[t][:, 8:16], keep[t][:, 16:24], ALU.add))
                    link(v.tensor_tensor(routed[:, t].rearrange("p (g e) -> p g e", g=4), over(hot, [P, 4, 8], 2),
                                         over(both, [P, 4, 8], 1), ALU.mult))
                tell(v.tensor_copy(route[:, 12:13], route[:, 0:1]), "routed")
                dve.wait_ge(sem("route_exp_out"), layer + 1)
                for t in range(NT):
                    hot = keep[t][:, 0:4]
                    link(v.tensor_reduce(route[:, 80:81], ex[:, t, 0:4], AX_X, ALU.add))
                    link(v.tensor_scalar(route[:, 81:82], ex[:, t, 4:5], 1.0, None, ALU.add))
                    link(v.reciprocal(route[:, 82:84], route[:, 80:82]))
                    link(v.tensor_tensor(route[:, 84:85], route[:, 82:83], route[:, 83:84], ALU.mult))
                    link(v.tensor_tensor(route[:, 85:86], route[:, 84:85], ex[:, t, 4:5], ALU.mult))
                    link(v.tensor_scalar(both, keep[t][:, 8:16], route[:, 84:85], None, ALU.mult))
                    link(v.scalar_tensor_tensor(both, keep[t][:, 16:24], route[:, 85:86], both, ALU.mult, ALU.add))
                    link(v.tensor_tensor(comb[:, t, 0:32].rearrange("p (g e) -> p g e", g=4), over(hot, [P, 4, 8], 2),
                                         over(both, [P, 4, 8], 1), ALU.mult))
                u = U[f"rank{layer}"][0]
                full(dve, u)
                ps = banks[u.bank]
                link(v.tensor_tensor(rank[:, :, 0:32], ps[:, 0:64].rearrange("p (t e) -> p t e", t=NT), routed, ALU.mult))
                link(v.tensor_scalar(rank[:, :, 0:32], rank[:, :, 0:32], -1.0, None, ALU.add))
                drain(v.tensor_reduce(route[:, 14:15], ps[:, 64:96], AX_X, ALU.max), u)
                tell(v.tensor_copy(most_tokens[:, layer:layer + 1], route[:, 14:15]), "counted")
                with short_path(dve, layer):
                    moe_short(layer)
                with dve.Else():
                    moe_dense(layer)
                for j in range(4):
                    drained(dve, U[name + ".down"][-4 + j])
                tell(v.tensor_copy(stat[:, 164:165], stat[:, 163:164]), "moe_done")

            def moe_short(layer):
                def take_seats(i):
                    for e in range(2):
                        for t in range(NT):
                            last = v.tensor_scalar(sel[:, t, e * SEATS:(e + 1) * SEATS], seats,
                                                   rank[:, t, bass.ds(i * 2 + e, 1)], None, ALU.is_equal)
                    last.then_inc(sem(f"seats{layer}"), 1)

                def weigh(i):
                    for e in range(2):
                        for t in range(NT):
                            r, w = (x[:, t, bass.ds(i * 2 + e, 1)] for x in (rank, comb))
                            last = v.tensor_scalar(weighted[:, t, e], over(seats, [P, 2, SEATS], 1), r, w,
                                                   ALU.is_equal, ALU.mult)
                    last.then_inc(sem(f"weights{layer}"), 1)

                def filled(name, r):
                    u = filling(layer, name, r)
                    dve.wait_ge(bank_full[u.bank], u.before + 1)
                    return u, banks[u.bank]

                def make_low(name, r):
                    for half in range(2):
                        n, hi = weight_part(name, r, half)
                        w, low = (weight_half(layer, name, half, x) for x in (False, True))
                        dve.wait_ge(sem(f"high{layer}"), n + 1)
                        v.tensor_tensor(low, w, hi.bitcast(F32), ALU.subtract)\
                            .then_inc(sem(f"low{layer}"), 1)

                def refill(name, r, first, last):
                    follower = next_weights(name, r, first, last)
                    if follower is not None:
                        make_low(*follower)

                def hide(e, r):
                    u, ps = filled(f"fold{e}", r)
                    dve.wait_ge(sem(f"silu{layer}"), r * 2 + (e + 1))
                    steps = sem(f"hide_step{layer}")
                    h4_, s4 = (x.rearrange("p (f c) -> p f c", f=4) for x in (pair_h, pair_silu))
                    v.tensor_tensor(h4_, s4, ps[:, 4 * SEATS:8 * SEATS].rearrange("p (f c) -> p f c", f=4), ALU.mult)\
                        .then_inc(bank_drained[u.bank], 1)
                    dve.wait_ge(bank_drained[u.bank], u.before + 1)
                    v.tensor_copy(hidden2[:, :, 0], h4_).then_inc(steps, 1)
                    dve.wait_ge(steps, r * 2 + (e + 1))
                    v.tensor_tensor(hidden2[:, :, 1], h4_, hidden2[:, :, 0].bitcast(F32), ALU.subtract)\
                        .then_inc(sem(f"hidden{layer}"), 1)

                def seated_low(r):
                    for j in range(2):
                        u, ps = filled(f"gather{j}", r)
                        dve.wait_ge(sem(f"seated_high{layer}"), r * 2 + (3 + j))
                        part_ = seated2[:, 4 * j:4 * j + 4]
                        v.tensor_tensor(part_[:, :, :, 1],
                                        ps[:, :].rearrange("p (k e c) -> p k e c", k=4, e=2), part_[:, :, :, 0].bitcast(F32),
                                        ALU.subtract).then_inc(bank_drained[u.bank], 1)

                def scatter(r):
                    for j in range(4):
                        u, ps = filled(f"out{j}", r)
                        dst = h3[:, j // 2, (j % 2) * 512:(j % 2 + 1) * 512]
                        v.tensor_tensor(dst, dst, ps[:, :], ALU.add).then_inc(bank_drained[u.bank], 1)

                def round_(r, first=False, last=False):
                    refill("gate0", r, first, last)
                    refill("up0", r, first, last)
                    if not first:
                        refill("down1", r, first, last)
                    hide(0, r)
                    if not first:
                        filled("turn", r)
                    weigh(r)
                    refill("gate1", r, first, last)
                    refill("up1", r, first, last)
                    if not first:
                        scatter(r)
                    if not last:
                        seated_low(r)
                        take_seats(r + 2)
                    refill("down0", r, first, last)
                    hide(1, r)

                v.tensor_tensor(fold, ident[:, 0:SEATS], ident[:, SEATS:2 * SEATS], ALU.add)
                take_seats(0)
                make_low("gate0", 0)
                make_low("up0", 0)
                seated_low(-1)
                take_seats(1)
                round_(0, first=True)
                round_(1)
                with dve.Fori(2, PAIRS - 1) as r:
                    round_(r)
                round_(PAIRS - 1, last=True)
                scatter(PAIRS)

            def moe_dense(layer):
                name = f"moe{layer}"
                with dve.Fori(0, PAIRS) as i:
                    for e in range(2):
                        for j in range(2):
                            gate_u = later(U[name + ".gate"][2 * e + j], i)
                            up_u = later(U[name + ".up"][2 * e + j], i)
                            dve.wait_ge(bank_full[up_u.bank], up_u.before + 1)
                            dve.wait_ge(bank_drained[gate_u.bank], gate_u.before + 1)
                            last_down = later(U[name + ".down"][4 * e + 3], i)
                            dve.wait_ge(bank_full[last_down.bank], last_down.before)
                            v.tensor_tensor(hidden[:, j * 512:(j + 1) * 512], silu_g[:, j * 512:(j + 1) * 512],
                                            banks[up_u.bank][:, :], ALU.mult).then_inc(bank_drained[up_u.bank], 1)
                        for j in range(4):
                            u = later(U[name + ".down"][4 * e + j], i)
                            dve.wait_ge(bank_full[u.bank], u.before + 1)
                            dve.wait_ge(bank_drained[u.bank], u.before)
                            dst = h3[:, j // 2, (j % 2) * 512:(j % 2 + 1) * 512]
                            v.scalar_tensor_tensor(dst, banks[u.bank][:, :], comb[:, j // 2, bass.ds(i * 2 + e, 1)],
                                                   dst, ALU.mult, ALU.add).then_inc(bank_drained[u.bank], 1)

            moe(0)
            norm_input()
            link(v.tensor_copy(stat[:, 170:172], pos_tile[:, :]))
            ang = od_tab[:, 0:128].rearrange("p (k t n) -> p k t n", k=2, t=NT)
            for kind in range(2):
                for t in range(NT):
                    link(v.tensor_scalar(ang[:, kind, t], row("inv_freq"), stat[:, 170 + t:171 + t], None, ALU.mult))
            wrap_angle(od_tab[:, 0:64], od_tab[:, 128:192])
            wrap_angle(od_tab[:, 64:128], od_tab[:, 128:192], 0.25)
            tell(v.tensor_copy(stat[:, 165:166], od_tab[:, 0:1]), "angles_ready")
            for i, (a, b) in enumerate((("lam_q1", "lam_k1"), ("lam_q2", "lam_k2"))):
                link(v.tensor_tensor(od_tab[:, 192:256], row(a), row(b), ALU.mult))
                link(v.tensor_reduce(small[:, 480 + i:481 + i], od_tab[:, 192:256], AX_X, ALU.add))
            tell(v.tensor_copy(stat[:, 165:166], small[:, 480:481]), "lam_sums")
            turn("turn.mix1", xT3)
            dve.wait_ge(sem("lam_exps"), 1)
            link(v.tensor_tensor(lam, small[:, 480:481], small[:, 481:482], ALU.subtract))
            link(v.tensor_scalar(neg_lam, lam, LAMBDA_INIT, -1.0, ALU.add, ALU.mult))
            dve.wait_ge(sem("rope_ready"), 1)
            link(v.tensor_scalar(row("diff_q"), row("diff_q"), 0.125, None, ALU.mult))
            link(v.tensor_scalar(row("subln"), row("subln"), 1.0 - LAMBDA_INIT, None, ALU.mult))
            for i, (x, g) in enumerate(((od_q, "diff_q"), (od_k, "diff_k"))):
                for u in U["odd_in"][4 * i:4 * i + 4]:
                    drained(dve, u)
                link(group_norm(x, 32, 64, scratch, row(g)))
                for t in range(NT):
                    x4 = x[:, t * D:(t + 1) * D].rearrange("p (g a n) -> p g a n", g=16, a=2)
                    rotate(x4, 16, 1, 32, ang[:, 1, t], ang[:, 0, t], u_buf)
                tell(v.tensor_copy(stat[:, 165:166], x[:, 0:1]), "odd_qk")
            dma_done(dve, "chunk_loaded")

            def combine(s):
                dve.wait_ge(sem("diff_exp"), 4 * s + 4)
                link(v.reciprocal(exp_inv[:, s % 4], exp_sum[:, s % 4]))
                link(v.tensor_scalar(exp_inv[:, s % 4, 1, :], exp_inv[:, s % 4, 1, :], neg_lam, None, ALU.mult))
                P0 = att_P[:, (s % 2) * 1024:(s % 2) * 1024 + 384]
                P1 = att_P[:, (s % 2) * 1024 + 384:(s % 2) * 1024 + 768]
                for g, (c0, n) in enumerate(((0, P), (P, 2 * P))):
                    link(v.tensor_scalar(P0[:, c0:c0 + n], P0[:, c0:c0 + n], exp_inv[:, s % 4, 0, g:g + 1], None,
                                         ALU.mult))
                    ins = v.scalar_tensor_tensor(P0[:, c0:c0 + n], P1[:, c0:c0 + n], exp_inv[:, s % 4, 1, g:g + 1],
                                                 P0[:, c0:c0 + n], ALU.mult, ALU.add)
                    if g == 0:
                        link(ins)
                tell(ins, "diff_probs")

            masked_attend("diff", 2, chunk_mask, od_L, P, od_o, "diff_exp", combine)
            link(group_norm(od_o_flat, 16, P, u_buf, row("subln")))
            tell(v.tensor_copy(stat[:, 165:166], od_o_flat[:, 0:1]), "diff_o")
            turn("turn.odd_out", xT3)
            add_to_h("odd_out")
            moe(1)

            tell(v.tensor_copy(small[:, 464:480], cols[:, COLS["c"][0]:COLS["c"][0] + 16]), "c_copied")
            dve.wait_ge(sem("c_silu"), 1)
            widen_c()
            for i in range(4):
                multiply_c("mod0.pre1", i, i)
            add_bias("mod0.pre1", [shift, scale, shift_c, scale_c], "bias0_pre1", 4)
            dma_done(dve, "ctx_loaded")
            g = gain_row()
            link(modulated(ctx_x, ctx_u, g, scale_c, shift_c))
            tell(v.tensor_copy(stat[:, 165:166], ctx_u[:, 0:1]), "ctx_normed")
            link(modulated(h[:, :], u_buf, g, scale, shift))
            v.tensor_copy(stat[:, 160:161], g[:, 0:1]).then_inc(sem("gain_used"), 1)
            v.tensor_copy(stat[:, 161:162], u_buf[:, 0:1]).then_inc(normed, 1)
            turn("turn.n1_0", ctxT)
            turn("turn.ctx", xT3)
            for u in U["mla_cq"]:
                drained(dve, u)
            link(group_norm(z_cq, 2, 384, at(0, 768), row("mla_q_a")))
            for u in U["mla_ckv"]:
                drained(dve, u)
            link(group_norm(z_ckv, 4, 256, at(0, 1024), row("mla_kv_a")))
            tell(v.tensor_copy(stat[:, 165:166], z_ckv[:, 0:1]), "lora_ready")
            dma_done(dve, "rope2d_loaded")

            def tables(start, nf, t):
                n = 2 * nf
                return [rope2d[:, start + (2 * kind + t) * n:start + (2 * kind + t + 1) * n]
                        .rearrange("p (a n) -> p a n", a=2) for kind in range(2)]

            for u in U["gqa_q"]:
                drained(dve, u)
            link(v.tensor_scalar(row("gqa_q"), row("gqa_q"), 0.125, None, ALU.mult))
            link(group_norm(z_gq, 16, 64, at(0, 1024), row("gqa_q")))
            for u in U["gqa_kv"]:
                drained(dve, u)
            link(group_norm(z_gk, 8, 64, at(0, 512), row("gqa_k")))
            tmp4 = at(0, 2048)
            for t in range(NT):
                cos, sin = tables(64, 16, t)
                rotate(z_gq[:, t * 512:(t + 1) * 512].rearrange("p (g a b n) -> p g a b n", g=8, a=2, b=2), 8, 2, 16,
                       cos, sin, tmp4)
                rotate(z_gk[:, t * P:(t + 1) * P].rearrange("p (g a b n) -> p g a b n", g=2, a=2, b=2), 2, 2, 16,
                       cos, sin, tmp4)
                cos, sin = tables(0, 8, t)
                rotate(z_kr[:, t * 32:(t + 1) * 32].rearrange("p (g a b n) -> p g a b n", g=1, a=2, b=2), 1, 2, 8,
                       cos, sin, tmp4)
            for u in U["mla_q"]:
                drained(dve, u)
            q4 = ml_q.rearrange("p (t h d) -> p t h d", t=NT, h=8)
            k4 = ml_k.rearrange("p (t h d) -> p t h d", t=4, h=8)
            for t in range(NT):
                cos, sin = tables(0, 8, t)
                link(v.tensor_copy(at(2048, 256).rearrange("p (g n) -> p g n", g=8), q4[:, t, :, 64:96]))
                rotate(at(2048, 256).rearrange("p (g a b n) -> p g a b n", g=8, a=2, b=2), 8, 2, 8, cos, sin, tmp4)
                link(v.tensor_copy(q4[:, t, :, 64:96], at(2048, 256).rearrange("p (g n) -> p g n", g=8)))
            link(v.tensor_scalar(ml_q, ml_q, float(96 ** -0.5), None, ALU.mult))
            for u in U["mla_kv"]:
                drained(dve, u)
            tell(v.tensor_copy(k4[:, :, :, 64:96], over(z_kr.rearrange("p (t d) -> p t d", t=4), [P, 4, 8, 32], 2)),
                 "mla_qk")
            full_attend("mla", b2_o)
            tell(v.tensor_copy(stat[:, 165:166], z_gq[:, 0:1]), "gqa_qk")
            full_attend("gqa", b2_o[:, :, 512:1024])
            turn("turn.a_out", xT3)
            for i in range(2):
                multiply_c("mod0.gate1", i, i)
            for i in range(2):
                multiply_c("mod0.pre2", i, i)
            add_bias("mod0.gate1", [gate], "bias0_gate1", 1)
            for i in range(2, 4):
                multiply_c("mod0.pre2", i, i)
            add_gated("a_out", gate)
            tell(v.tensor_copy(stat[:, 165:166], gate[:, 0:1]), "gate_used")

            def mlp(layer):
                name = f"mlp{layer}"
                def make_low(n):
                    _, loaded, w_low, w_high = mlp_part(layer, n)
                    dve.wait_ge(sem("mlp_high"), len(MLP_PARTS) * layer + n + 1)
                    v.tensor_tensor(w_low, loaded, w_high.bitcast(F32), ALU.subtract).then_inc(sem("mlp_low"), 1)

                for n in range(4):
                    make_low(n)
                for n, (w, j, half) in enumerate(MLP_PARTS):
                    if w == half == 0 and j in GATE_SUMS:
                        i = GATE_SUMS.index(j)
                        if i == 0:
                            dma_done(dve, f"bias{layer}_gate2")
                        u, cs = U[f"mod{layer}.gate2"][i], slice(i * 512, (i + 1) * 512)
                        full(dve, u)
                        drain(v.tensor_tensor(gate2[:, cs], gate2[:, cs], banks[u.bank][:, :], ALU.add), u)
                    if w == 0:
                        u = U[name + ".hidden"][2 * j + half]
                        drained(dve, u)
                        r = squares[half]
                        h_high, h_low = (mlp_hidden[j % 2][:, a, 2 * half:2 * half + 2].rearrange("p f s -> p (f s)")
                                         for a in range(2))
                        link(v.tensor_tensor(r, r, r, ALU.mult))
                        link(v.tensor_copy(h_high, r))
                        v.tensor_tensor(h_low, r, h_high.bitcast(F32), ALU.subtract).then_inc(sem("mlp_hidden"), 1)
                    else:
                        for tile in range(NT):
                            u = U[name + ".out"][4 * j + 2 * half + tile]
                            full(dve, u)
                            dst = mlp_y[:, tile, half * 512:(half + 1) * 512]
                            if j == 0:
                                drain(v.tensor_copy(dst, banks[u.bank][:, :]), u)
                            else:
                                drain(v.tensor_tensor(dst, dst, banks[u.bank][:, :], ALU.add), u)
                    if n + 4 < len(MLP_PARTS):
                        make_low(n + 4)
                    if w == 0 and half == 1:
                        for i, at_step in enumerate(GATE_SUMS):
                            if j + 2 == at_step:
                                multiply_c(f"mod{layer}.gate2", i, i, (0, KD // 2))
                            if j + 1 == at_step:
                                multiply_c(f"mod{layer}.gate2", i, i, (KD // 2, KD))
                link(v.tensor_tensor(mlp_y, mlp_y, over(gate2, [P, NT, D], 1), ALU.mult))
                link(v.tensor_tensor(h3, h3, mlp_y, ALU.add))
                tell(v.tensor_copy(stat[:, 164:165], stat[:, 163:164]), "mlp_done")

            add_bias("mod0.pre2", [shift, scale], "bias0_pre2", 2)
            modulated_input()
            turn_low("turn.n2_0", 0)
            mlp(0)

            widen_c()
            for i in range(2, 4):
                multiply_c("mod1.pre1", i, i - 2)
            add_bias("mod1.pre1", [shift, scale], "bias1_pre1", 2)
            modulated_input()
            turn("turn.n1_1", xT3)
            for i, u in enumerate(U["filter_mlp"]):
                full(dve, u)
                x, turns = at(10240, 256)[0:64, :], at(10496, 256)[0:64, :]
                drain(v.tensor_scalar(x, banks[u.bank][0:64, 0:S], col("filt_b", i, 1, 64), col("filt_freq", i, 1, 64),
                                      ALU.add, ALU.mult), u)
                wrap_angle(x, turns)
                tell(v.tensor_copy(stat[:, 165:166], stat[:, 163:164]), "filter_angle")
                dve.wait_ge(sem("filter_h"), i + 1)
            dma_done(dve, "window_loaded")
            h44 = h4.rearrange("p (a t d) -> p a t d", a=2, t=NT)
            w3 = window.rearrange("p (t d) -> p t d", t=NT)
            f3 = f_sum.rearrange("p (i d) -> p i d", i=4)
            for n in range(2):
                for j, u in enumerate(U[f"filter{n}"]):
                    direction, tile, half = j // 4, j // 2 % 2, j % 2
                    full(dve, u)
                    hs = slice(half * 512, (half + 1) * 512)
                    drain(v.tensor_tensor(h44[:, direction, tile, hs], banks[u.bank][:, :], w3[:, tile, hs], ALU.mult), u)
                h4i = h4.rearrange("p (i d) -> p i d", i=4)
                for half in range(2):
                    hs = slice(half * 512, (half + 1) * 512)
                    if half:
                        full(dve, U[f"filter_norm{n}"][0])
                    tell(v.tensor_tensor(f3, h4i[:, :, hs], h4i[:, :, hs], ALU.mult), "filter_squares")
                full(dve, U[f"filter_norm{n}"][1])
                for half, u in enumerate(U[f"filter_norm{n}"]):
                    drained(dve, u)
                link(v.reciprocal(f_norm, f_norm))
                link(v.tensor_scalar(h44[:, 1, 0], h44[:, 1, 0], col("not_first"), None, ALU.mult))
                fs3 = f_sum.rearrange("p (t d) -> p t d", t=NT)
                nrm = over(f_norm, [P, NT, D], 1)
                link(v.tensor_tensor(fs3, h44[:, 0], h44[:, 1], ALU.add))
                tell(v.tensor_tensor(fs3, fs3, nrm, ALU.mult), "filter_sums")
                link(v.tensor_tensor(h44[:, 0], h44[:, 0], h44[:, 1], ALU.subtract))
                tell(v.tensor_tensor(h44[:, 0], h44[:, 0], nrm, ALU.mult), "filter_sums")
            last_norm = U["filter_dft1"][-1]
            full(dve, last_norm)
            tell(v.memset(z_pad, 0.0), "pad_ready")
            for i in range(6):
                z4 = z_pad[:, (i % 2) * 1032:(i % 2 + 1) * 1032].rearrange("p (c s) -> p c s", c=4)
                for u in U["hyena_in"][2 * i:2 * i + 2]:
                    drained(dve, u)
                if i:
                    full(dve, U["hyena_turn"][2 * i - 1])
                for c in range(4):
                    ct = 4 * i + c
                    dst = conv[:, c * S:(c + 1) * S]
                    w = [col("conv_w", 24 * k + ct) for k in range(3)]
                    link(v.tensor_scalar(dst, z4[:, c, 0:S], w[0], col("conv_b", ct), ALU.mult, ALU.add))
                    link(v.scalar_tensor_tensor(dst, z4[:, c, 1:S + 1], w[1], dst, ALU.mult, ALU.add))
                    link(v.scalar_tensor_tensor(dst, z4[:, c, 2:S + 2], w[2], dst, ALU.mult, ALU.add))
                tell(v.tensor_copy(stat[:, 165:166], conv[:, 0:1]), "conv_ready")
            for u in U["hyena_turn"]:
                drained(dve, u)
            sp5 = spectra.rearrange("p (n k f d) -> p n k f d", n=2, k=2, f=NT)
            for n in range(2):
                skip = gain_row()
                for j in range(4):
                    ft, half = j // 2, j % 2
                    uc, us = U[f"dft{n}"][2 * j:2 * j + 2]
                    hs = slice(half * 512, (half + 1) * 512)
                    A_, B_ = sp5[:, n, 0, ft, hs], sp5[:, n, 1, ft, hs]
                    re = y_re[:, ft * D + half * 512:ft * D + (half + 1) * 512]
                    im = y_im[:, ft * D + half * 512:ft * D + (half + 1) * 512]
                    full(dve, uc)
                    full(dve, us)
                    link(v.tensor_tensor(prod[0], banks[uc.bank][:, :], A_, ALU.mult))
                    link(v.tensor_tensor(prod[1], banks[us.bank][:, :], B_, ALU.mult))
                    link(v.tensor_tensor(re, prod[0], prod[1], ALU.subtract))
                    drain(v.tensor_tensor(prod[0], banks[uc.bank][:, :], B_, ALU.mult), uc)
                    drain(v.tensor_tensor(prod[1], banks[us.bank][:, :], A_, ALU.mult), us)
                    tell(v.tensor_tensor(im, prod[0], prod[1], ALU.add), "spectrum_ready")
                for j, u in enumerate(U[f"idft{n}"]):
                    tile, half = j // 2, j % 2
                    cs = slice(tile * D + half * 512, tile * D + (half + 1) * 512)
                    y = hy_x[2][:, cs]
                    full(dve, u)
                    link(v.tensor_tensor(y, y, skip[:, half * 512:(half + 1) * 512], ALU.mult))
                    drain(v.tensor_tensor(y, y, banks[u.bank][:, :], ALU.add), u)
                    tell(v.tensor_tensor(y, y, hy_x[n][:, cs], ALU.mult), "hyena_y")
                v.tensor_copy(stat[:, 160:161], skip[:, 0:1]).then_inc(sem("gain_used"), 1)
            turn("turn.hyena_out", xT3)
            for i in range(2):
                multiply_c("mod1.gate1", i, i)
            for i in range(2):
                multiply_c("mod1.pre2", i, i)
            add_bias("mod1.gate1", [gate], "bias1_gate1", 1)
            for i in range(2, 4):
                multiply_c("mod1.pre2", i, i)
            add_gated("hyena_out", gate)
            tell(v.tensor_copy(stat[:, 165:166], gate[:, 0:1]), "gate_used")
            add_bias("mod1.pre2", [shift, scale], "bias1_pre2", 2)
            modulated_input()
            turn_low("turn.n2_1", 1)
            mlp(1)
            link(norm(h[:, :], u_buf, gain_row()))
            v.tensor_copy(stat[:, 161:162], u_buf[:, 0:1]).then_inc(sem("result_ready"), 1)


_ORDER = ["x", "ctx", "gains", "rows", "cols", "positions", "routers", "even_w_in", "even_w_out", "odd_w_in",
          "odd_w_out", "moe_w_gate", "moe_w_up", "moe_w_down", "w_mod", "b_mod", "mlp_w1", "mlp_w2", "a_w_in",
          "a_w_q_b", "a_w_kv_b", "a_w_out", "h_w_in", "h_f_w1", "h_f_w2", "h_f_w3", "h_f_w4", "h_w_out",
          "resident", "even_tables", "chunk_mask", "rope2d", "dft", "feats", "window"]


def lay_out(I):
    a = {k: np.asarray(x) for k, x in I.items()}
    table = constants()

    def per_partition(x, n):
        return np.ascontiguousarray(x.reshape(n, P).T)

    d = {"x": a["x"][0], "ctx": a["ctx_2"][0]}
    d["gains"] = np.stack([a["norm_mix"][0], a["norm_ffn"][0], a["norm_mix"][1], a["norm_ffn"][1], a["norm1_g_2"][0],
                           a["norm2_g_2"][0], a["norm1_g_2"][1], a["h_skip_2"][0, 0], a["h_skip_2"][0, 1],
                           a["norm2_g_2"][1], a["final_g_2"]])
    d["rows"] = np.concatenate([x.reshape(-1) for x in (
        a["fox_q_norm"], a["fox_k_norm"], a["hgrn_out_norm"], a["diff_q_norm"], a["diff_k_norm"],
        a["diff_lambda_q1"], a["diff_lambda_k1"], a["diff_lambda_q2"], a["diff_lambda_k2"], a["diff_subln"],
        a["fox_f_bias"], a["a_q_norm_g_2"], a["a_k_norm_g_2"], a["a_q_a_g_2"], a["a_kv_a_g_2"],
        table["inv_freq"])])
    filt = np.zeros((P, 6), np.float32)
    for i, n in enumerate(("h_f_b1_2", "h_f_b2_2", "h_f_b3_2")):
        filt[0:64, i] = a[n][0]
        filt[0:64, 3 + i] = a["h_f_freq_2"][0, i]
    not_first = np.ones((P, 1), np.float32)
    not_first[0] = 0
    d["cols"] = np.concatenate([
        per_partition(a["hgrn_lb_logits"], 8), per_partition(a["h_conv_w_2"], 72), per_partition(a["h_conv_b_2"], 24),
        filt, per_partition(a["c_2"], 8), per_partition(a["c_ctx_2"], 8), not_first], 1)
    d["positions"] = np.ascontiguousarray(a["positions"].reshape(NT, P).T)
    d["routers"] = np.concatenate([a["moe_router_group"],
                                   a["moe_router_expert"].transpose(0, 2, 1, 3).reshape(2, D, N_EXPERTS)], 2)
    for n in ("moe_w_gate", "moe_w_up"):
        d[n] = a[n].reshape(2 * N_EXPERTS, D, 512)
    d["moe_w_down"] = a["moe_w_down"].reshape(2 * N_EXPERTS, 512, D)
    for n in ("even_w_in", "even_w_out", "odd_w_in", "odd_w_out"):
        d[n] = a[n][0]
    for n in ("a_w_in", "a_w_q_b", "a_w_kv_b", "a_w_out", "h_w_in", "h_f_w1", "h_f_w2", "h_f_w3", "h_f_w4", "h_w_out"):
        d[n] = a[n + "_2"][0]
    for n in ("w_mod", "b_mod", "mlp_w1", "mlp_w2"):
        d[n] = a[n + "_2"]
    for n in ("resident", "even_tables", "chunk_mask", "rope2d", "dft", "feats", "window"):
        d[n] = table[n]
    return {n: np.ascontiguousarray(d[n]) for n in _ORDER}


def kernel(**inputs):
    import concourse.bacc as bacc
    from concourse.bass_utils import run_bass_kernel_spmd

    nc = bacc.Bacc("TRN2", target_bir_lowering=False, num_devices=1)
    arrays = {f"in_{n}": a for n, a in lay_out(inputs).items()}
    args = {n[3:]: nc.dram_tensor(n, a.shape, mybir.dt.from_np(a.dtype), kind="ExternalInput").ap()
            for n, a in arrays.items()}
    out = nc.dram_tensor("out_0", (S, D), F32, kind="ExternalOutput").ap()
    build(nc, args, out)
    got = run_bass_kernel_spmd(nc, [arrays], core_ids=[0])
    return got.results[0]["out_0"].reshape(1, S, D)
```
